# Optimizing a Trainium2 kernel written in Bass

```python
import jax
import jax.numpy as jnp
from jax import lax
import numpy as np

D_MODEL = 1024
BATCH = 1
SEQ = 128
DEPTH = 1
DEC_BATCH = 1
DEC_SEQ = 128
PAST_LEN = 128

GRID_W = 64
N_HEADS = 8
HEAD_K = D_MODEL // N_HEADS
HEAD_V = D_MODEL // N_HEADS
HGRN_K = N_HEADS * HEAD_K
HGRN_V = N_HEADS * HEAD_V
CHUNK = 16
CONV_DIM = D_MODEL // 2
CONV_WIDTH = 31
N_EXPERTS = 64
N_GROUPS = 8
TOPK_GROUPS = 4
TOP_K = 8
EXPERT_FF = 256
SHARED_FF = 256
ROUTED_SCALE = 2.5
N_MOD = 6
EPS = 1e-6
IN_COLS = 3 * HGRN_K + 2 * HGRN_V + 2 * CONV_DIM + 2 * D_MODEL

kernel_name = 'hybrid_hgrn2_conformer_moe_prefix_diffusion'

def _rmsnorm(x, g):
    xf = x.astype(jnp.float32)
    return xf * lax.rsqrt(jnp.mean(xf * xf, axis=-1, keepdims=True) + EPS) * g.astype(jnp.float32)

def _hgrn_direction(q, k, v, log_f, s0):
    bsz, length, heads, _ = q.shape
    dv = v.shape[-1]
    n = length // CHUNK

    def to_chunks(t):
        return t.reshape(bsz, n, CHUNK, heads, t.shape[-1]).transpose(0, 1, 3, 2, 4)

    q, k, v, log_f = to_chunks(q), to_chunks(k), to_chunks(v), to_chunks(log_f)
    b = jnp.cumsum(log_f, axis=3)
    mask = jnp.tril(jnp.ones((CHUNK, CHUNK), dtype=bool))[:, :, None]
    diff = b[:, :, :, :, None, :] - b[:, :, :, None, :, :]
    decay = jnp.exp(jnp.where(mask, diff, -jnp.inf))
    scores = jnp.einsum('bnhtd,bnhtsd,bnhsd->bnhts', q, decay, k)
    o_intra = jnp.einsum('bnhts,bnhse->bnhte', scores, v)
    b_last = b[:, :, :, -1, :]
    kv = jnp.einsum('bnhsd,bnhse->bnhde', k * jnp.exp(b_last[:, :, :, None, :] - b), v)

    def step(s, inp):
        dec, kv_c = inp
        return dec[..., None] * s + kv_c, s

    s_final, s_start = lax.scan(step, s0, (jnp.moveaxis(jnp.exp(b_last), 1, 0), jnp.moveaxis(kv, 1, 0)))
    s_start = jnp.moveaxis(s_start, 0, 1)
    o_inter = jnp.einsum('bnhtd,bnhde->bnhte', q * jnp.exp(b), s_start)
    o = (o_intra + o_inter).transpose(0, 1, 3, 2, 4).reshape(bsz, length, heads, dv)
    return o, s_final

def _forget(z, lb):
    lb = lb.astype(jnp.float32).reshape(N_HEADS, HEAD_K)
    log_f = jnp.logaddexp(jnp.log(lb), jnp.log1p(-lb) + jax.nn.log_sigmoid(z))
    k = (1.0 - lb) * jax.nn.sigmoid(-z)
    return log_f, k

def _mixers(h, s0_f, s0_b, lb_f, lb_b, w_in, hgrn_norm_g, w_proj_hgrn, conv_dw_w, conv_dw_b,
            conv_norm_g, conv_norm_b, w_proj_conv, w_out):
    bsz, length, _ = h.shape
    z = jnp.einsum('bld,dc->blc', h, w_in).astype(jnp.float32)
    splits = [HGRN_K, HGRN_K + HGRN_V, 2 * HGRN_K + HGRN_V, 3 * HGRN_K + HGRN_V,
              3 * HGRN_K + 2 * HGRN_V, 3 * HGRN_K + 2 * HGRN_V + 2 * CONV_DIM]
    q, v, zf, zb, og, u, gz = jnp.split(z, splits, axis=-1)

    def heads(t):
        return t.reshape(bsz, length, N_HEADS, t.shape[-1] // N_HEADS)

    def flip(t):
        return jnp.flip(t, axis=1)

    q, v = heads(q), heads(v)
    log_ff, kf = _forget(heads(zf), lb_f)
    log_fb, kb = _forget(heads(zb), lb_b)
    o_f, s_f = _hgrn_direction(q, kf, v, log_ff, s0_f)
    o_b, s_b = _hgrn_direction(flip(q), flip(kb), flip(v), flip(log_fb), s0_b)
    o = o_f + flip(o_b)
    o = o * lax.rsqrt(jnp.mean(o * o, axis=-1, keepdims=True) + EPS)
    o = o.reshape(bsz, length, HGRN_V) * hgrn_norm_g * jax.nn.silu(og)
    y_a = o @ w_proj_hgrn

    u = u[..., :CONV_DIM] * jax.nn.sigmoid(u[..., CONV_DIM:])
    u = lax.conv_general_dilated(u, conv_dw_w.astype(u.dtype)[:, None, :], window_strides=(1,),
                                 padding=[(CONV_WIDTH // 2, CONV_WIDTH // 2)],
                                 dimension_numbers=('NWC', 'WIO', 'NWC'),
                                 feature_group_count=CONV_DIM) + conv_dw_b
    mu = jnp.mean(u, axis=-1, keepdims=True)
    var = jnp.mean(jnp.square(u - mu), axis=-1, keepdims=True)
    u = (u - mu) * lax.rsqrt(var + EPS) * conv_norm_g + conv_norm_b
    y_b = jax.nn.silu(u) @ w_proj_conv

    g_a, g_b = jnp.split(jax.nn.sigmoid(gz), 2, axis=-1)
    out = (g_a * y_a + g_b * y_b) @ w_out
    return out.astype(jnp.float32), s_f, s_b

def _moe(h, w_router, router_bias, w_expert_gate_up, w_expert_down, w_shared_gate_up, w_shared_down):
    bsz, length, d = h.shape
    t = h.reshape(bsz * length, d)
    scores = jax.nn.sigmoid((t @ w_router).astype(jnp.float32))
    sel = scores + router_bias.astype(jnp.float32)
    per_group = N_EXPERTS // N_GROUPS
    grp = jnp.sum(lax.top_k(sel.reshape(-1, N_GROUPS, per_group), 2)[0], axis=-1)
    _, gi = lax.top_k(grp, TOPK_GROUPS)
    gmask = jnp.any(gi[..., None] == jnp.arange(N_GROUPS), axis=-2)
    sel = jnp.where(jnp.repeat(gmask, per_group, axis=-1), sel, -jnp.inf)
    _, ei = lax.top_k(sel, TOP_K)
    w = jnp.take_along_axis(scores, ei, axis=-1)
    w = w / jnp.sum(w, axis=-1, keepdims=True) * ROUTED_SCALE
    combine = jnp.sum(jax.nn.one_hot(ei, N_EXPERTS, dtype=jnp.float32) * w[..., None], axis=1)
    gu = jnp.einsum('td,edf->etf', t, w_expert_gate_up)
    g, u = jnp.split(gu, 2, axis=-1)
    act = jax.nn.silu(g) * u * combine.T[:, :, None]
    routed = jnp.einsum('etf,efd->td', act, w_expert_down)
    sg, su = jnp.split(t @ w_shared_gate_up, 2, axis=-1)
    shared = (jax.nn.silu(sg) * su) @ w_shared_down
    return (routed + shared).astype(jnp.float32).reshape(bsz, length, d)

def _layer(x, mod, s0_f, s0_b, lb_f, lb_b, p):
    (norm1_g, w_in, hgrn_norm_g, w_proj_hgrn, conv_dw_w, conv_dw_b, conv_norm_g, conv_norm_b,
     w_proj_conv, w_out, norm2_g, w_router, router_bias, w_expert_gate_up, w_expert_down,
     w_shared_gate_up, w_shared_down) = p
    shift1, scale1, gate1, shift2, scale2, gate2 = jnp.split(mod.astype(jnp.float32)[:, None, :], N_MOD, axis=-1)
    h = _rmsnorm(x, norm1_g) * (1.0 + scale1) + shift1
    mix, s_f, s_b = _mixers(h, s0_f, s0_b, lb_f, lb_b, w_in, hgrn_norm_g, w_proj_hgrn, conv_dw_w,
                            conv_dw_b, conv_norm_g, conv_norm_b, w_proj_conv, w_out)
    xf = x.astype(jnp.float32) + gate1 * mix
    h = _rmsnorm(xf, norm2_g) * (1.0 + scale2) + shift2
    xf = xf + gate2 * _moe(h, w_router, router_bias, w_expert_gate_up, w_expert_down,
                           w_shared_gate_up, w_shared_down)
    return xf.astype(x.dtype), s_f, s_b

def setup_inputs(seed: int = 0) -> dict:
    key = jax.random.key(seed)
    ks = jax.random.split(key, 32)

    def nrm(k, shape, scale):
        return jax.random.normal(k, shape, jnp.float32) * scale

    d = D_MODEL
    return {
        'x_prompt': nrm(ks[0], (BATCH, SEQ, d), 1.0),
        'x_sample': nrm(ks[1], (DEC_BATCH, DEC_SEQ, d), 1.0),
        'state_hgrn': nrm(ks[2], (DEC_BATCH, DEPTH, 2, N_HEADS, HEAD_K, HEAD_V), 0.3),
        'c': nrm(ks[3], (DEC_BATCH, d), 1.0),
        'c_ctx': nrm(ks[4], (d,), 1.0),
        'w_ada': nrm(ks[5], (DEPTH, d, N_MOD * d), 0.5 * d ** -0.5),
        'b_ada': nrm(ks[6], (DEPTH, N_MOD * d), 0.02),
        'norm1_g': 1.0 + nrm(ks[7], (DEPTH, d), 0.02),
        'w_in': nrm(ks[8], (DEPTH, d, IN_COLS), d ** -0.5),
        'hgrn_lb_logits': nrm(ks[9], (DEPTH, 2, HGRN_K), 0.5),
        'hgrn_norm_g': 1.0 + nrm(ks[10], (DEPTH, HGRN_V), 0.02),
        'w_proj_hgrn': nrm(ks[11], (DEPTH, HGRN_V, d), HGRN_V ** -0.5),
        'conv_dw_w': nrm(ks[12], (DEPTH, CONV_WIDTH, CONV_DIM), CONV_WIDTH ** -0.5),
        'conv_dw_b': nrm(ks[13], (DEPTH, CONV_DIM), 0.02),
        'conv_norm_g': 1.0 + nrm(ks[14], (DEPTH, CONV_DIM), 0.02),
        'conv_norm_b': nrm(ks[15], (DEPTH, CONV_DIM), 0.02),
        'w_proj_conv': nrm(ks[16], (DEPTH, CONV_DIM, d), CONV_DIM ** -0.5),
        'w_out': nrm(ks[17], (DEPTH, d, d), d ** -0.5),
        'norm2_g': 1.0 + nrm(ks[18], (DEPTH, d), 0.02),
        'w_router': nrm(ks[19], (DEPTH, d, N_EXPERTS), d ** -0.5),
        'router_bias': nrm(ks[20], (DEPTH, N_EXPERTS), 0.01),
        'w_expert_gate_up': nrm(ks[21], (DEPTH, N_EXPERTS, d, 2 * EXPERT_FF), d ** -0.5),
        'w_expert_down': nrm(ks[22], (DEPTH, N_EXPERTS, EXPERT_FF, d), EXPERT_FF ** -0.5),
        'w_shared_gate_up': nrm(ks[23], (DEPTH, d, 2 * SHARED_FF), d ** -0.5),
        'w_shared_down': nrm(ks[24], (DEPTH, SHARED_FF, d), SHARED_FF ** -0.5),
        'final_norm_g': 1.0 + nrm(ks[25], (d,), 0.02),
    }

def reference(x_prompt, x_sample, state_hgrn, c, c_ctx, w_ada, b_ada, norm1_g, w_in, hgrn_lb_logits,
              hgrn_norm_g, w_proj_hgrn, conv_dw_w, conv_dw_b, conv_norm_g, conv_norm_b, w_proj_conv,
              w_out, norm2_g, w_router, router_bias, w_expert_gate_up, w_expert_down,
              w_shared_gate_up, w_shared_down, final_norm_g):
    n_lat = x_sample.shape[1]
    rows = n_lat // GRID_W
    if rows * GRID_W != n_lat:
        raise ValueError('latent token count must fill whole grid rows')

    lb = jnp.cumsum(jax.nn.softmax(hgrn_lb_logits.astype(jnp.float32), axis=0), axis=0)
    lb = lb - lb[:1]

    layers = [(norm1_g[l], w_in[l], hgrn_norm_g[l], w_proj_hgrn[l], conv_dw_w[l], conv_dw_b[l],
               conv_norm_g[l], conv_norm_b[l], w_proj_conv[l], w_out[l], norm2_g[l], w_router[l],
               router_bias[l], w_expert_gate_up[l], w_expert_down[l], w_shared_gate_up[l],
               w_shared_down[l]) for l in range(DEPTH)]

    xp = x_prompt
    zeros = jnp.zeros((x_prompt.shape[0], N_HEADS, HEAD_K, HEAD_V), jnp.float32)
    ctx_states = []
    for l in range(DEPTH):
        mod = (jax.nn.silu(c_ctx.astype(jnp.float32)) @ w_ada[l] + b_ada[l])[None, :]
        xp, s_f, s_b = _layer(xp, mod, zeros, zeros, lb[l, 0], lb[l, 1], layers[l])
        ctx_states.append(jnp.stack([s_f, s_b], axis=1))
    new_state_hgrn = jnp.stack(ctx_states, axis=1).astype(x_prompt.dtype)

    xs = x_sample
    for l in range(DEPTH):
        mod = jax.nn.silu(c.astype(jnp.float32)) @ w_ada[l] + b_ada[l]
        xs, _, _ = _layer(xs, mod, state_hgrn[:, l, 0].astype(jnp.float32),
                          state_hgrn[:, l, 1].astype(jnp.float32), lb[l, 0], lb[l, 1], layers[l])

    y_prompt = _rmsnorm(xp, final_norm_g).astype(x_prompt.dtype)
    y_sample = _rmsnorm(xs, final_norm_g).astype(x_sample.dtype)
    return (y_prompt, y_sample, new_state_hgrn)


_drawn_inputs = setup_inputs


def setup_inputs(seed=0):
    import zlib

    import numpy as np

    out = dict(_drawn_inputs(seed))
    spreads = {}
    factors = {'state_hgrn': 8.0,
     'norm1_g': 2.875,
     'hgrn_norm_g': 6.231,
     'conv_dw_b': 19.177,
     'conv_norm_g': 29.614,
     'conv_norm_b': 37.912,
     'final_norm_g': 7.965,
     'norm2_g': 4.464,
     'router_bias': 3.184}
    for name, (base, spread) in spreads.items():
        noise = np.random.default_rng([zlib.crc32(name.encode()), seed]).standard_normal(out[name].shape)
        drawn = base * np.exp(spread * noise) if base else spread * noise
        out[name] = jnp.asarray(drawn.astype(out[name].dtype))
    for name, factor in factors.items():
        out[name] = (out[name] * factor).astype(out[name].dtype)
    return out
```

```python
from contextlib import ExitStack

import concourse.bass as bass
from concourse import mybir
from concourse.alu_op_type import AluOpType as ALU

ACT = mybir.ActivationFunctionType
F32 = mybir.dt.float32
F32R = mybir.dt.float32r
I32 = mybir.dt.int32
U32 = mybir.dt.uint32
AX = mybir.AxisListType.X

P = 128
D = 1024
KD = D // P
NS = 2
T = NS * P
H = 8
NE = 64
FF = 256
TOPK = 8
ROUTED_SCALE = 2.5
EPS = 1e-6
CW = 31
CC = 4
PAD = CW // 2
UW = P + 2 * PAD
C = 64
LEVELS = 7

NX = T * TOPK // C
NI = NE + NX
ITERS = NI // 4
MAIN = NE // 4
BIG = 3.0e38
USE_IF = True

C_ID, C_MASK = 0, P
C_TRI = C_MASK + LEVELS * P
C_TRIE = C_TRI + P
C_IOTA = C_TRIE + NE
C_LT = C_IOTA + C
C_ECOL = C_LT + 64
C_ALL = C_ECOL + 1

R_C, R_BADA, R_G1, R_G2, R_HG, R_LB = 0, 16, 64, 72, 80, 88
R_DWB, R_CNG, R_CNB = 104, 108, 112
R_ALL = 116

Q0, V0, ZF0, ZB0, OG0, U0, GZ0 = 0, 1024, 2048, 3072, 4096, 5120, 6144
M_SH1, M_SC1, M_GT1, M_SH2, M_SC2, M_GT2 = 0, 8, 16, 24, 32, 40

KB = 1024
BASE = 16512


class Own:

    def __init__(self, eng, sem):
        self.eng, self.sem, self.n = eng, sem, 0

    def mark(self, instruction):
        instruction.then_inc(self.sem, 1)
        self.n += 1
        return self.n

    def wait(self, n=None):
        self.eng.wait_ge(self.sem, self.n if n is None else n)

    def step(self, instruction):
        self.mark(instruction)
        self.wait()


def build(nc, A, outs):
    y_prompt, y_sample, new_state = outs
    ctx = ExitStack()
    with ctx:
        def at(name, kb, shape, dt=F32):
            return nc.alloc_sbuf_tensor_at(name, shape, dt, offset=BASE + int(kb * KB))

        def sem(name):
            return ctx.enter_context(nc.semaphore(name))

        ring = [at(f"ring{i}", 16 * i, [P, 4096]) for i in range(4)]
        ga = at("ga", 64, [P, H, T])
        gb = at("gb", 72, [P, H, T])
        att = at("att", 80, [P, 16, P])
        og = at("og", 88, [P, H, T])
        x_t = at("x_t", 96, [P, KD, T])
        h_t = at("h_t", 104, [P, KD, T])
        qk = at("qk", 112, [P, 4, 16 * P])
        xn = at("xn", 128, [P, NS, D])
        fg = at("fg", 144, [P, 2, 16 * P])
        o_t = at("o_t", 144, [P, H, T])
        k_tok = at("k_tok", 152, [P, 16, P])
        x_tok = at("x_tok", 160, [P, NS, D])
        v_tok = at("v_tok", 160, [P, NS, D])
        s0 = at("s0", 168, [P, 16, P])
        upad = at("upad", 176, [P, CC, NS, UW])
        conv = at("conv", 181, [P, CC, T])
        tmp = at("tmp", 185, [P, 2, 512])
        consts = at("consts", 189, [P, C_ALL])
        vec = at("vec", 194.5, [P, P])
        small = at("small", 195, [P, 256])
        ones = at("ones", 196, [P, P])
        dw = at("dw", 196.5, [P, CW, CC])
        rows = at("rows", 197, [P, P])
        rows_dw = at("rows_dw", 198, [P, P])
        s_new = at("s_new", 197, [P, 16, P])
        k_mix = at("k_mix", 197, [P, 16 * P])
        w_r = at("w_r", 205, [P, KD, NE])
        b_router = at("b_router", 207, [P, NE])
        mod = at("mod", 207.25, [P, 48, NS])
        w_gu = [at(f"w_gu{i}", 24 * i, [P, KD, 2 * FF]) for i in range(4)]
        w_dn = [at(f"w_dn{i}", 24 * i + 16, [P, 2, D]) for i in range(4)]
        h_hi = at("h_hi", 112, [P, NS, KD, P], F32R)
        h_lo = at("h_lo", 120, [P, NS, KD, P], F32R)
        x1 = at("x1", 128, [P, NS, D])
        xn2 = at("xn2", 136, [P, NS, D])
        g2row = at("g2row", 136, [P, NS, D])
        xg = [at(f"xg{i}", 144 + 4 * i, [P, KD, P]) for i in range(2)]
        sel_p = [at(f"sel_p{i}", 152 + i, [P, NS, P], F32R) for i in range(2)]
        sel_t = [at(f"sel_t{i}", 154 + i, [P, T], F32R) for i in range(2)]
        act_t = [at(f"act_t{i}", 156 + i, [P, 2, P]) for i in range(2)]
        sil = at("sil", 158, [P, 2 * P])
        y_hi = [at(f"y_hi{i}", 160 + 2 * i, [P, 512], F32R) for i in range(2)]
        y_lo = [at(f"y_lo{i}", 164 + 2 * i, [P, 512], F32R) for i in range(2)]
        fin_g = at("fin_g", 168, [P, D])
        pos_i = at("pos_i", 172, [P, NS, NI + 4])
        comb_i = at("comb_i", 173, [P, NS, NI + 4])
        comb_p = [at(f"comb_p{i}", 174 + i / 32, [P, NS, 2]) for i in range(2)]
        w_slot = [at(f"w_slot{i}", 174.125 + i / 32, [P, 1]) for i in range(2)]
        e_row = at("e_row", 174.5, [P, NX + 4], I32)
        act_s = at("act_s", 176, [P, 2, T])
        sil_s = at("sil_s", 178, [P, 2, T])
        w_sd = at("w_sd", 104, [P, 2, D])
        fin = at("fin", 96, [P, NS, D])
        rt = at("rt", 197, [P, 2048])

        def pb(name):
            return ctx.enter_context(nc.psum_tensor(name, [P, 512], F32))

        bank = [pb(f"bank{i}") for i in range(8)]
        y_acc = [[bank[4 + 2 * s + h] for h in range(2)] for s in range(NS)]

        ident = consts[:, C_ID:C_ID + P]

        def sm(lo, n):
            return small[:, lo:lo + n]

        csil = sm(0, 16)
        gain1 = sm(16, 16)
        gain2 = sm(32, 16)
        lb = sm(48, 16)
        oml = sm(64, 16)
        csig = sm(80, 16)
        ssq = sm(96, 2)
        rms = sm(98, 2)
        ssq_c = sm(100, 2)
        rms_c = sm(102, 2)
        ssq_o = sm(104, 16)
        rms_o = sm(120, 16)
        mhalf = sm(136, 16)
        ssq2 = sm(152, 2)
        rms2 = sm(154, 2)
        ssqf = sm(156, 2)
        rmsf = sm(158, 2)
        nwork = small[0:1, 162:163].bitcast(I32)
        mod_v = mod[:, :, :]

        s_x, s_cst, s_rows, s_s0, s_wr, s_fing = map(sem, ("x_loaded", "consts_loaded", "rows_loaded", "s0_loaded", "router_loaded", "fing_loaded"))
        s_w = [sem(f"ring_loaded{i}") for i in range(4)]
        s_gu = [sem(f"gu_loaded{i}") for i in range(4)]
        s_dn = [sem(f"dn_loaded{i}") for i in range(4)]
        s_init = sem("init_done")
        own_dve, own_act, own_pool = sem("own_dve"), sem("own_act"), sem("own_pool")
        vec_ready, vec_copied = sem("vec_ready"), sem("vec_copied")
        ssq_ready, rms_ready = sem("ssq_ready"), sem("rms_ready")
        c_sig, c_silu = sem("c_sig"), sem("c_silu")
        xt_ready, xt_copied = sem("xt_ready"), sem("xt_copied")
        xn_done = sem("xn_done")
        mod_ready, mod_done = sem("mod_ready"), sem("mod_done")
        proj_ready = sem("proj_ready")
        act_evac, dve_evac = sem("act_evac"), sem("dve_evac")
        u_gated, fk_done, og_sig = sem("u_gated"), sem("fk_done"), sem("og_sig")
        sc_ready, sc_used = sem("scores_ready"), sem("scores_used")
        mix_done = sem("keys_mixed")
        q_done, k_done, tot_done = sem("q_updated"), sem("k_updated"), sem("totals_done")
        conv_done, mean_ready, cen_done, csq_done = map(sem, ("conv_done", "mean_ready", "centred", "conv_squared"))
        cvar_ready, cms_done, crms_done, cdiag_done = map(sem, ("cvar_ready", "cms_done", "crms_done", "cdiag_done"))
        cb_ready, cn_done, cs_done, cact_done = map(sem, ("conv_bcast_ready", "conv_normed", "conv_sig", "conv_act"))
        o_ready, o_copied, osq_ready = sem("o_ready"), sem("o_copied"), sem("o_ssq_ready")
        oms_done, orms_done = sem("o_ms_done"), sem("o_rms_done")
        odiag_done, ob_ready, ob_used = sem("o_diag_done"), sem("o_bcast_ready"), sem("o_normed")
        kt_ready, kt_copied, st_ready, st_copied, s_state = map(sem, ("k_tok_ready", "k_tok_copied", "state_ready", "state_copied", "state_stored"))
        merged = sem("merged")
        tt_ready, tt_copied = sem("x1_tok_ready"), sem("x1_tok_copied")
        ssq2_done, rms2_done, xn2_done = sem("ssq2_done"), sem("rms2_done"), sem("xn2_done")
        lg_ready, lg_sig, lg_mask = sem("logits_ready"), sem("scores_done"), sem("mask_done")
        hr_ready, hr_hi, hr_done = sem("h2_tok_ready"), sem("h2_hi_done"), sem("h2_tok_done")
        s_sd = sem("shared_down_loaded")
        cnt_ready, nx_done, end_ready, oh_done = map(sem, ("count_ready", "nx_done", "end_ready", "onehot_done"))
        posm_done, pt1_ready, pt1_copied = sem("posm_done"), sem("post_ready"), sem("post_copied")
        items_ready, items_done = sem("items_ready"), sem("items_done")
        gr_ready, gr_done = sem("g2row_ready"), sem("g2row_done")
        built, ga_ready, ga_evac, gbk_ready, gbk_evac = map(sem, ("built", "gather_a", "gather_a_evac", "gather_b", "gather_b_evac"))
        pt_ready, pt_evac = sem("sel_t_ready"), sem("sel_t_evac")
        gu_ready, sil_ready, act_ready = sem("gu_ready"), sem("sil_ready"), sem("act_ready")
        dn_ready, hi_ready, y_ready = sem("dn_ready"), sem("y_hi_ready"), sem("y_split_ready")
        loop_done, y_done, x2_done, f_ssq, f_rms, out_done, s_out = map(sem, ("loop_done", "y_done", "x2_done", "final_ssq", "final_rms", "out_done", "stored"))

        def cols(w, c0):
            return w.rearrange("(k p) c -> p k c", p=P)[:, :, c0:c0 + 512]

        w_ada, w_in = A["w_ada"][0], A["w_in"][0]
        blocks = [(f"ada{j}", cols(w_ada, 512 * j)) for j in range(4)]
        for name, c0 in (("u1", U0), ("u2", U0 + 512), ("q0", Q0), ("zf0", ZF0), ("zb0", ZB0), ("q1", Q0 + 512),
                         ("zf1", ZF0 + 512), ("zb1", ZB0 + 512), ("v0", V0), ("v1", V0 + 512),
                         ("og0", OG0), ("og1", OG0 + 512), ("ga0", GZ0), ("ga1", GZ0 + 512), ("gb0", GZ0 + 1024), ("gb1", GZ0 + 1536)):
            blocks.append((name, cols(w_in, c0)))
        blocks += [(f"ada{j}", cols(w_ada, 512 * j)) for j in range(4, 12)]
        blocks.append(("pc", A["w_proj_conv"][0].rearrange("(k p) c -> p k c", p=P)))
        blocks += [(f"ph{j}", cols(A["w_proj_hgrn"][0], 512 * j)) for j in range(2)]
        blocks += [(f"wo{j}", cols(A["w_out"][0], 512 * j)) for j in range(2)]
        blocks.append(("sg", cols(A["w_shared_gate_up"][0], 0)))
        number = {name: n for n, (name, _) in enumerate(blocks)}

        def tile_of(name):
            src = blocks[number[name]][1]
            k, n = src.shape[1], src.shape[2]
            return ring[number[name] % 4][:, 0:k * n].rearrange("p (k c) -> p k c", k=k)

        gu_src = A["w_expert_gate_up"][0].rearrange("e (p k) f -> e p k f", k=KD)
        dn_src = A["w_expert_down"][0].rearrange("e (c p) d -> e p c d", p=P)

        fills, n_act, n_dve = [], 0, 0
        for name, n, by in ([(f"xt{j}", 1, "act") for j in range(4)] + [(f"h{j}", 1, "dve") for j in range(4)]
                            + [("u1", 2, "act"), ("u2", 2, "act"), ("q0", 2, "act"), ("zf0", 2, "act"), ("zb0", 2, "act"),
                               ("q1", 2, "act"), ("zf1", 2, "act"), ("zb1", 2, "act"), ("v0", 2, "act"), ("v1", 2, "act"),
                               ("og0", 2, "dve"), ("og1", 2, "dve"), ("ga0", 2, "act"), ("ga1", 2, "act"), ("gb0", 2, "act"),
                               ("gb1", 2, "act"), ("pc", 4, "dve"), ("ph0", 2, "dve"), ("ph1", 2, "dve"), ("wo0", 2, "dve"), ("wo1", 2, "dve"),
                               ("t1", 4, "act"), ("n2", 4, "dve"), ("hr", 4, "dve"), ("sg", 1, "act"), ("su", 1, "dve")]):
            for j in range(n):
                if by == "act":
                    n_act += 1
                    fills.append((name, j, act_evac, n_act))
                else:
                    n_dve += 1
                    fills.append((name, j, dve_evac, n_dve))
        fill_no = {(name, j): n for n, (name, j, _, _) in enumerate(fills)}

        def fill_bank(name, j=0):
            return bank[fill_no[name, j] % 4]

        def released(eng, name):
            if name[:3] == "ada":
                eng.wait_ge(mod_ready, int(name[3:]) + 1)
            else:
                last = {"sg": ("su", 0), "pc": ("pc", 3)}.get(name, (name, 1))
                eng.wait_ge(proj_ready, fill_no[last] + 1)

        def evacuated(eng, name, j=0):
            eng.wait_ge(fills[fill_no[name, j]][2], fills[fill_no[name, j]][3])

        def filled(eng, name, j=0):
            eng.wait_ge(proj_ready, fill_no[name, j] + 1)

        def query_mix(level, g):
            m = 1 << level
            base = qk[:, 0, g * P:(g + 1) * P]
            dims = [list(base.ap[0]), [2 * m, P // (2 * m)], [16 * P + m, 2]]
            if m > 1:
                dims.append([1, m])
            return bass.AP(base.tensor, base.offset, dims)

        def halves(arr, level):
            m = 1 << level
            return arr.rearrange("p (n h m) -> p n h m", h=2, m=m)

        off = [0]

        def r(n, *shape):
            v = rt[:, off[0]:off[0] + n]
            off[0] += n
            return v

        score = r(NS * NE).rearrange("p (s e) -> p s e", s=NS)
        sel = r(NS * NE).rearrange("p (s e) -> p s e", s=NS)
        top = r(NS * 64).rearrange("p (s g j) -> p s g j", s=NS, g=8)
        grp = r(16).rearrange("p (s g) -> p s g", s=NS)
        cmp = r(NS * 64).rearrange("p (s g j) -> p s g j", s=NS, g=8)
        ceq = r(NS * 64).rearrange("p (s g j) -> p s g j", s=NS, g=8)
        rank = r(16)
        gmask = r(16).rearrange("p (s g) -> p s g", s=NS)
        selm = r(NS * NE).rearrange("p (s e) -> p s e", s=NS)
        rep = r(NS * NE).rearrange("p (s e) -> p s e", s=NS)
        best = r(16).rearrange("p (s j) -> p s j", s=NS)
        mask = r(NS * NE).rearrange("p (s e) -> p s e", s=NS)
        comb = r(NS * NE).rearrange("p (s e) -> p s e", s=NS)
        wsum = r(2)
        wrec = r(2)
        posm = r(NS * NE).rearrange("p (s e) -> p s e", s=NS)
        nxt = r(4)
        endx = r(2)
        hot = r(NX)
        hot2 = r(NX)
        hotb = r(NX)
        neg = r(P)
        assert off[0] <= 2048
        ecol = consts[:, C_ECOL:C_ECOL + 1]
        iota_x = consts[0:NE, C_IOTA:C_IOTA + NX]

        def loop(eng, pair):
            if USE_IF:
                eng.wait_ge(items_done, 2)
                n = eng.value_load(nwork, min_val=0, max_val=NI)
            with eng.Fori(0, ITERS) as i:
                if USE_IF:
                    with eng.If(n > i * 4):
                        for b in range(2):
                            pair(b, i * 2 + b)
                else:
                    for b in range(2):
                        pair(b, i * 2 + b)

        block = ctx.enter_context(nc.Block())

        @block.sync
        def _(sp):
            for s, name in enumerate(("x_prompt", "x_sample")):
                sp.dma_start(x_tok[:, s, :], A[name][0]).then_inc(s_x, 16)
            for n, (name, src) in enumerate(blocks):
                if n >= 4:
                    released(sp, blocks[n - 4][0])
                sp.dma_start(tile_of(name), src).then_inc(s_w[n % 4], 16)
                if name == "u2":
                    sp.dma_start(w_r[:, :, :], A["w_router"][0].rearrange("(k p) e -> p k e", p=P)).then_inc(s_wr, 16)
                if name == "v0":
                    sp.dma_start(s0[:, :, :], A["state_hgrn"][0, 0].rearrange("a h k v -> k (a h) v")).then_inc(s_s0, 16)
                if name == "ph1":
                    sp.wait_ge(st_copied, 4)
                    sp.dma_start(new_state[0, 0].rearrange("a h k v -> k (a h) v"), s_new[:, :, :]).then_inc(s_state, 16)
                if name == "wo1":
                    sp.wait_ge(o_copied, 4)
                    sp.dma_start(fin_g[:, :], A["final_norm_g"].rearrange("(a d) -> a d", a=1).broadcast_to([P, D])).then_inc(s_fing, 16)

            def load(slot, e):
                sp.dma_start(w_gu[slot][:, :, :], gu_src[e]).then_inc(s_gu[slot], 16)
                sp.dma_start(w_dn[slot][:, :, :], dn_src[e]).then_inc(s_dn[slot], 16)

            last = {i: max(n for n in range(len(blocks)) if n % 4 == i) for i in range(4)}
            for slot, over in enumerate(((0, 1), (1, 2), (3,), ())):
                for i in over:
                    released(sp, blocks[last[i]][0])
                if slot == 2:
                    released(sp, "wo1")
                load(slot, slot)
            with sp.Fori(1, MAIN) as i:
                for slot in range(4):
                    if slot % 2 == 0:
                        sp.wait_ge(dn_ready, i * 4 - 2 + 2 * (slot // 2))
                    load(slot, i * 4 + slot)
            sp.wait_ge(items_done, 2)
            with sp.Fori(MAIN, ITERS) as i:
                def extra():
                    for slot in range(4):
                        e = sp.value_load(e_row[0:1, bass.ds(i * 4 + (slot - NE), 1)], min_val=0, max_val=NE - 1)
                        if slot % 2 == 0:
                            sp.wait_ge(dn_ready, i * 4 - 2 + 2 * (slot // 2))
                        sp.dma_start(w_gu[slot][:, :, :], gu_src[bass.ds(e, 1)].rearrange("a p k f -> (a p) k f")).then_inc(s_gu[slot], 16)
                        sp.dma_start(w_dn[slot][:, :, :], dn_src[bass.ds(e, 1)].rearrange("a p c d -> (a p) c d")).then_inc(s_dn[slot], 16)
                if USE_IF:
                    n = sp.value_load(nwork, min_val=0, max_val=NI)
                    with sp.If(n > i * 4):
                        extra()
                else:
                    extra()
            for s, out in enumerate((y_prompt, y_sample)):
                sp.wait_ge(out_done, s + 1)
                sp.dma_start(out[0], fin[:, s, :]).then_inc(s_out, 16)
            sp.wait_ge(s_state, 16)
            sp.wait_ge(s_out, 32)

        @block.gpsimd
        def _(pool):
            own = Own(pool, own_pool)

            def rsqrt(out, in_, n):
                return nc.gpsimd.tensor_tensor(out, in_, mhalf[:, 0:n], ALU.pow)

            nc.gpsimd.memset(mhalf, -0.5).then_inc(s_init, 1)
            nc.gpsimd.memset(ones[:, :], 1.0).then_inc(s_init, 1)
            nc.gpsimd.memset(upad[:, :, :, :], 0.0).then_inc(s_init, 1)
            pool.wait_ge(s_init, 3)
            pool.wait_ge(ssq_ready, 1)
            rsqrt(rms, ssq, 2).then_inc(rms_ready, 1)
            pool.wait_ge(vec_copied, 3)
            for half in range(2):
                for d in range(2):
                    for j in range(2):
                        evacuated(pool, f"{('zf', 'zb')[d]}{half}", j)
                        for hh in range(2):
                            hd = half * 4 + j * 2 + hh
                            c = slice(hd * T, (hd + 1) * T)
                            i = d * H + hd
                            nc.gpsimd.tensor_scalar(fg[:, d, c], fg[:, d, c], oml[:, i:i + 1], lb[:, i:i + 1],
                                                    ALU.mult, ALU.add).then_inc(fk_done, 1)
                            nc.gpsimd.tensor_scalar(qk[:, 2 + d, c], qk[:, 2 + d, c], oml[:, i:i + 1], None,
                                                    ALU.mult).then_inc(fk_done, 1)
            pool.wait_ge(fk_done, 32)
            for level in range(LEVELS):
                m = 1 << level
                if level == 4:
                    pool.wait_ge(cms_done, 1)
                    rsqrt(rms_c, ssq_c, 2).then_inc(crms_done, 1)
                pool.wait_ge(sc_ready, 4 * (level + 2))
                pool.wait_ge(mix_done, level + 1)
                if level:
                    pool.wait_ge(tot_done, level)
                kf, kb = halves(qk[:, 2, :], level), halves(qk[:, 3, :], level)
                tf, tb = halves(fg[:, 0, :], level), halves(fg[:, 1, :], level)
                nb = 16 * P // (2 * m)
                nc.gpsimd.tensor_tensor(kf[:, :, 0, :], kf[:, :, 0, :], tf[:, :, 1, 0:1].broadcast_to([P, nb, m]), ALU.mult).then_inc(k_done, 1)
                nc.gpsimd.tensor_tensor(kb[:, :, 1, :], kb[:, :, 1, :], tb[:, :, 0, 0:1].broadcast_to([P, nb, m]), ALU.mult).then_inc(k_done, 1)
            pool.wait_ge(oms_done, 1)
            rsqrt(rms_o, ssq_o, 16).then_inc(orms_done, 1)
            pool.wait_ge(ssq2_done, 1)
            rsqrt(rms2, ssq2, 2).then_inc(rms2_done, 1)
            pool.wait_ge(f_ssq, 1)
            rsqrt(rmsf, ssqf, 2).then_inc(f_rms, 1)

        @block.scalar
        def _(act):
            own = Own(act, own_act)

            def rows_of(x, r0, n):
                act.dma_start(rows[r0:r0 + n, :], x).then_inc(s_rows, 16)

            act.dma_start(consts[:, :], A["consts"]).then_inc(s_cst, 16)
            rows_of(A["c_ctx"].rearrange("(k p) -> k p", p=P), R_C, 8)
            rows_of(A["c"][0].rearrange("(k p) -> k p", p=P), R_C + 8, 8)
            rows_of(A["b_ada"][0].rearrange("(k p) -> k p", p=P), R_BADA, 48)
            rows_of(A["norm1_g"][0].rearrange("(k p) -> k p", p=P), R_G1, 8)
            rows_of(A["norm2_g"][0].rearrange("(k p) -> k p", p=P), R_G2, 8)
            rows_of(A["hgrn_norm_g"][0].rearrange("(k p) -> k p", p=P), R_HG, 8)
            rows_of(A["hgrn_lb_logits"][0].rearrange("a (k p) -> (a k) p", p=P), R_LB, 16)
            rows_of(A["conv_dw_b"][0].rearrange("(k p) -> k p", p=P), R_DWB, 4)
            rows_of(A["conv_norm_g"][0].rearrange("(k p) -> k p", p=P), R_CNG, 4)
            rows_of(A["conv_norm_b"][0].rearrange("(k p) -> k p", p=P), R_CNB, 4)
            act.dma_start(rows_dw[0:CW * CC, :], A["conv_dw_w"][0].rearrange("w (c p) -> (w c) p", p=P)).then_inc(s_rows, 16)
            act.dma_start(b_router[:, :], A["router_bias"].broadcast_to([P, NE])).then_inc(s_rows, 16)

            act.wait_ge(s_x, 32)
            for s in range(NS):
                junk = tmp[:, :, :].rearrange("p a n -> p (a n)")
                if s:
                    own.wait()
                own.mark(nc.scalar.activation(junk, x_tok[:, s, :], ACT.Square, accum_out=ssq[:, s:s + 1]))
            act.wait_ge(vec_copied, 1)
            nc.scalar.activation(csig, vec[:, R_C:R_C + 16], ACT.Sigmoid).then_inc(c_sig, 1)

            for j in range(4):
                filled(act, f"xt{j}")
                nc.scalar.activation(x_t[:, 2 * j:2 * j + 2, :].rearrange("p k t -> p (k t)"), fill_bank(f"xt{j}")[:, :],
                                     ACT.Copy).then_inc(act_evac, 1)

            act.wait_ge(s_init, 3)
            for j in range(2):
                filled(act, "u1", j)
                for c in range(2):
                    ins = nc.scalar.activation(upad[:, 2 * j + c, :, PAD:PAD + P],
                                               fill_bank("u1", j)[:, c * T:(c + 1) * T].rearrange("p (s t) -> p s t", s=NS), ACT.Copy)
                ins.then_inc(act_evac, 1)
            for j in range(2):
                filled(act, "u2", j)
                nc.scalar.activation(tmp[:, j, :], fill_bank("u2", j)[:, :], ACT.Sigmoid).then_inc(act_evac, 1)

            def heads(arr, half, j):
                h0 = (half * 4 + j * 2) * T
                return arr[:, h0:h0 + 2 * T]

            for half in range(2):
                for j in range(2):
                    filled(act, f"q{half}", j)
                    nc.scalar.activation(heads(qk[:, 1, :], half, j), fill_bank(f"q{half}", j)[:, :], ACT.Copy).then_inc(act_evac, 1)
                for d, z in enumerate(("zf", "zb")):
                    for j in range(2):
                        filled(act, f"{z}{half}", j)
                        src = fill_bank(f"{z}{half}", j)[:, :]
                        nc.scalar.activation(heads(fg[:, d, :], half, j), src, ACT.Sigmoid)
                        nc.scalar.activation(heads(qk[:, 2 + d, :], half, j), src, ACT.Sigmoid, scale=-1.0).then_inc(act_evac, 1)
            for half in range(2):
                for s in range(NS):
                    filled(act, f"v{half}", s)
                    nc.scalar.activation(v_tok[:, s, half * 512:(half + 1) * 512], fill_bank(f"v{half}", s)[:, :], ACT.Copy).then_inc(act_evac, 1)

            def mix_keys(level):
                if level:
                    act.wait_ge(k_done, 2 * level)
                    act.wait_ge(sc_ready, 4 * (level + 1))
                else:
                    act.wait_ge(fk_done, 32)
                dst = halves(k_mix[:, :], level)
                nc.scalar.activation(dst[:, :, 0, :], halves(qk[:, 2, :], level)[:, :, 0, :], ACT.Copy)
                nc.scalar.activation(dst[:, :, 1, :], halves(qk[:, 3, :], level)[:, :, 1, :], ACT.Copy).then_inc(mix_done, 1)

            for half in range(2):
                for j in range(2):
                    n = half * 2 + j
                    filled(act, f"og{half}", j)
                    if n < 2:
                        act.wait_ge(u_gated, 2)
                    else:
                        evacuated(act, f"og{(n - 2) // 2}", n % 2)
                    nc.scalar.activation(tmp[:, n % 2, :], fill_bank(f"og{half}", j)[:, :], ACT.Sigmoid).then_inc(og_sig, 1)
                mix_keys(half)
            for name, dst in (("ga", ga), ("gb", gb)):
                for half in range(2):
                    if name == "ga" and half == 1:
                        act.wait_ge(cen_done, CC)
                        nc.scalar.activation(upad[:, :, :, :].rearrange("p c s u -> p (c s u)")[:, 0:CC * T],
                                             conv[:, :, :].rearrange("p c t -> p (c t)"), ACT.Square).then_inc(csq_done, 1)
                    for j in range(2):
                        filled(act, f"{name}{half}", j)
                        h0 = half * 4 + j * 2
                        nc.scalar.activation(dst[:, h0:h0 + 2, :].rearrange("p h t -> p (h t)"), fill_bank(f"{name}{half}", j)[:, :],
                                             ACT.Sigmoid).then_inc(act_evac, 1)
                    mix_keys(2 + 2 * (name == "gb") + half)
            mix_keys(6)
            act.wait_ge(cn_done, CC)
            for c in range(CC):
                nc.scalar.activation(upad[:, :, :, :].rearrange("p c s u -> p (c s u)")[:, c * T:(c + 1) * T], conv[:, c, :], ACT.Sigmoid).then_inc(cs_done, 1)
            for g in range(4):
                act.wait_ge(o_ready, g + 1)
                if g >= 2:
                    act.wait_ge(osq_ready, g - 1)
                elif g == 0:
                    act.wait_ge(tot_done, LEVELS)
                    act.wait_ge(k_done, 2 * LEVELS)
                    act.wait_ge(q_done, 2 * (LEVELS + 1))
                src = bank[4 + g % 2][:, :]
                nc.scalar.activation(o_t[:, 2 * g:2 * g + 2, :].rearrange("p h t -> p (h t)"), src, ACT.Copy)
                nc.scalar.activation(tmp[:, g % 2, :], src, ACT.Square).then_inc(o_copied, 1)
            for r in range(4):
                act.wait_ge(kt_ready, r + 1)
                nc.scalar.activation(k_tok[:, 4 * r:4 * r + 4, :].rearrange("p a b -> p (a b)"), bank[6][:, :], ACT.Copy).then_inc(kt_copied, 1)
            for r in range(4):
                act.wait_ge(st_ready, r + 1)
                nc.scalar.activation(s_new[:, 4 * r:4 * r + 4, :].rearrange("p a b -> p (a b)"), bank[6][:, :], ACT.Copy).then_inc(st_copied, 1)
            for s in range(NS):
                for hf in range(2):
                    filled(act, "t1", 2 * s + hf)
                    nc.scalar.activation(x1[:, s, hf * 512:(hf + 1) * 512], fill_bank("t1", 2 * s + hf)[:, :], ACT.Copy).then_inc(act_evac, 1)
            evacuated(act, "t1", 3)
            for s in range(NS):
                junk = tmp[:, :, :].rearrange("p a n -> p (a n)")
                if s == 0:
                    act.wait_ge(osq_ready, 4)
                    act.wait_ge(ob_ready, 4)
                else:
                    own.wait()
                own.mark(nc.scalar.activation(junk, x1[:, s, :], ACT.Square, accum_out=ssq2[:, s:s + 1]))
            act.wait_ge(lg_ready, 1)
            act.wait_ge(s_state, 16)
            nc.scalar.activation(rt[:, 0:NS * NE], bank[4][:, 0:NS * NE], ACT.Sigmoid).then_inc(lg_sig, 1)
            for j in range(4):
                filled(act, "hr", j)
                s, hf = j // 2, j % 2
                nc.scalar.activation(h_hi[:, s, :, 64 * hf:64 * hf + 64].rearrange("t k p -> t p k"),
                                     fill_bank("hr", j)[:, :].rearrange("t (p k) -> t p k", k=KD), ACT.Copy).then_inc(hr_hi, 1)
            filled(act, "sg", 0)
            nc.scalar.activation(sil_s[:, :, :].rearrange("p c t -> p (c t)"), fill_bank("sg")[:, :], ACT.Silu).then_inc(act_evac, 1)
            filled(act, "su")
            act.dma_start(w_sd[:, :, :], A["w_shared_down"][0].rearrange("(k p) c -> p k c", p=P)).then_inc(s_sd, 16)
            act.wait_ge(ga_ready, 1)
            nc.scalar.activation(xg[0][:, 0:4, :].rearrange("p k n -> p (k n)"), bank[0][:, :], ACT.Copy).then_inc(ga_evac, 1)

            def pair(b, p):
                act.wait_ge(gu_ready, p + 1)
                nc.scalar.activation(sil[:, :], bank[2][:, 0:2 * P], ACT.Silu).then_inc(sil_ready, 1)
                act.wait_ge(ga_ready, p + 2)
                nc.scalar.activation(xg[1 - b][:, 0:4, :].rearrange("p k n -> p (k n)"), bank[0][:, :], ACT.Copy).then_inc(ga_evac, 1)
                act.wait_ge(pt_evac, p + 1)
                for h in range(2):
                    act.wait_ge(dn_ready, p * 2 + (h + 1))
                    nc.scalar.activation(y_hi[h][:, :], bank[3][:, :], ACT.Copy, scale=w_slot[b][:, 0:1]).then_inc(hi_ready, 1)

            loop(act, pair)
            for s in range(NS):
                act.wait_ge(x2_done, s + 1)
                if s:
                    own.wait()
                own.mark(nc.scalar.activation(tmp[:, :, :].rearrange("p a n -> p (a n)"), fin[:, s, :], ACT.Square, accum_out=ssqf[:, s:s + 1]))

        @block.vector
        def _(dve):
            own = Own(dve, own_dve)
            V = nc.vector

            dve.wait_ge(vec_ready, 1)
            V.tensor_copy(vec[:, 0:R_ALL], bank[7][:, 0:R_ALL]).then_inc(vec_copied, 1)
            V.tensor_copy(dw[:, :, :].rearrange("p w c -> p (w c)"), bank[7][:, P:P + CW * CC]).then_inc(vec_copied, 1)
            dve.wait_ge(vec_copied, 2)
            own.step(V.tensor_tensor(oml, vec[:, R_LB:R_LB + 16], vec[:, R_LB:R_LB + 16], ALU.subtract))
            own.step(V.tensor_scalar(oml, oml, 1.0, None, ALU.add))
            own.step(V.tensor_tensor(lb, oml, oml, ALU.subtract))
            V.tensor_scalar(oml, lb, -1.0, 1.0, ALU.mult, ALU.add).then_inc(vec_copied, 1)
            dve.wait_ge(c_sig, 1)
            V.tensor_tensor(csil, csig, vec[:, R_C:R_C + 16], ALU.mult).then_inc(c_silu, 1)
            dve.wait_ge(own_act, 2)
            V.tensor_scalar(ssq, ssq, 1.0 / D, EPS, ALU.mult, ALU.add).then_inc(ssq_ready, 1)
            dve.wait_ge(rms_ready, 1)
            for s in range(NS):
                V.tensor_scalar(xn[:, s, :], x_tok[:, s, :], rms[:, s:s + 1], None, ALU.mult).then_inc(xn_done, 1)

            def modulation(j0, j1, ready):
                dve.wait_ge(mod_ready, ready)
                for s in range(NS):
                    last = V.tensor_tensor(mod_v[:, j0:j1, s], bank[7][:, 256 + 2 * j0:256 + 2 * j1].rearrange("p (j s) -> p j s", s=NS)[:, :, s],
                                           vec[:, R_BADA + j0:R_BADA + j1], ALU.add)
                    last.then_inc(mod_done, 1)
                dve.wait_ge(mod_done, 2 if j0 == 0 else 4)

            def gains(dst, scale, gain):
                g = dst.rearrange("p (k s) -> p k s", s=NS)
                for s in range(NS):
                    own.step(V.scalar_tensor_tensor(g[:, :, s], mod_v[:, scale:scale + 8, s], 1.0, vec[:, gain:gain + 8], ALU.add, ALU.mult))

            modulation(0, 16, 4)
            gains(gain1, M_SC1, R_G1)
            for j in range(4):
                filled(dve, f"h{j}")
                for kk in range(2):
                    for s in range(NS):
                        k = 2 * j + kk
                        src = fill_bank(f"h{j}")[:, kk * T + s * P:kk * T + (s + 1) * P]
                        ins = V.tensor_scalar(h_t[:, k, s * P:(s + 1) * P], src, gain1[:, 2 * k + s:2 * k + s + 1],
                                              mod_v[:, M_SH1 + k, s:s + 1], ALU.mult, ALU.add)
                ins.then_inc(dve_evac, 1)

            for j in range(2):
                evacuated(dve, "u2", j)
                sg = tmp[:, j, :].rearrange("p (c s t) -> p c s t", c=2, s=NS)
                for c in range(2):
                    uu = upad[:, 2 * j + c, :, PAD:PAD + P]
                    ins = V.tensor_tensor(uu, uu, sg[:, c], ALU.mult)
                ins.then_inc(u_gated, 1)
            dve.wait_ge(u_gated, 2)
            marks = []
            for w in range(CW):
                for c in range(CC):
                    dst = conv[:, c, :].rearrange("p (s t) -> p s t", s=NS)
                    src = upad[:, c, :, w:w + P]
                    tap = dw[:, w, c:c + 1]
                    if w == 0:
                        ins = V.tensor_scalar(dst, src, tap, vec[:, R_DWB + c:R_DWB + c + 1], ALU.mult, ALU.add)
                    else:
                        own.wait(marks[CC * (w - 1) + c])
                        ins = V.scalar_tensor_tensor(dst, src, tap, dst, ALU.mult, ALU.add)
                    if w < CW - 1:
                        marks.append(own.mark(ins))
                    else:
                        ins.then_inc(conv_done, 1)

            mask_of = [consts[:, C_MASK + P * lv:C_MASK + P * (lv + 1)].unsqueeze(1).broadcast_to([P, 4, P]) for lv in range(LEVELS)]
            dve.wait_ge(s_cst, 16)

            def score_tiles(level):
                for g in range(4):
                    n = 4 * (level + 1) + g
                    dve.wait_ge(sc_ready, n + 1)
                    src = bank[4 + n % 2][:, :].rearrange("p (a t) -> p a t", a=4)
                    dst = att[:, 4 * g:4 * g + 4, :]
                    if level < 0:
                        V.tensor_tensor(dst, src, ident.unsqueeze(1).broadcast_to([P, 4, P]), ALU.mult).then_inc(sc_used, 1)
                    else:
                        V.copy_predicated(dst, mask_of[level].bitcast(U32), src).then_inc(sc_used, 1)

            score_tiles(-1)
            dve.wait_ge(fk_done, 32)
            for d in (1, 0):
                V.tensor_tensor(qk[:, 1 - d, :], qk[:, 1, :], fg[:, d, :], ALU.mult).then_inc(q_done, 1)
            dve.wait_ge(q_done, 2)

            dve.wait_ge(mean_ready, 1)
            for c in range(CC):
                V.scalar_tensor_tensor(conv[:, c, :], bank[6][:, 0:T], -1.0 / (CC * P), conv[:, c, :], ALU.mult, ALU.add).then_inc(cen_done, 1)

            def og_gate(half):
                for j in range(2):
                    n = half * 2 + j
                    dve.wait_ge(og_sig, n + 1)
                    for hh in range(2):
                        hd = half * 4 + j * 2 + hh
                        ins = V.scalar_tensor_tensor(og[:, hd, :], fill_bank(f"og{half}", j)[:, hh * T:(hh + 1) * T], vec[:, R_HG + hd:R_HG + hd + 1],
                                                     tmp[:, n % 2, hh * T:(hh + 1) * T], ALU.mult, ALU.mult)
                    ins.then_inc(dve_evac, 1)

            for level in range(LEVELS):
                m = 1 << level
                score_tiles(level)
                nb = 16 * P // (2 * m)
                qb, qf = halves(qk[:, 0, :], level), halves(qk[:, 1, :], level)
                tf, tb = halves(fg[:, 0, :], level), halves(fg[:, 1, :], level)
                if level:
                    dve.wait_ge(tot_done, level)
                V.tensor_tensor(qf[:, :, 1, :], qf[:, :, 1, :], tf[:, :, 0, 0:1].broadcast_to([P, nb, m]), ALU.mult).then_inc(q_done, 1)
                V.tensor_tensor(qb[:, :, 0, :], qb[:, :, 0, :], tb[:, :, 1, 0:1].broadcast_to([P, nb, m]), ALU.mult).then_inc(q_done, 1)
                dve.wait_ge(q_done, 2 * (level + 2))
                dve.wait_ge(k_done, 2 * (level + 1))
                tot = fg[:, :, :].rearrange("p d (n h m) -> p d n h m", h=2, m=m)[:, :, :, :, 0]
                V.tensor_tensor(tot[:, :, :, 0], tot[:, :, :, 0], tot[:, :, :, 1], ALU.mult).then_inc(tot_done, 1)
                if level < 2:
                    og_gate(level)
                if level == 3:
                    dve.wait_ge(cvar_ready, 1)
                    V.tensor_scalar(ssq_c, bank[6][:, 256:258], 1.0 / (CC * P), EPS, ALU.mult, ALU.add).then_inc(cms_done, 1)
                if level == 4:
                    dve.wait_ge(crms_done, 1)
                    diag = tmp[:, 0, 0:T]
                    for s in range(NS):
                        V.tensor_scalar(diag[:, s * P:(s + 1) * P], ident, rms_c[:, s:s + 1], None, ALU.mult).then_inc(cdiag_done, 1)
                if level == 5:
                    dve.wait_ge(cb_ready, 1)
                    for c in range(CC):
                        own.mark(V.tensor_tensor(conv[:, c, :], conv[:, c, :], bank[6][:, 0:T], ALU.mult))
                    own.wait()
                    for c in range(CC):
                        V.tensor_scalar(conv[:, c, :], conv[:, c, :], vec[:, R_CNG + c:R_CNG + c + 1], vec[:, R_CNB + c:R_CNB + c + 1],
                                        ALU.mult, ALU.add).then_inc(cn_done, 1)
            dve.wait_ge(cn_done, CC)
            dve.wait_ge(cs_done, CC)
            for c in range(CC):
                V.tensor_tensor(conv[:, c, :], conv[:, c, :], upad[:, :, :, :].rearrange("p c s u -> p (c s u)")[:, c * T:(c + 1) * T],
                                ALU.mult).then_inc(cact_done, 1)
            modulation(16, 48, 12)
            gains(gain2, M_SC2, R_G2)

            dve.wait_ge(osq_ready, 4)
            V.tensor_scalar(ssq_o, bank[7][:, 384:400], 1.0 / P, EPS, ALU.mult, ALU.add).then_inc(oms_done, 1)
            dve.wait_ge(orms_done, 1)
            dve.wait_ge(o_copied, 4)
            for g in range(4):
                if g >= 2:
                    dve.wait_ge(ob_ready, g - 1)
                for i in range(4):
                    V.tensor_scalar(tmp[:, g % 2, i * P:(i + 1) * P], ident, rms_o[:, 4 * g + i:4 * g + i + 1], None, ALU.mult).then_inc(odiag_done, 1)
            for g in range(4):
                dve.wait_ge(ob_ready, g + 1)
                oo = o_t[:, 2 * g:2 * g + 2, :].rearrange("p h t -> p (h t)")
                own.step(V.tensor_tensor(oo, oo, bank[4 + g % 2][:, :], ALU.mult))
                V.tensor_tensor(oo, oo, og[:, 2 * g:2 * g + 2, :].rearrange("p h t -> p (h t)"), ALU.mult).then_inc(ob_used, 1)

            for name, dst in (("pc", gb), ("ph", ga)):
                for j in range(4):
                    key = ("pc", j) if name == "pc" else (f"ph{j // 2}", j % 2)
                    filled(dve, *key)
                    dd = dst[:, 2 * j:2 * j + 2, :].rearrange("p h t -> p (h t)")
                    V.tensor_tensor(dd, dd, fill_bank(*key)[:, :], ALU.mult).then_inc(dve_evac, 1)
                    if name == "ph":
                        evacuated(dve, *key)
                        V.tensor_tensor(dd, dd, gb[:, 2 * j:2 * j + 2, :].rearrange("p h t -> p (h t)"), ALU.add).then_inc(merged, 1)
            for j in range(4):
                key = (f"wo{j // 2}", j % 2)
                filled(dve, *key)
                for kk in range(2):
                    for s in range(NS):
                        k = 2 * j + kk
                        dst = x_t[:, k, s * P:(s + 1) * P]
                        ins = V.scalar_tensor_tensor(dst, fill_bank(*key)[:, kk * T + s * P:kk * T + (s + 1) * P], mod_v[:, M_GT1 + k, s:s + 1], dst, ALU.mult, ALU.add)
                ins.then_inc(dve_evac, 1)
            dve.wait_ge(own_act, 4)
            V.tensor_scalar(ssq2, ssq2, 1.0 / D, EPS, ALU.mult, ALU.add).then_inc(ssq2_done, 1)
            dve.wait_ge(rms2_done, 1)
            for s in range(NS):
                V.tensor_scalar(xn2[:, s, :], x1[:, s, :], rms2[:, s:s + 1], None, ALU.mult).then_inc(xn2_done, 1)
            for j in range(4):
                filled(dve, "n2", j)
                for kk in range(2):
                    for s in range(NS):
                        k = 2 * j + kk
                        src = fill_bank("n2", j)[:, kk * T + s * P:kk * T + (s + 1) * P]
                        ins = V.tensor_scalar(h_t[:, k, s * P:(s + 1) * P], src, gain2[:, 2 * k + s:2 * k + s + 1],
                                              mod_v[:, M_SH2 + k, s:s + 1], ALU.mult, ALU.add)
                ins.then_inc(dve_evac, 1)

            for j in range(4):
                filled(dve, "hr", j)
                dve.wait_ge(hr_hi, j + 1)
                s, hf = j // 2, j % 2
                V.tensor_tensor(h_lo[:, s, :, 64 * hf:64 * hf + 64].rearrange("t k p -> t p k"),
                                fill_bank("hr", j)[:, :].rearrange("t (p k) -> t p k", k=KD),
                                h_hi[:, s, :, 64 * hf:64 * hf + 64].rearrange("t k p -> t p k").bitcast(F32), ALU.subtract).then_inc(dve_evac, 1)
            dve.wait_ge(lg_sig, 1)
            dve.wait_ge(s_rows, 16 * 12)
            for s in range(NS):
                own.mark(V.tensor_tensor(sel[:, s, :], score[:, s, :], b_router[:, :], ALU.add))
            own.mark(V.memset(selm, -BIG))
            own.mark(V.memset(neg, -1.0))
            own.wait()
            for s in range(NS):
                for g in range(8):
                    own.mark(V.max(top[:, s, g, :], sel[:, s, 8 * g:8 * g + 8]))
            own.wait()
            own.step(V.tensor_tensor(grp, top[:, :, :, 0], top[:, :, :, 1], ALU.add))
            for s in range(NS):
                other = grp[:, s, :].unsqueeze(1).broadcast_to([P, 8, 8])
                mine = grp[:, s, :].unsqueeze(2).broadcast_to([P, 8, 8])
                own.mark(V.tensor_tensor(cmp[:, s], other, mine, ALU.is_gt))
                own.step(V.tensor_tensor(ceq[:, s], other, mine, ALU.is_equal))
                own.step(V.tensor_tensor(ceq[:, s], ceq[:, s], consts[:, C_LT:C_LT + 64].rearrange("p (g j) -> p g j", g=8), ALU.mult))
                own.step(V.tensor_tensor(cmp[:, s], cmp[:, s], ceq[:, s], ALU.add))
            own.step(V.tensor_reduce(rank, cmp.rearrange("p s g j -> p (s g) j"), AX, ALU.add))
            own.step(V.tensor_scalar(gmask.rearrange("p s g -> p (s g)"), rank, 4.0, None, ALU.is_lt))
            for s in range(NS):
                own.step(V.copy_predicated(selm[:, s, :].rearrange("p (g j) -> p g j", g=8), gmask[:, s, :].unsqueeze(2).broadcast_to([P, 8, 8]).bitcast(U32),
                                           sel[:, s, :].rearrange("p (g j) -> p g j", g=8)))
                own.step(V.max(best[:, s, :], selm[:, s, :]))
                own.step(V.match_replace(rep[:, s, :], best[:, s, :], selm[:, s, :], BIG))
            V.tensor_tensor(mask, rep, selm, ALU.not_equal).then_inc(lg_mask, 1)
            dve.wait_ge(lg_mask, 1)
            own.step(V.tensor_tensor(comb, score, mask, ALU.mult))
            own.step(V.tensor_reduce(wsum, comb, AX, ALU.add))
            own.step(V.reciprocal(wrec, wsum))
            for s in range(NS):
                own.mark(V.tensor_scalar(comb[:, s, :], comb[:, s, :], wrec[:, s:s + 1], ROUTED_SCALE, ALU.mult, ALU.mult))
            dve.wait_ge(cnt_ready, 1)
            for s in range(NS):
                own.mark(V.scalar_tensor_tensor(posm[:, s, :], bank[5][:, s * NE:(s + 1) * NE], 1.0, mask[:, s, :], ALU.add, ALU.mult))
            for j in range(3):
                V.tensor_scalar(nxt[0:NE, j:j + 1], bank[5][0:NE, 128:129], C * (j + 1.0), None, ALU.is_gt).then_inc(posm_done, 1)
            dve.wait_ge(posm_done, 3)
            own.step(V.tensor_tensor(nxt[0:NE, 0:1], nxt[0:NE, 0:1], nxt[0:NE, 1:2], ALU.add))
            V.tensor_tensor(nxt[0:NE, 3:4], nxt[0:NE, 0:1], nxt[0:NE, 2:3], ALU.add).then_inc(nx_done, 1)
            dve.wait_ge(nx_done, 1)
            dve.wait_ge(end_ready, 1)
            own.step(V.tensor_copy(endx[0:NE, 0:1], bank[5][0:NE, 130:131]))
            own.step(V.tensor_tensor(endx[0:NE, 1:2], endx[0:NE, 0:1], nxt[0:NE, 3:4], ALU.subtract))
            own.mark(V.tensor_scalar(hot[0:NE, :], iota_x, endx[0:NE, 0:1], None, ALU.is_ge))
            own.mark(V.tensor_scalar(hot2[0:NE, :], iota_x, endx[0:NE, 1:2], None, ALU.is_ge))
            own.step(V.tensor_scalar(hotb[0:NE, :], iota_x, endx[0:NE, 1:2], 1.0, ALU.subtract, ALU.add))
            own.step(V.tensor_tensor(hot[0:NE, :], hot2[0:NE, :], hot[0:NE, :], ALU.subtract))
            V.scalar_tensor_tensor(hotb[0:NE, :], hotb[0:NE, :], float(C), hot[0:NE, :], ALU.mult, ALU.mult).then_inc(oh_done, 1)
            dve.wait_ge(pt1_ready, 1)
            pos_t = tmp[0:NE, 0, 0:T]
            comb_t = tmp[0:NE, 0, T:2 * T]
            V.tensor_copy(tmp[0:NE, 0, :], bank[6][0:NE, :]).then_inc(pt1_copied, 1)
            dve.wait_ge(items_ready, 1)
            own.mark(V.memset(pos_i[:, :, NI:NI + 4], -1.0))
            own.mark(V.memset(comb_i[:, :, NI:NI + 4], 0.0))
            own.mark(V.memset(e_row[:, :], 0))
            own.wait()
            own.mark(V.tensor_copy(e_row[0:1, 0:NX], bank[5][0:1, 256:256 + NX]))
            own.mark(V.tensor_scalar(nwork, bank[5][0:1, 296:297], float(NE), None, ALU.add))
            for s in range(NS):
                own.mark(V.tensor_scalar(pos_i[:, s, 0:NE], posm[:, s, :], 1.0, None, ALU.subtract))
                own.mark(V.tensor_copy(comb_i[:, s, 0:NE], comb[:, s, :]))
                own.mark(V.tensor_scalar(pos_i[:, s, NE:NI], bank[5][:, 320 + s * NX:320 + (s + 1) * NX], 1.0, None, ALU.subtract))
                V.tensor_copy(comb_i[:, s, NE:NI], bank[5][:, 384 + s * NX:384 + (s + 1) * NX]).then_inc(items_done, 1)

            for j in range(4):
                s, hf = j // 2, j % 2
                dve.wait_ge(gr_ready, j + 1)
                V.tensor_copy(g2row[:, s, hf * 512:(hf + 1) * 512], bank[4 + j][:, :]).then_inc(gr_done, 1)
            filled(dve, "su")
            evacuated(dve, "sg")
            V.tensor_tensor(act_s[:, :, :].rearrange("p c t -> p (c t)"), sil_s[:, :, :].rearrange("p c t -> p (c t)"), fill_bank("su")[:, :], ALU.mult).then_inc(dve_evac, 1)

            iota2 = consts[:, C_IOTA:C_IOTA + C].unsqueeze(1).broadcast_to([P, 2, C])

            def one_hots(b, p2):
                for s in range(NS):
                    V.tensor_tensor(sel_p[b][:, s, :].rearrange("t (e j) -> t e j", e=2), iota2,
                                    pos_i[:, s, bass.ds(p2, 2)].unsqueeze(2).broadcast_to([P, 2, C]), ALU.is_equal)
                ins = V.tensor_copy(comb_p[b][:, :, :], comb_i[:, :, bass.ds(p2, 2)])
                ins.then_inc(built, 1)

            def transposed(b, p1):
                dve.wait_ge(pt_ready, p1)
                V.tensor_copy(sel_t[b][:, :], bank[0][:, 0:T])
                V.tensor_copy(w_slot[b][0:C, :], bank[0][0:C, T:T + 1])
                V.tensor_copy(w_slot[b][C:P, :], bank[0][C:P, T + 1:T + 2]).then_inc(pt_evac, 1)

            def right_half(b, p1):
                dve.wait_ge(gbk_ready, p1)
                V.tensor_copy(xg[b][:, 4:8, :].rearrange("p k n -> p (k n)"), bank[1][:, :]).then_inc(gbk_evac, 1)

            own.mark(V.memset(sel_t[1][:, :].bitcast(F32), 0.0))
            own.mark(V.memset(y_hi[1][:, :].bitcast(F32), 0.0))
            own.wait()
            V.memset(y_lo[1][:, :].bitcast(F32), 0.0).then_inc(y_ready, 1)
            one_hots(0, 0)
            right_half(0, 1)
            transposed(0, 1)

            def pair(b, p):
                one_hots(1 - b, p * 2 + 2)
                dve.wait_ge(sil_ready, p + 1)
                V.tensor_tensor(act_t[b][:, :, :].rearrange("p c n -> p (c n)"), sil[:, :], bank[2][:, 2 * P:4 * P], ALU.mult).then_inc(act_ready, 1)

                def low(h):
                    dve.wait_ge(hi_ready, p * 2 + (h + 1))
                    V.scalar_tensor_tensor(y_lo[h][:, :], bank[3][:, :], w_slot[b][:, 0:1], y_hi[h][:, :].bitcast(F32),
                                           ALU.mult, ALU.subtract).then_inc(y_ready, 1)

                low(0)
                right_half(1 - b, p + 2)
                transposed(1 - b, p + 2)
                low(1)

            loop(dve, pair)
            V.memset(small[:, 179:180], 0.0).then_inc(loop_done, 1)

            dve.wait_ge(y_done, 1)
            for s in range(NS):
                for hf in range(2):
                    c = slice(hf * 512, (hf + 1) * 512)
                    own.step(V.tensor_tensor(fin[:, s, c], g2row[:, s, c], y_acc[s][hf][:, :], ALU.mult))
                    ins = V.tensor_tensor(fin[:, s, c], fin[:, s, c], x1[:, s, c], ALU.add)
                    if hf:
                        ins.then_inc(x2_done, 1)
                    else:
                        own.mark(ins)
            dve.wait_ge(own_act, 6)
            V.tensor_scalar(ssqf, ssqf, 1.0 / D, EPS, ALU.mult, ALU.add).then_inc(f_ssq, 1)
            dve.wait_ge(f_rms, 1)
            dve.wait_ge(s_fing, 16)
            for s in range(NS):
                V.scalar_tensor_tensor(fin[:, s, :], fin[:, s, :], rmsf[:, s:s + 1], fin_g[:, :], ALU.mult, ALU.mult).then_inc(out_done, 1)

        @block.tensor
        def _(pe):
            mm = nc.tensor.matmul

            def arrived(name):
                n = number[name]
                pe.wait_ge(s_w[n % 4], 16 * (n // 4 + 1))

            def open_fill(name, j=0):
                n = fill_no[name, j]
                if n >= 4:
                    pe.wait_ge(fills[n - 4][2], fills[n - 4][3])
                return bank[n % 4]

            pe.wait_ge(s_cst, 16)
            pe.wait_ge(s_rows, 16 * 12)
            nc.tensor.transpose(bank[7][:, 0:R_ALL], rows[0:R_ALL, :], ident[0:R_ALL, 0:R_ALL])
            nc.tensor.transpose(bank[7][:, P:P + CW * CC], rows_dw[0:CW * CC, :], ident[0:CW * CC, 0:CW * CC]).then_inc(vec_ready, 1)
            pe.wait_ge(s_x, 32)

            def to_channels(name, src, j):
                b = open_fill(*name)
                for kk in range(2):
                    for s in range(NS):
                        k = 2 * j + kk
                        ins = nc.tensor.transpose(b[:, kk * T + s * P:kk * T + (s + 1) * P], src[:, s, k * P:(k + 1) * P], ident)
                return ins

            for j in range(4):
                to_channels((f"xt{j}", 0), x_tok, j).then_inc(proj_ready, 1)

            def ada(j, tail=None):
                arrived(f"ada{j}")
                w = tile_of(f"ada{j}")
                for c in range(4):
                    col = 256 + 2 * (4 * j + c)
                    for k in range(KD):
                        ins = mm(bank[7][:, col:col + 2], w[:, k, c * P:(c + 1) * P], csil.rearrange("p (s k) -> p k s", s=NS)[:, k, :], start=(k == 0), stop=(k == KD - 1))
                ins.then_inc(mod_ready, 1)

            pe.wait_ge(vec_copied, 2)
            pe.wait_ge(c_silu, 1)
            for j in range(4):
                ada(j)
            pe.wait_ge(xn_done, 2)
            for j in range(4):
                to_channels((f"h{j}", 0), xn, j).then_inc(proj_ready, 1)

            def project(name, rhs, kk=KD, n=2):
                arrived(name)
                w = tile_of(name)
                for j in range(n):
                    b = open_fill(name, j)
                    for c in range(2):
                        col = (2 * j + c) * P
                        for k in range(kk):
                            ins = mm(b[:, c * T:(c + 1) * T], w[:, k, col:col + P], rhs[:, k, :], start=(k == 0), stop=(k == kk - 1))
                            if k == kk - 1 and c == 1:
                                ins.then_inc(proj_ready, 1)

            def project_tokens(name):
                arrived(name)
                w = tile_of(name)
                for s in range(NS):
                    b = open_fill(name, s)
                    for k in range(KD):
                        ins = mm(b[:, :], h_t[:, k, s * P:(s + 1) * P], w[:, k, :], start=(k == 0), stop=(k == KD - 1))
                    ins.then_inc(proj_ready, 1)

            def scores(level):
                for g in range(4):
                    n = 4 * (level + 1) + g
                    if n >= 2:
                        pe.wait_ge(sc_used, n - 1)
                    for i in range(4):
                        out, at_ = bank[4 + n % 2][:, i * P:(i + 1) * P], 4 * g + i
                        if level < 0:
                            q = qk[:, 1, at_ * P:(at_ + 1) * P]
                            mm(out, qk[:, 2, at_ * P:(at_ + 1) * P], q, start=True, stop=False)
                            ins = mm(out, qk[:, 3, at_ * P:(at_ + 1) * P], q, start=False, stop=True)
                        else:
                            ins = mm(out, k_mix[:, at_ * P:(at_ + 1) * P], query_mix(level, at_), start=True, stop=True)
                    ins.then_inc(sc_ready, 1)

            evacuated(pe, "h3")
            for name in ("u1", "u2", "q0", "zf0", "zb0", "q1", "zf1", "zb1"):
                project(name, h_t)
            project_tokens("v0")
            project_tokens("v1")
            pe.wait_ge(fk_done, 32)
            evacuated(pe, "q1", 1)
            scores(-1)
            pe.wait_ge(conv_done, CC)
            pe.wait_ge(s_init, 3)
            for c in range(CC):
                ins = mm(bank[6][:, 0:T], ones[:, :], conv[:, c, :], start=(c == 0), stop=(c == CC - 1))
            ins.then_inc(mean_ready, 1)
            between = ["og0", "og1", "ga0", "ga1", "gb0", "gb1"]
            for level in range(LEVELS):
                if level < 6:
                    project(between[level], h_t)
                pe.wait_ge(q_done, 2 * (level + 1))
                pe.wait_ge(mix_done, level + 1)
                scores(level)
                if level == 3:
                    pe.wait_ge(csq_done, 1)
                    sq = upad[:, :, :, :].rearrange("p c s u -> p (c s u)")
                    for s in range(NS):
                        for c in range(CC):
                            ins = mm(bank[6][:, 256 + s:257 + s], sq[:, c * T + s * P:c * T + (s + 1) * P], ones[:, 0:1], start=(c == 0), stop=(c == CC - 1))
                    ins.then_inc(cvar_ready, 1)
                if level == 5:
                    pe.wait_ge(cdiag_done, 2)
                    mm(bank[6][:, 0:T], ones[:, :], tmp[:, 0, 0:T], start=True, stop=True).then_inc(cb_ready, 1)
            pe.wait_ge(mod_done, 2)
            for j in range(4, 12):
                ada(j)
            pe.wait_ge(sc_used, 4 * (LEVELS + 1))
            pe.wait_ge(q_done, 2 * (LEVELS + 1))
            pe.wait_ge(s_s0, 16)
            evacuated(pe, "v1", 1)

            def squares(g):
                pe.wait_ge(o_copied, g + 1)
                if g == 0:
                    pe.wait_ge(mod_done, 4)
                for i in range(4):
                    col = 384 + 4 * g + i
                    ins = mm(bank[7][:, col:col + 1], tmp[:, g % 2, i * P:(i + 1) * P], ones[:, 0:1], start=True, stop=True)
                ins.then_inc(osq_ready, 1)

            for g in range(4):
                if g >= 2:
                    squares(g - 2)
                for i in range(4):
                    at_ = 4 * g + i
                    h, s = at_ // 2, at_ % 2
                    out = bank[4 + g % 2][:, i * P:(i + 1) * P]
                    ins = mm(out, v_tok[:, s, h * P:(h + 1) * P], att[:, at_, :], start=True, stop=(s == 0))
                    if s:
                        mm(out, s0[:, h, :], qk[:, 1, at_ * P:(at_ + 1) * P], start=False, stop=False)
                        ins = mm(out, s0[:, H + h, :], qk[:, 0, at_ * P:(at_ + 1) * P], start=False, stop=True)
                ins.then_inc(o_ready, 1)
            squares(2)
            squares(3)
            pe.wait_ge(cact_done, CC)
            project("pc", conv, kk=CC, n=4)
            for g in range(4):
                pe.wait_ge(odiag_done, 4 * (g + 1))
                if g >= 2:
                    pe.wait_ge(ob_used, g - 1)
                mm(bank[4 + g % 2][:, :], ones[:, :], tmp[:, g % 2, :], start=True, stop=True).then_inc(ob_ready, 1)
            pe.wait_ge(k_done, 2 * LEVELS)
            for r_ in range(4):
                if r_:
                    pe.wait_ge(kt_copied, r_)
                for i in range(4):
                    d, h = divmod(4 * r_ + i, H)
                    ins = nc.tensor.transpose(bank[6][:, i * P:(i + 1) * P], qk[:, 2 + d, 2 * h * P:(2 * h + 1) * P], ident)
                ins.then_inc(kt_ready, 1)
            for r_ in range(4):
                if r_:
                    pe.wait_ge(st_copied, r_)
                else:
                    pe.wait_ge(kt_copied, 4)
                for i in range(4):
                    h = (4 * r_ + i) % H
                    ins = mm(bank[6][:, i * P:(i + 1) * P], k_tok[:, 4 * r_ + i, :], v_tok[:, 0, h * P:(h + 1) * P], start=True, stop=True)
                ins.then_inc(st_ready, 1)
            pe.wait_ge(ob_used, 4)
            project("ph0", o_t)
            project("ph1", o_t)
            pe.wait_ge(merged, 4)
            project("wo0", ga)
            project("wo1", ga)

            def to_tokens(name, src):
                for j in range(4):
                    s, hf = j // 2, j % 2
                    b = open_fill(name, j)
                    for i in range(4):
                        ins = nc.tensor.transpose(b[:, i * P:(i + 1) * P], src[:, 4 * hf + i, s * P:(s + 1) * P], ident)
                    ins.then_inc(proj_ready, 1)

            evacuated(pe, "wo1", 1)
            to_tokens("t1", x_t)
            pe.wait_ge(xn2_done, 2)
            for j in range(4):
                to_channels(("n2", j), xn2, j).then_inc(proj_ready, 1)
            evacuated(pe, "n2", 3)
            pe.wait_ge(s_wr, 16)
            for s in range(NS):
                for k in range(KD):
                    ins = mm(bank[4][:, s * NE:(s + 1) * NE], h_t[:, k, s * P:(s + 1) * P], w_r[:, k, :], start=(k == 0), stop=(k == KD - 1))
            ins.then_inc(lg_ready, 1)
            to_tokens("hr", h_t)
            arrived("sg")
            for name, col in (("sg", 0), ("su", FF)):
                b = open_fill(name)
                for c in range(2):
                    for k in range(KD):
                        ins = mm(b[:, c * T:(c + 1) * T], tile_of("sg")[:, k, col + c * P:col + (c + 1) * P], h_t[:, k, :], start=(k == 0), stop=(k == KD - 1))
                ins.then_inc(proj_ready, 1)
            tri = consts[:, C_TRI:C_TRI + P]
            pe.wait_ge(lg_mask, 1)
            mm(bank[5][:, 0:NE], tri, mask[:, 0, :], start=True, stop=True)
            mm(bank[5][:, NE:2 * NE], tri, mask[:, 1, :], start=True, stop=False)
            mm(bank[5][:, NE:2 * NE], ones[:, :], mask[:, 0, :], start=False, stop=True)
            for s in range(NS):
                ins = mm(bank[5][0:NE, 128:129], mask[:, s, :], ones[:, 0:1], start=(s == 0), stop=(s == 1))
            ins.then_inc(cnt_ready, 1)
            pe.wait_ge(nx_done, 1)
            mm(bank[5][0:NE, 130:131], consts[0:NE, C_TRIE:C_TRIE + NE], nxt[0:NE, 3:4], start=True, stop=True).then_inc(end_ready, 1)
            for s in range(NS):
                nc.tensor.transpose(bank[6][0:NE, s * P:(s + 1) * P], posm[:, s, :], ident)
                ins = nc.tensor.transpose(bank[6][0:NE, T + s * P:T + (s + 1) * P], comb[:, s, :], ident)
            ins.then_inc(pt1_ready, 1)
            pe.wait_ge(oh_done, 1)
            pe.wait_ge(pt1_copied, 1)
            for s in range(NS):
                out = bank[5][:, 320 + s * NX:320 + (s + 1) * NX]
                mm(out, tmp[0:NE, 0, s * P:(s + 1) * P], hot[0:NE, :], start=True, stop=False)
                mm(out, neg[0:NE, :], hotb[0:NE, :], start=False, stop=True)
                mm(bank[5][:, 384 + s * NX:384 + (s + 1) * NX], tmp[0:NE, 0, T + s * P:T + (s + 1) * P], hot[0:NE, :], start=True, stop=True)
            mm(bank[5][0:1, 256:256 + NX], consts[0:NE, C_ECOL:C_ECOL + 1], hot[0:NE, :], start=True, stop=True)
            mm(bank[5][0:1, 296:297], nxt[0:NE, 3:4], ones[0:NE, 0:1], start=True, stop=True).then_inc(items_ready, 1)
            pe.wait_ge(items_done, 2)
            for j in range(4):
                s, hf = j // 2, j % 2
                for i in range(4):
                    k = 4 * hf + i
                    ins = mm(bank[4 + j][:, i * P:(i + 1) * P], mod_v[:, M_GT2 + k, s:s + 1].broadcast_to([P, P]), ident, start=True, stop=True)
                ins.then_inc(gr_ready, 1)

            def gather(b, half, p1):
                for i in range(4):
                    k = 4 * half + i
                    for n, (s, part) in enumerate(((0, h_hi), (0, h_lo), (1, h_hi), (1, h_lo))):
                        ins = mm(bank[half][:, i * P:(i + 1) * P], part[:, s, k, :], sel_p[b][:, s, :], start=(n == 0), stop=(n == 3))
                ins.then_inc(gbk_ready if half else ga_ready, 1)

            def turn(b):
                for s in range(NS):
                    nc.tensor.transpose(bank[0][:, s * P:(s + 1) * P], sel_p[b][:, s, :].bitcast(F32), ident)
                for s in range(NS):
                    ins = mm(bank[0][:, T:T + 2], sel_p[b][:, s, :].bitcast(F32), comb_p[b][:, s, :], start=(s == 0), stop=(s == 1))
                ins.then_inc(pt_ready, 1)

            def scatter(b, h, start=False):
                for s in range(NS):
                    for part in ((y_hi,) if start else (y_hi, y_lo)):
                        ins = mm(y_acc[s][h][:, :], sel_t[b][:, s * P:(s + 1) * P], part[1 if start else h][:, :], start=start, stop=False)
                return ins

            pe.wait_ge(gr_done, 4)
            pe.wait_ge(y_ready, 1)
            for h in range(2):
                scatter(1, h, start=True)
            pe.wait_ge(built, 1)
            evacuated(pe, "hr", 2)
            evacuated(pe, "hr", 3)
            gather(0, 0, 1)
            gather(0, 1, 1)
            pe.wait_ge(ga_evac, 1)
            turn(0)
            evacuated(pe, "sg")
            evacuated(pe, "su")

            def pair(b, p):
                slots = (2 * b, 2 * b + 1)
                i = p // 2 if isinstance(p, int) else iteration[0]
                pe.wait_ge(gbk_evac, p + 1)
                for e in range(2):
                    pe.wait_ge(s_gu[slots[e]], i * 16 + 16)
                    for f in range(4):
                        for k in range(KD):
                            ins = mm(bank[2][:, f * P + e * C:f * P + (e + 1) * C], w_gu[slots[e]][:, k, f * P:(f + 1) * P], xg[b][:, k, e * C:(e + 1) * C],
                                     start=(k == 0), stop=(k == KD - 1))
                ins.then_inc(gu_ready, 1)
                pe.wait_ge(y_ready, p * 2 + 1)
                scatter(1 - b, 1)
                pe.wait_ge(built, p + 2)
                pe.wait_ge(pt_evac, p + 1)
                gather(1 - b, 0, p + 2)
                pe.wait_ge(act_ready, p + 1)

                def down(h):
                    for e in range(2):
                        for c in range(2):
                            ins = mm(bank[3][e * C:(e + 1) * C, :], act_t[b][:, c, e * C:(e + 1) * C], w_dn[slots[e]][:, c, h * 512:(h + 1) * 512],
                                     start=(c == 0), stop=(c == 1))
                    ins.then_inc(dn_ready, 1)

                for e in range(2):
                    pe.wait_ge(s_dn[slots[e]], i * 16 + 16)
                down(0)
                gather(1 - b, 1, p + 2)
                pe.wait_ge(ga_evac, p + 2)
                turn(1 - b)
                pe.wait_ge(y_ready, p * 2 + 2)
                scatter(b, 0)
                down(1)

            iteration = [None]
            if USE_IF:
                n = pe.value_load(nwork, min_val=0, max_val=NI)
            with pe.Fori(0, ITERS) as i:
                iteration[0] = i
                if USE_IF:
                    with pe.If(n > i * 4):
                        for b in range(2):
                            pair(b, i * 2 + b)
                else:
                    for b in range(2):
                        pair(b, i * 2 + b)
            pe.wait_ge(loop_done, 1)
            scatter(1, 1)
            pe.wait_ge(s_sd, 16)
            for s in range(NS):
                for hf in range(2):
                    for c in range(2):
                        ins = mm(y_acc[s][hf][:, :], act_s[:, c, s * P:(s + 1) * P], w_sd[:, c, hf * 512:(hf + 1) * 512], start=False, stop=(c == 1))
            ins.then_inc(y_done, 1)


INPUTS = ["x_prompt", "x_sample", "state_hgrn", "c", "c_ctx", "w_ada", "b_ada", "norm1_g", "w_in", "hgrn_lb_logits", "hgrn_norm_g",
          "w_proj_hgrn", "conv_dw_w", "conv_dw_b", "conv_norm_g", "conv_norm_b", "w_proj_conv", "w_out", "norm2_g", "w_router",
          "router_bias", "w_expert_gate_up", "w_expert_down", "w_shared_gate_up", "w_shared_down", "final_norm_g"]


def constants():
    import numpy as np

    n = np.arange(P)
    out = np.zeros((P, C_ALL), np.float32)
    out[:, C_ID:C_ID + P] = n[:, None] == n
    for level in range(LEVELS):
        out[:, C_MASK + P * level:C_MASK + P * (level + 1)] = ((n[:, None] ^ n) >> level) == 1
    out[:, C_TRI:C_TRI + P] = n[:, None] < n
    out[:NE, C_TRIE:C_TRIE + NE] = n[:NE, None] <= n[:NE]
    out[:, C_IOTA:C_IOTA + C] = n[:C]
    out[:, C_LT:C_LT + 64] = (np.arange(8)[:, None] > np.arange(8)).reshape(-1)
    out[:, C_ECOL] = n
    return out


def kernel(**inputs):
    import numpy as np
    import concourse.bacc as bacc
    from concourse.bass_utils import run_bass_kernel_spmd

    nc = bacc.Bacc("TRN2", target_bir_lowering=False, num_devices=1)
    arrays, aps = {}, {}
    for name in INPUTS:
        array = np.ascontiguousarray(inputs[name])
        arrays[f"in_{name}"] = array
        aps[name] = nc.dram_tensor(f"in_{name}", array.shape, mybir.dt.from_np(array.dtype), kind="ExternalInput").ap()
    arrays["in_consts"] = constants()
    aps["consts"] = nc.dram_tensor("in_consts", (P, C_ALL), F32, kind="ExternalInput").ap()
    shapes = [(1, P, D), (1, P, D), (1, 1, 2, H, P, P)]
    outs = [nc.dram_tensor(f"out_{i}", shape, F32, kind="ExternalOutput").ap() for i, shape in enumerate(shapes)]
    build(nc, aps, outs)
    result = run_bass_kernel_spmd(nc, [arrays], core_ids=[0]).results[0]
    return tuple(result[f"out_{i}"] for i in range(len(shapes)))
```

```python
from contextlib import ExitStack

import concourse.bass as bass
from concourse import mybir
from concourse.alu_op_type import AluOpType as ALU

ACT = mybir.ActivationFunctionType
F32 = mybir.dt.float32
F32R = mybir.dt.float32r
I32 = mybir.dt.int32
U32 = mybir.dt.uint32
AX = mybir.AxisListType.X

P = 128
D = 1024
KD = D // P
NS = 2
T = NS * P
H = 8
NE = 64
FF = 256
TOPK = 8
ROUTED_SCALE = 2.5
EPS = 1e-6
CW = 31
CC = 4
PAD = CW // 2
UW = P + 2 * PAD
C = 64
LEVELS = 7

NX = T * TOPK // C
NI = NE + NX
ITERS = NI // 4
MAIN = NE // 4
BIG = 3.0e38
USE_IF = True

C_ID, C_MASK = 0, P
C_TRI = C_MASK + LEVELS * P
C_TRIE = C_TRI + P
C_IOTA = C_TRIE + NE
C_LT = C_IOTA + C
C_ECOL = C_LT + 64
C_SUM = C_ECOL + 1
C_ALL = C_SUM + NS

R_C, R_BADA, R_G1, R_G2, R_HG, R_LB = 0, 16, 64, 72, 80, 88
R_DWB, R_CNG, R_CNB = 104, 108, 112
R_ALL = 116

Q0, V0, ZF0, ZB0, OG0, U0, GZ0 = 0, 1024, 2048, 3072, 4096, 5120, 6144
M_SH1, M_SC1, M_GT1, M_SH2, M_SC2, M_GT2 = 0, 8, 16, 24, 32, 40

KB = 1024
BASE = 16512


class Own:

    def __init__(self, eng, sem):
        self.eng, self.sem, self.n = eng, sem, 0

    def mark(self, instruction):
        instruction.then_inc(self.sem, 1)
        self.n += 1
        return self.n

    def wait(self, n=None):
        self.eng.wait_ge(self.sem, self.n if n is None else n)

    def step(self, instruction):
        self.mark(instruction)
        self.wait()


def build(nc, A, outs):
    y_prompt, y_sample, new_state = outs
    ctx = ExitStack()
    with ctx:
        def at(name, kb, shape, dt=F32):
            return nc.alloc_sbuf_tensor_at(name, shape, dt, offset=BASE + int(kb * KB))

        def sem(name):
            return ctx.enter_context(nc.semaphore(name))

        ring = [at(f"ring{i}", 16 * i, [P, 4096]) for i in range(4)]
        ga = at("ga", 64, [P, H, T])
        gb = at("gb", 72, [P, H, T])
        att = at("att", 80, [P, 16, P])
        og = at("og", 88, [P, H, T])
        x_t = at("x_t", 96, [P, KD, T])
        h_t = at("h_t", 104, [P, KD, T])
        qk = at("qk", 112, [P, 4, 16 * P])
        xn = at("xn", 128, [P, NS, D])
        fg = at("fg", 144, [P, 2, 16 * P])
        o_t = at("o_t", 144, [P, H, T])
        k_tok = at("k_tok", 152, [P, 16, P])
        x_tok = at("x_tok", 160, [P, NS, D])
        v_tok = at("v_tok", 160, [P, NS, D])
        s0 = at("s0", 168, [P, 16, P])
        upad = at("upad", 176, [P, CC, NS, UW])
        conv = at("conv", 181, [P, CC, T])
        tmp = at("tmp", 185, [P, 2, 512])
        consts = at("consts", 189, [P, C_ALL])
        vec = at("vec", 194.5, [P, P])
        small = at("small", 195, [P, 256])
        ones = at("ones", 196, [P, P])
        dw = at("dw", 196.5, [P, CW, CC])
        rows = at("rows", 197, [P, P])
        rows_dw = at("rows_dw", 198, [P, P])
        s_new = at("s_new", 197, [P, 16, P])
        k_mix = at("k_mix", 197, [P, 16 * P])
        w_r = at("w_r", 181, [P, KD, NE])
        c_pad = at("c_pad", 205, [P, KD, 32])
        b_router = at("b_router", 207, [P, NE])
        mod = at("mod", 207.25, [P, 48, NS])
        w_gu = [at(f"w_gu{i}", 24 * i, [P, KD, 2 * FF]) for i in range(4)]
        w_dn = [at(f"w_dn{i}", 24 * i + 16, [P, 2, D]) for i in range(4)]
        h_hi = at("h_hi", 112, [P, NS, KD, P], F32R)
        h_lo = at("h_lo", 120, [P, NS, KD, P], F32R)
        x1 = at("x1", 128, [P, NS, D])
        xn2 = at("xn2", 136, [P, NS, D])
        g2row = at("g2row", 136, [P, NS, D])
        xg = [at(f"xg{i}", 144 + 4 * i, [P, KD, P]) for i in range(2)]
        sel_p = [at(f"sel_p{i}", 152 + i, [P, NS, P], F32R) for i in range(2)]
        sel_t = [at(f"sel_t{i}", 154 + i, [P, T], F32R) for i in range(2)]
        act_t = at("act_t", 156, [P, 2, P])
        act_r = at("act_r", 157, [P, 2 * P])
        sil = at("sil", 158, [P, 2 * P])
        y_hi = [at(f"y_hi{i}", 160 + 2 * i, [P, 512], F32R) for i in range(2)]
        y_lo = [at(f"y_lo{i}", 164 + 2 * i, [P, 512], F32R) for i in range(2)]
        fin_g = at("fin_g", 168, [P, D])
        pos_i = at("pos_i", 172, [P, NS, NI + 4])
        comb_i = at("comb_i", 173, [P, NS, NI + 4])
        comb_p = [at(f"comb_p{i}", 174 + i / 32, [P, NS, 2]) for i in range(2)]
        w_slot = [at(f"w_slot{i}", 174.125 + i / 32, [P, 1]) for i in range(2)]
        e_row = at("e_row", 174.5, [P, NX + 4], I32)
        act_s = at("act_s", 176, [P, 2, T])
        sil_s = at("sil_s", 178, [P, 2, T])
        w_sg = at("w_sg", 80, [P, KD, 2 * FF])
        w_sd = at("w_sd", 104, [P, 2, D])
        fin = at("fin", 96, [P, NS, D])
        rt = at("rt", 197, [P, 2048])

        def pb(name):
            return ctx.enter_context(nc.psum_tensor(name, [P, 512], F32))

        bank = [pb(f"bank{i}") for i in range(8)]
        y_acc = [[bank[4 + 2 * s + h] for h in range(2)] for s in range(NS)]

        ident = consts[:, C_ID:C_ID + P]

        def sm(lo, n):
            return small[:, lo:lo + n]

        csil = sm(0, 16)
        gain1 = sm(16, 16)
        gain2 = sm(32, 16)
        lb = sm(48, 16)
        oml = sm(64, 16)
        csig = sm(80, 16)
        ssq = sm(96, 2)
        rms = sm(98, 2)
        ssq_c = sm(100, 2)
        rms_c = sm(102, 2)
        ssq_o = sm(104, 16)
        rms_o = sm(120, 16)
        mhalf = sm(136, 16)
        ssq2 = sm(152, 2)
        rms2 = sm(154, 2)
        ssqf = sm(156, 2)
        rmsf = sm(158, 2)
        nwork = small[0:1, 162:163].bitcast(I32)
        mod_v = mod[:, :, :]

        s_x, s_cst, s_rows, s_s0, s_wr, s_fing = map(sem, ("x_loaded", "consts_loaded", "rows_loaded", "s0_loaded", "router_loaded", "fing_loaded"))
        s_w = [sem(f"ring_loaded{i}") for i in range(4)]
        s_gu = [sem(f"gu_loaded{i}") for i in range(4)]
        s_dn = [sem(f"dn_loaded{i}") for i in range(4)]
        s_init = sem("init_done")
        own_dve, own_act, own_pool = sem("own_dve"), sem("own_act"), sem("own_pool")
        vec_ready, vec_copied = sem("vec_ready"), sem("vec_copied")
        ssq_ready, rms_ready = sem("ssq_ready"), sem("rms_ready")
        s_pad, part_ready, part_copied = sem("pad_zeroed"), sem("ada_partial"), sem("ada_partial_copied")
        c_sig, c_silu = sem("c_sig"), sem("c_silu")
        xt_ready, xt_copied = sem("xt_ready"), sem("xt_copied")
        xn_done = sem("xn_done")
        mod_ready, mod_done = sem("mod_ready"), sem("mod_done")
        proj_ready = sem("proj_ready")
        act_evac, dve_evac = sem("act_evac"), sem("dve_evac")
        u_gated, fk_done, og_sig = sem("u_gated"), sem("fk_done"), sem("og_sig")
        sc_ready, sc_used = sem("scores_ready"), sem("scores_used")
        mix_done = sem("keys_mixed")
        q_done, k_done, tot_done = sem("q_updated"), sem("k_updated"), sem("totals_done")
        conv_done, mean_ready, cen_done, csq_done = map(sem, ("conv_done", "mean_ready", "centred", "conv_squared"))
        cvar_ready, cms_done, crms_done, cdiag_done = map(sem, ("cvar_ready", "cms_done", "crms_done", "cdiag_done"))
        cb_ready, cn_done, cs_done, cact_done = map(sem, ("conv_bcast_ready", "conv_normed", "conv_sig", "conv_act"))
        o_ready, o_copied, osq_ready = sem("o_ready"), sem("o_copied"), sem("o_ssq_ready")
        oms_done, orms_done = sem("o_ms_done"), sem("o_rms_done")
        odiag_done, ob_ready, ob_used = sem("o_diag_done"), sem("o_bcast_ready"), sem("o_normed")
        kt_ready, kt_copied, st_ready, st_copied, s_state = map(sem, ("k_tok_ready", "k_tok_copied", "state_ready", "state_copied", "state_stored"))
        merged = sem("merged")
        tt_ready, tt_copied = sem("x1_tok_ready"), sem("x1_tok_copied")
        ssq2_done, rms2_done, xn2_done = sem("ssq2_done"), sem("rms2_done"), sem("xn2_done")
        lg_ready, lg_sig, lg_mask = sem("logits_ready"), sem("scores_done"), sem("mask_done")
        hr_ready, hr_hi, hr_done = sem("h2_tok_ready"), sem("h2_hi_done"), sem("h2_tok_done")
        s_sg, s_sd = sem("shared_gate_up_loaded"), sem("shared_down_loaded")
        cnt_ready, nx_done, end_ready, oh_done = map(sem, ("count_ready", "nx_done", "end_ready", "onehot_done"))
        posm_done, pt1_ready, pt1_copied = sem("posm_done"), sem("post_ready"), sem("post_copied")
        items_ready, items_done = sem("items_ready"), sem("items_done")
        gr_ready, gr_done = sem("g2row_ready"), sem("g2row_done")
        built, ga_ready, ga_evac, gbk_ready, gbk_evac = map(sem, ("built", "gather_a", "gather_a_evac", "gather_b", "gather_b_evac"))
        pt_ready, pt_evac = sem("sel_t_ready"), sem("sel_t_evac")
        gu_ready, sil_ready, act_ready = sem("gu_ready"), sem("sil_ready"), sem("act_ready")
        t_ready, t_evac = sem("act_t_ready"), sem("act_t_evac")
        dn_ready, hi_ready, y_ready = sem("dn_ready"), sem("y_hi_ready"), sem("y_split_ready")
        loop_done, y_done, x2_done, f_ssq, f_rms, out_done, s_out = map(sem, ("loop_done", "y_done", "x2_done", "final_ssq", "final_rms", "out_done", "stored"))

        def cols(w, c0):
            return w.rearrange("(k p) c -> p k c", p=P)[:, :, c0:c0 + 512]

        w_ada, w_in = A["w_ada"][0], A["w_in"][0]
        blocks = [(f"ada{j}", cols(w_ada, 512 * j)) for j in range(4)]
        ada_after = {name: 4 + n for n, name in enumerate(("u1", "u2", "q0", "zf0", "zb0", "q1", "zf1", "zb1"))}
        for name, c0 in (("u1", U0), ("u2", U0 + 512), ("q0", Q0), ("zf0", ZF0), ("zb0", ZB0), ("q1", Q0 + 512),
                         ("zf1", ZF0 + 512), ("zb1", ZB0 + 512), ("v0", V0), ("v1", V0 + 512),
                         ("og0", OG0), ("og1", OG0 + 512), ("ga0", GZ0), ("ga1", GZ0 + 512), ("gb0", GZ0 + 1024), ("gb1", GZ0 + 1536)):
            blocks.append((name, cols(w_in, c0)))
            if name in ada_after:
                j = ada_after[name]
                blocks.append((f"ada{j}", cols(w_ada, 512 * j)))
        blocks.append(("pc", A["w_proj_conv"][0].rearrange("(k p) c -> p k c", p=P)))
        blocks += [(f"ph{j}", cols(A["w_proj_hgrn"][0], 512 * j)) for j in range(2)]
        blocks += [(f"wo{j}", cols(A["w_out"][0], 512 * j)) for j in range(2)]
        number = {name: n for n, (name, _) in enumerate(blocks)}

        def tile_of(name):
            src = blocks[number[name]][1]
            k, n = src.shape[1], src.shape[2]
            return ring[number[name] % 4][:, 0:k * n].rearrange("p (k c) -> p k c", k=k)

        gu_src = A["w_expert_gate_up"][0].rearrange("e (p k) f -> e p k f", k=KD)
        dn_src = A["w_expert_down"][0].rearrange("e (c p) d -> e p c d", p=P)

        fills, n_act, n_dve = [], 0, 0
        for name, n, by in ([(f"xt{j}", 1, "act") for j in range(4)] + [(f"h{j}", 1, "dve") for j in range(4)]
                            + [("u1", 2, "act"), ("u2", 2, "act"), ("q0", 2, "act"), ("zf0", 2, "act"), ("zb0", 2, "act"),
                               ("q1", 2, "act"), ("zf1", 2, "act"), ("zb1", 2, "act"), ("v0", 2, "act"), ("v1", 2, "act"),
                               ("og0", 2, "dve"), ("og1", 2, "dve"), ("ga0", 2, "act"), ("ga1", 2, "act"), ("gb0", 2, "act"),
                               ("gb1", 2, "act"), ("pc", 4, "dve"), ("kt", 4, "act"), ("st", 4, "act"), ("ph0", 2, "dve"), ("ph1", 2, "dve"), ("wo0", 2, "dve"), ("wo1", 2, "dve"),
                               ("t1", 4, "act"), ("n2", 4, "dve"), ("hr", 4, "dve"), ("sg", 1, "act"), ("su", 1, "dve")]):
            for j in range(n):
                if by == "act":
                    n_act += 1
                    fills.append((name, j, act_evac, n_act))
                else:
                    n_dve += 1
                    fills.append((name, j, dve_evac, n_dve))
        fill_no = {(name, j): n for n, (name, j, _, _) in enumerate(fills)}

        def fill_bank(name, j=0):
            return bank[fill_no[name, j] % 4]

        def released(eng, name):
            if name[:3] == "ada":
                eng.wait_ge(part_ready, int(name[3:]) + 1)
            else:
                last = {"pc": ("pc", 3)}.get(name, (name, 1))
                eng.wait_ge(proj_ready, fill_no[last] + 1)

        def evacuated(eng, name, j=0):
            eng.wait_ge(fills[fill_no[name, j]][2], fills[fill_no[name, j]][3])

        def filled(eng, name, j=0):
            eng.wait_ge(proj_ready, fill_no[name, j] + 1)

        def query_mix(level, g):
            m = 1 << level
            base = qk[:, 0, g * P:(g + 1) * P]
            dims = [list(base.ap[0]), [2 * m, P // (2 * m)], [16 * P + m, 2]]
            if m > 1:
                dims.append([1, m])
            return bass.AP(base.tensor, base.offset, dims)

        def halves(arr, level):
            m = 1 << level
            return arr.rearrange("p (n h m) -> p n h m", h=2, m=m)

        off = [0]

        def r(n, *shape):
            v = rt[:, off[0]:off[0] + n]
            off[0] += n
            return v

        score = r(NS * NE).rearrange("p (s e) -> p s e", s=NS)
        sel = r(NS * NE).rearrange("p (s e) -> p s e", s=NS)
        top = r(NS * 64).rearrange("p (s g j) -> p s g j", s=NS, g=8)
        grp = r(16).rearrange("p (s g) -> p s g", s=NS)
        cmp = r(NS * 64).rearrange("p (s g j) -> p s g j", s=NS, g=8)
        ceq = r(NS * 64).rearrange("p (s g j) -> p s g j", s=NS, g=8)
        rank = r(16)
        gmask = r(16).rearrange("p (s g) -> p s g", s=NS)
        selm = r(NS * NE).rearrange("p (s e) -> p s e", s=NS)
        rep = r(NS * NE).rearrange("p (s e) -> p s e", s=NS)
        best = r(16).rearrange("p (s j) -> p s j", s=NS)
        mask = r(NS * NE).rearrange("p (s e) -> p s e", s=NS)
        comb = r(NS * NE).rearrange("p (s e) -> p s e", s=NS)
        wsum = r(2)
        wrec = r(2)
        posm = r(NS * NE).rearrange("p (s e) -> p s e", s=NS)
        nxt = r(4)
        endx = r(2)
        hot = r(NX)
        hot2 = r(NX)
        hotb = r(NX)
        neg = r(P)
        assert off[0] <= 2048
        ecol = consts[:, C_ECOL:C_ECOL + 1]
        iota_x = consts[0:NE, C_IOTA:C_IOTA + NX]

        def loop(eng, pair):
            if USE_IF:
                eng.wait_ge(items_done, 2)
                n = eng.value_load(nwork, min_val=0, max_val=NI)
            with eng.Fori(0, ITERS) as i:
                if USE_IF:
                    with eng.If(n > i * 4):
                        for b in range(2):
                            pair(b, i * 2 + b)
                else:
                    for b in range(2):
                        pair(b, i * 2 + b)

        def by_row(x):
            return x.rearrange("(k p) -> k p", p=P)

        loads_small = [(by_row(A["c_ctx"]), rows[R_C:R_C + 8, :]), (by_row(A["c"][0]), rows[R_C + 8:R_C + 16, :]),
                       (by_row(A["b_ada"][0]), rows[R_BADA:R_BADA + 48, :]), (by_row(A["norm1_g"][0]), rows[R_G1:R_G1 + 8, :]),
                       (by_row(A["norm2_g"][0]), rows[R_G2:R_G2 + 8, :]), (by_row(A["hgrn_norm_g"][0]), rows[R_HG:R_HG + 8, :]),
                       (A["hgrn_lb_logits"][0].rearrange("a (k p) -> (a k) p", p=P), rows[R_LB:R_LB + 16, :]),
                       (by_row(A["conv_dw_b"][0]), rows[R_DWB:R_DWB + 4, :]), (by_row(A["conv_norm_g"][0]), rows[R_CNG:R_CNG + 4, :]),
                       (by_row(A["conv_norm_b"][0]), rows[R_CNB:R_CNB + 4, :]),
                       (A["conv_dw_w"][0].rearrange("w (c p) -> (w c) p", p=P), rows_dw[0:CW * CC, :]),
                       (A["router_bias"].broadcast_to([P, NE]), b_router[:, :])]

        block = ctx.enter_context(nc.Block())

        @block.sync
        def _(sp):
            sp.dma_start(consts[:, :], A["consts"]).then_inc(s_cst, 16)
            for x, dst in loads_small[0::2]:
                sp.dma_start(dst, x).then_inc(s_rows, 16)
            for s, name in enumerate(("x_prompt", "x_sample")):
                sp.dma_start(x_tok[:, s, :], A[name][0]).then_inc(s_x, 16)
            for n, (name, src) in enumerate(blocks):
                if n >= 4:
                    released(sp, blocks[n - 4][0])
                sp.dma_start(tile_of(name), src).then_inc(s_w[n % 4], 16)
                if name == "ph1":
                    released(sp, "pc")
                    sp.dma_start(w_r[:, :, :], A["w_router"][0].rearrange("(k p) e -> p k e", p=P)).then_inc(s_wr, 16)
                if name == "v0":
                    sp.dma_start(s0[:, :, :], A["state_hgrn"][0, 0].rearrange("a h k v -> k (a h) v")).then_inc(s_s0, 16)
                if name == "ph1":
                    evacuated(sp, "st", 3)
                    sp.dma_start(new_state[0, 0].rearrange("a h k v -> k (a h) v"), s_new[:, :, :]).then_inc(s_state, 16)
                if name == "wo1":
                    sp.wait_ge(ob_used, 4)
                    sp.dma_start(w_sg[:, :, :], cols(A["w_shared_gate_up"][0], 0)).then_inc(s_sg, 16)
                    sp.dma_start(fin_g[:, :], A["final_norm_g"].rearrange("(a d) -> a d", a=1).broadcast_to([P, D])).then_inc(s_fing, 16)

            def load(slot, e):
                sp.dma_start(w_gu[slot][:, :, :], gu_src[e]).then_inc(s_gu[slot], 16)
                sp.dma_start(w_dn[slot][:, :, :], dn_src[e]).then_inc(s_dn[slot], 16)

            last = {i: max(n for n in range(len(blocks)) if n % 4 == i) for i in range(4)}
            for slot, over in ((1, (1, 2)), (0, (0, 1)), (2, (3,)), (3, ())):
                for i in over:
                    released(sp, blocks[last[i]][0])
                if slot == 2:
                    released(sp, "wo1")
                if slot == 3:
                    sp.wait_ge(proj_ready, fill_no["su", 0] + 1)
                load(slot, slot)
            with sp.Fori(1, MAIN) as i:
                for slot in range(4):
                    if slot % 2 == 0:
                        sp.wait_ge(dn_ready, i * 4 - 2 + 2 * (slot // 2))
                    load(slot, i * 4 + slot)
            sp.wait_ge(items_done, 2)
            with sp.Fori(MAIN, ITERS) as i:
                def extra():
                    for slot in range(4):
                        e = sp.value_load(e_row[0:1, bass.ds(i * 4 + (slot - NE), 1)], min_val=0, max_val=NE - 1)
                        if slot % 2 == 0:
                            sp.wait_ge(dn_ready, i * 4 - 2 + 2 * (slot // 2))
                        sp.dma_start(w_gu[slot][:, :, :], gu_src[bass.ds(e, 1)].rearrange("a p k f -> (a p) k f")).then_inc(s_gu[slot], 16)
                        sp.dma_start(w_dn[slot][:, :, :], dn_src[bass.ds(e, 1)].rearrange("a p c d -> (a p) c d")).then_inc(s_dn[slot], 16)
                if USE_IF:
                    n = sp.value_load(nwork, min_val=0, max_val=NI)
                    with sp.If(n > i * 4):
                        extra()
                else:
                    extra()
            for s, out in enumerate((y_prompt, y_sample)):
                sp.wait_ge(out_done, s + 1)
                sp.dma_start(out[0], fin[:, s, :]).then_inc(s_out, 16)
            sp.wait_ge(s_state, 16)
            sp.wait_ge(s_out, 32)

        @block.gpsimd
        def _(pool):
            own = Own(pool, own_pool)

            def rsqrt(out, in_, n):
                return nc.gpsimd.tensor_tensor(out, in_, mhalf[:, 0:n], ALU.pow)

            nc.gpsimd.memset(c_pad[:, :, :], 0.0).then_inc(s_pad, 1)
            nc.gpsimd.memset(mhalf, -0.5).then_inc(s_init, 1)
            nc.gpsimd.memset(ones[:, :], 1.0).then_inc(s_init, 1)
            nc.gpsimd.memset(upad[:, :, :, :], 0.0).then_inc(s_init, 1)
            pool.wait_ge(s_init, 3)
            pool.wait_ge(ssq_ready, 1)
            rsqrt(rms, ssq, 2).then_inc(rms_ready, 1)
            pool.wait_ge(vec_copied, 3)
            for half in range(2):
                for d in range(2):
                    for j in range(2):
                        evacuated(pool, f"{('zf', 'zb')[d]}{half}", j)
                        for hh in range(2):
                            hd = half * 4 + j * 2 + hh
                            c = slice(hd * T, (hd + 1) * T)
                            i = d * H + hd
                            nc.gpsimd.tensor_scalar(fg[:, d, c], fg[:, d, c], oml[:, i:i + 1], lb[:, i:i + 1],
                                                    ALU.mult, ALU.add).then_inc(fk_done, 1)
                            nc.gpsimd.tensor_scalar(qk[:, 2 + d, c], qk[:, 2 + d, c], oml[:, i:i + 1], None,
                                                    ALU.mult).then_inc(fk_done, 1)
            pool.wait_ge(fk_done, 32)
            for level in range(LEVELS):
                m = 1 << level
                if level == 3:
                    pool.wait_ge(cms_done, 1)
                    rsqrt(rms_c, ssq_c, 2).then_inc(crms_done, 1)
                pool.wait_ge(sc_ready, 4 * (level + 2))
                pool.wait_ge(mix_done, level + 1)
                if level:
                    pool.wait_ge(tot_done, level)
                kf, kb = halves(qk[:, 2, :], level), halves(qk[:, 3, :], level)
                tf, tb = halves(fg[:, 0, :], level), halves(fg[:, 1, :], level)
                nb = 16 * P // (2 * m)
                nc.gpsimd.tensor_tensor(kf[:, :, 0, :], kf[:, :, 0, :], tf[:, :, 1, 0:1].broadcast_to([P, nb, m]), ALU.mult).then_inc(k_done, 1)
                nc.gpsimd.tensor_tensor(kb[:, :, 1, :], kb[:, :, 1, :], tb[:, :, 0, 0:1].broadcast_to([P, nb, m]), ALU.mult).then_inc(k_done, 1)
            for g in range(4):
                pool.wait_ge(oms_done, g + 1)
                rsqrt(rms_o[:, 4 * g:4 * g + 4], ssq_o[:, 4 * g:4 * g + 4], 4).then_inc(orms_done, 1)
            pool.wait_ge(ssq2_done, 1)
            rsqrt(rms2, ssq2, 2).then_inc(rms2_done, 1)
            pool.wait_ge(f_ssq, 1)
            rsqrt(rmsf, ssqf, 2).then_inc(f_rms, 1)

        @block.scalar
        def _(act):
            own = Own(act, own_act)

            for x, dst in loads_small[1::2]:
                act.dma_start(dst, x).then_inc(s_rows, 16)

            act.wait_ge(s_x, 32)
            for s in range(NS):
                junk = tmp[:, :, :].rearrange("p a n -> p (a n)")
                if s:
                    own.wait()
                own.mark(nc.scalar.activation(junk, x_tok[:, s, :], ACT.Square, accum_out=ssq[:, s:s + 1]))
            act.wait_ge(vec_copied, 1)
            nc.scalar.activation(csig, vec[:, R_C:R_C + 16], ACT.Sigmoid).then_inc(c_sig, 1)

            def copy_partial(j):
                act.wait_ge(part_ready, j + 1)
                if j >= 2:
                    act.wait_ge(mod_ready, j - 1)
                nc.scalar.activation(tmp[:, j % 2, :], bank[4 + j % 2][:, :], ACT.Copy).then_inc(part_copied, 1)

            for j in range(4):
                filled(act, f"xt{j}")
                nc.scalar.activation(x_t[:, 2 * j:2 * j + 2, :].rearrange("p k t -> p (k t)"), fill_bank(f"xt{j}")[:, :],
                                     ACT.Copy).then_inc(act_evac, 1)

            own.wait()
            for j in range(4):
                copy_partial(j)
            act.wait_ge(s_init, 3)
            for j in range(2):
                filled(act, "u1", j)
                for c in range(2):
                    ins = nc.scalar.activation(upad[:, 2 * j + c, :, PAD:PAD + P],
                                               fill_bank("u1", j)[:, c * T:(c + 1) * T].rearrange("p (s t) -> p s t", s=NS), ACT.Copy)
                ins.then_inc(act_evac, 1)
            copy_partial(ada_after["u1"])
            act.wait_ge(mod_ready, ada_after["u1"] + 1)
            for j in range(2):
                filled(act, "u2", j)
                nc.scalar.activation(tmp[:, j, :], fill_bank("u2", j)[:, :], ACT.Sigmoid).then_inc(act_evac, 1)
            act.wait_ge(u_gated, 2)
            copy_partial(ada_after["u2"])

            def heads(arr, half, j):
                h0 = (half * 4 + j * 2) * T
                return arr[:, h0:h0 + 2 * T]

            for half in range(2):
                for j in range(2):
                    filled(act, f"q{half}", j)
                    nc.scalar.activation(heads(qk[:, 1, :], half, j), fill_bank(f"q{half}", j)[:, :], ACT.Copy).then_inc(act_evac, 1)
                copy_partial(ada_after[f"q{half}"])
                for d, z in enumerate(("zf", "zb")):
                    for j in range(2):
                        filled(act, f"{z}{half}", j)
                        src = fill_bank(f"{z}{half}", j)[:, :]
                        nc.scalar.activation(heads(fg[:, d, :], half, j), src, ACT.Sigmoid)
                        nc.scalar.activation(heads(qk[:, 2 + d, :], half, j), src, ACT.Sigmoid, scale=-1.0).then_inc(act_evac, 1)
                    copy_partial(ada_after[f"{z}{half}"])
            def mix_keys(level):
                if level:
                    act.wait_ge(k_done, 2 * level)
                    act.wait_ge(sc_ready, 4 * (level + 1))
                else:
                    act.wait_ge(fk_done, 32)
                dst = halves(k_mix[:, :], level)
                nc.scalar.activation(dst[:, :, 0, :], halves(qk[:, 2, :], level)[:, :, 0, :], ACT.Copy)
                nc.scalar.activation(dst[:, :, 1, :], halves(qk[:, 3, :], level)[:, :, 1, :], ACT.Copy).then_inc(mix_done, 1)

            for half in range(2):
                for s in range(NS):
                    filled(act, f"v{half}", s)
                    nc.scalar.activation(v_tok[:, s, half * 512:(half + 1) * 512], fill_bank(f"v{half}", s)[:, :], ACT.Copy).then_inc(act_evac, 1)
                    if half == 1 and s == 0:
                        mix_keys(0)
            upad_row = upad[:, :, :, :].rearrange("p c s u -> p (c s u)")
            act.wait_ge(cen_done, CC)
            nc.scalar.activation(upad_row[:, 0:CC * T], conv[:, :, :].rearrange("p c t -> p (c t)"), ACT.Square).then_inc(csq_done, 1)
            for half in range(2):
                for j in range(2):
                    n = half * 2 + j
                    filled(act, f"og{half}", j)
                    if n < 2:
                        act.wait_ge(mod_ready, 12)
                    else:
                        evacuated(act, f"og{(n - 2) // 2}", n % 2)
                    nc.scalar.activation(tmp[:, n % 2, :], fill_bank(f"og{half}", j)[:, :], ACT.Sigmoid).then_inc(og_sig, 1)
                    if j == 0:
                        mix_keys(1 + half)
            for name, dst in (("ga", ga), ("gb", gb)):
                for half in range(2):
                    for j in range(2):
                        filled(act, f"{name}{half}", j)
                        h0 = half * 4 + j * 2
                        nc.scalar.activation(dst[:, h0:h0 + 2, :].rearrange("p h t -> p (h t)"), fill_bank(f"{name}{half}", j)[:, :],
                                             ACT.Sigmoid).then_inc(act_evac, 1)
                        if j == 0:
                            mix_keys(3 + 2 * (name == "gb") + half)
                    if name == "gb" and half == 0:
                        act.wait_ge(cn_done, CC)
                        for c in range(CC):
                            nc.scalar.activation(upad_row[:, c * T:(c + 1) * T], conv[:, c, :], ACT.Sigmoid).then_inc(cs_done, 1)
            act.wait_ge(cb_ready, 1)
            def o_and_squares(g):
                act.wait_ge(o_ready, g + 1)
                src = bank[4 + g % 2][:, :]
                nc.scalar.activation(o_t[:, 2 * g:2 * g + 2, :].rearrange("p h t -> p (h t)"), src, ACT.Copy)
                if g >= 2:
                    act.wait_ge(ob_ready, g - 1)
                nc.scalar.activation(tmp[:, g % 2, :], src, ACT.Square).then_inc(o_copied, 1)

            def four_heads(name, dst, j):
                filled(act, name, j)
                nc.scalar.activation(dst[:, 4 * j:4 * j + 4, :].rearrange("p a b -> p (a b)"), fill_bank(name, j)[:, :], ACT.Copy).then_inc(act_evac, 1)

            act.wait_ge(tot_done, LEVELS)
            act.wait_ge(k_done, 2 * LEVELS)
            act.wait_ge(q_done, 2 * (LEVELS + 1))
            o_and_squares(0)
            o_and_squares(1)
            four_heads("kt", k_tok, 0)
            four_heads("kt", k_tok, 1)
            o_and_squares(2)
            four_heads("kt", k_tok, 2)
            o_and_squares(3)
            four_heads("kt", k_tok, 3)
            for j in range(4):
                four_heads("st", s_new, j)
            for s in range(NS):
                for hf in range(2):
                    filled(act, "t1", 2 * s + hf)
                    nc.scalar.activation(x1[:, s, hf * 512:(hf + 1) * 512], fill_bank("t1", 2 * s + hf)[:, :], ACT.Copy).then_inc(act_evac, 1)
            evacuated(act, "t1", 3)
            for s in range(NS):
                junk = tmp[:, :, :].rearrange("p a n -> p (a n)")
                if s == 0:
                    act.wait_ge(osq_ready, 4)
                    act.wait_ge(ob_ready, 4)
                else:
                    own.wait()
                own.mark(nc.scalar.activation(junk, x1[:, s, :], ACT.Square, accum_out=ssq2[:, s:s + 1]))
            act.wait_ge(lg_ready, 1)
            act.wait_ge(s_state, 16)
            nc.scalar.activation(rt[:, 0:NS * NE], bank[4][:, 0:NS * NE], ACT.Sigmoid).then_inc(lg_sig, 1)
            for j in range(4):
                filled(act, "hr", j)
                s, hf = j // 2, j % 2
                nc.scalar.activation(h_hi[:, s, :, 64 * hf:64 * hf + 64].rearrange("t k p -> t p k"),
                                     fill_bank("hr", j)[:, :].rearrange("t (p k) -> t p k", k=KD), ACT.Copy).then_inc(hr_hi, 1)
            filled(act, "sg", 0)
            nc.scalar.activation(sil_s[:, :, :].rearrange("p c t -> p (c t)"), fill_bank("sg")[:, :], ACT.Silu).then_inc(act_evac, 1)
            filled(act, "su")
            act.dma_start(w_sd[:, :, :], A["w_shared_down"][0].rearrange("(k p) c -> p k c", p=P)).then_inc(s_sd, 16)
            act.wait_ge(ga_ready, 1)
            nc.scalar.activation(xg[0][:, 0:4, :].rearrange("p k n -> p (k n)"), bank[0][:, :], ACT.Copy).then_inc(ga_evac, 1)

            def pair(b, p):
                act.wait_ge(gu_ready, p + 1)
                nc.scalar.activation(sil[:, :], bank[2 + b][:, 0:FF], ACT.Silu).then_inc(sil_ready, 1)
                act.wait_ge(ga_ready, p + 2)
                nc.scalar.activation(xg[1 - b][:, 0:4, :].rearrange("p k n -> p (k n)"), bank[0][:, :], ACT.Copy).then_inc(ga_evac, 1)
                act.wait_ge(t_ready, p + 1)
                nc.scalar.activation(act_t[:, :, :].rearrange("p c n -> p (c n)"), bank[2 + b][:, 0:2 * P], ACT.Copy).then_inc(t_evac, 1)
                for h in range(2):
                    act.wait_ge(dn_ready, p * 2 + (h + 1))
                    nc.scalar.activation(y_hi[h][:, :], bank[(3 - b, 2 + b)[h]][:, :], ACT.Copy).then_inc(hi_ready, 1)

            loop(act, pair)
            for s in range(NS):
                act.wait_ge(x2_done, s + 1)
                if s:
                    own.wait()
                own.mark(nc.scalar.activation(tmp[:, :, :].rearrange("p a n -> p (a n)"), fin[:, s, :], ACT.Square, accum_out=ssqf[:, s:s + 1]))

        @block.vector
        def _(dve):
            own = Own(dve, own_dve)
            V = nc.vector

            dve.wait_ge(vec_ready, 1)
            V.tensor_copy(vec[:, 0:R_ALL], bank[7][:, 0:R_ALL]).then_inc(vec_copied, 1)
            V.tensor_copy(dw[:, :, :].rearrange("p w c -> p (w c)"), bank[7][:, P:P + CW * CC]).then_inc(vec_copied, 1)
            dve.wait_ge(vec_copied, 2)
            own.step(V.tensor_tensor(oml, vec[:, R_LB:R_LB + 16], vec[:, R_LB:R_LB + 16], ALU.subtract))
            own.step(V.tensor_scalar(oml, oml, 1.0, None, ALU.add))
            own.step(V.tensor_tensor(lb, oml, oml, ALU.subtract))
            V.tensor_scalar(oml, lb, -1.0, 1.0, ALU.mult, ALU.add).then_inc(vec_copied, 1)
            dve.wait_ge(c_sig, 1)
            dve.wait_ge(s_pad, 1)
            V.tensor_tensor(c_pad[:, :, 0:NS].rearrange("p k s -> p s k"), csig.rearrange("p (s k) -> p s k", s=NS),
                            vec[:, R_C:R_C + 16].rearrange("p (s k) -> p s k", s=NS), ALU.mult).then_inc(c_silu, 1)
            dve.wait_ge(own_act, 2)
            V.tensor_scalar(ssq, ssq, 1.0 / D, EPS, ALU.mult, ALU.add).then_inc(ssq_ready, 1)
            dve.wait_ge(rms_ready, 1)
            for s in range(NS):
                V.tensor_scalar(xn[:, s, :], x_tok[:, s, :], rms[:, s:s + 1], None, ALU.mult).then_inc(xn_done, 1)

            def modulation(j0, j1, ready):
                dve.wait_ge(mod_ready, ready)
                for s in range(NS):
                    last = V.tensor_tensor(mod_v[:, j0:j1, s], bank[7][:, 256 + 2 * j0:256 + 2 * j1].rearrange("p (j s) -> p j s", s=NS)[:, :, s],
                                           vec[:, R_BADA + j0:R_BADA + j1], ALU.add)
                    last.then_inc(mod_done, 1)
                dve.wait_ge(mod_done, 2 if j0 == 0 else 4)

            def gains(dst, scale, gain):
                g = dst.rearrange("p (k s) -> p k s", s=NS)
                for s in range(NS):
                    own.step(V.scalar_tensor_tensor(g[:, :, s], mod_v[:, scale:scale + 8, s], 1.0, vec[:, gain:gain + 8], ALU.add, ALU.mult))

            modulation(0, 16, 4)
            gains(gain1, M_SC1, R_G1)
            for j in range(4):
                filled(dve, f"h{j}")
                for kk in range(2):
                    for s in range(NS):
                        k = 2 * j + kk
                        src = fill_bank(f"h{j}")[:, kk * T + s * P:kk * T + (s + 1) * P]
                        ins = V.tensor_scalar(h_t[:, k, s * P:(s + 1) * P], src, gain1[:, 2 * k + s:2 * k + s + 1],
                                              mod_v[:, M_SH1 + k, s:s + 1], ALU.mult, ALU.add)
                ins.then_inc(dve_evac, 1)

            for j in range(2):
                evacuated(dve, "u2", j)
                sg = tmp[:, j, :].rearrange("p (c s t) -> p c s t", c=2, s=NS)
                for c in range(2):
                    uu = upad[:, 2 * j + c, :, PAD:PAD + P]
                    ins = V.tensor_tensor(uu, uu, sg[:, c], ALU.mult)
                ins.then_inc(u_gated, 1)
            dve.wait_ge(u_gated, 2)
            marks = []
            for w in range(CW):
                for c in range(CC):
                    dst = conv[:, c, :].rearrange("p (s t) -> p s t", s=NS)
                    src = upad[:, c, :, w:w + P]
                    tap = dw[:, w, c:c + 1]
                    if w == 0:
                        ins = V.tensor_scalar(dst, src, tap, vec[:, R_DWB + c:R_DWB + c + 1], ALU.mult, ALU.add)
                    else:
                        own.wait(marks[CC * (w - 1) + c])
                        ins = V.scalar_tensor_tensor(dst, src, tap, dst, ALU.mult, ALU.add)
                    if w < CW - 1:
                        marks.append(own.mark(ins))
                    else:
                        ins.then_inc(conv_done, 1)

            mask_of = [consts[:, C_MASK + P * lv:C_MASK + P * (lv + 1)].unsqueeze(1).broadcast_to([P, 4, P]) for lv in range(LEVELS)]
            dve.wait_ge(s_cst, 16)

            def score_tiles(level):
                for g in range(4):
                    n = 4 * (level + 1) + g
                    dve.wait_ge(sc_ready, n + 1)
                    src = bank[4 + n % 2][:, :].rearrange("p (a t) -> p a t", a=4)
                    dst = att[:, 4 * g:4 * g + 4, :]
                    if level < 0:
                        V.tensor_tensor(dst, src, ident.unsqueeze(1).broadcast_to([P, 4, P]), ALU.mult).then_inc(sc_used, 1)
                    else:
                        V.copy_predicated(dst, mask_of[level].bitcast(U32), src).then_inc(sc_used, 1)

            score_tiles(-1)
            dve.wait_ge(fk_done, 32)
            for d in (1, 0):
                V.tensor_tensor(qk[:, 1 - d, :], qk[:, 1, :], fg[:, d, :], ALU.mult).then_inc(q_done, 1)
            dve.wait_ge(q_done, 2)

            dve.wait_ge(mean_ready, 1)
            for c in range(CC):
                V.scalar_tensor_tensor(conv[:, c, :], bank[6][:, 0:T], -1.0 / (CC * P), conv[:, c, :], ALU.mult, ALU.add).then_inc(cen_done, 1)

            def og_gate(half):
                for j in range(2):
                    n = half * 2 + j
                    dve.wait_ge(og_sig, n + 1)
                    for hh in range(2):
                        hd = half * 4 + j * 2 + hh
                        ins = V.scalar_tensor_tensor(og[:, hd, :], fill_bank(f"og{half}", j)[:, hh * T:(hh + 1) * T], vec[:, R_HG + hd:R_HG + hd + 1],
                                                     tmp[:, n % 2, hh * T:(hh + 1) * T], ALU.mult, ALU.mult)
                    ins.then_inc(dve_evac, 1)

            modulation(16, 48, 12)
            gains(gain2, M_SC2, R_G2)
            for level in range(LEVELS):
                m = 1 << level
                score_tiles(level)
                nb = 16 * P // (2 * m)
                qb, qf = halves(qk[:, 0, :], level), halves(qk[:, 1, :], level)
                tf, tb = halves(fg[:, 0, :], level), halves(fg[:, 1, :], level)
                if level:
                    dve.wait_ge(tot_done, level)
                V.tensor_tensor(qf[:, :, 1, :], qf[:, :, 1, :], tf[:, :, 0, 0:1].broadcast_to([P, nb, m]), ALU.mult).then_inc(q_done, 1)
                V.tensor_tensor(qb[:, :, 0, :], qb[:, :, 0, :], tb[:, :, 1, 0:1].broadcast_to([P, nb, m]), ALU.mult).then_inc(q_done, 1)
                dve.wait_ge(q_done, 2 * (level + 2))
                dve.wait_ge(k_done, 2 * (level + 1))
                tot = fg[:, :, :].rearrange("p d (n h m) -> p d n h m", h=2, m=m)[:, :, :, :, 0]
                V.tensor_tensor(tot[:, :, :, 0], tot[:, :, :, 0], tot[:, :, :, 1], ALU.mult).then_inc(tot_done, 1)
                if level in (1, 2):
                    og_gate(level - 1)
                if level == 2:
                    dve.wait_ge(cvar_ready, 1)
                    V.tensor_scalar(ssq_c, bank[6][:, 256:258], 1.0 / (CC * P), EPS, ALU.mult, ALU.add).then_inc(cms_done, 1)
                if level == 3:
                    dve.wait_ge(crms_done, 1)
                    diag = tmp[:, 0, 0:T]
                    for s in range(NS):
                        V.tensor_scalar(diag[:, s * P:(s + 1) * P], ident, rms_c[:, s:s + 1], None, ALU.mult).then_inc(cdiag_done, 1)
                if level == 4:
                    dve.wait_ge(cb_ready, 1)
                    for c in range(CC):
                        own.mark(V.tensor_tensor(conv[:, c, :], conv[:, c, :], bank[6][:, 0:T], ALU.mult))
                    own.wait()
                    for c in range(CC):
                        V.tensor_scalar(conv[:, c, :], conv[:, c, :], vec[:, R_CNG + c:R_CNG + c + 1], vec[:, R_CNB + c:R_CNB + c + 1],
                                        ALU.mult, ALU.add).then_inc(cn_done, 1)
                if level == 5:
                    dve.wait_ge(cn_done, CC)
                    dve.wait_ge(cs_done, CC)
                    for c in range(CC):
                        V.tensor_tensor(conv[:, c, :], conv[:, c, :], upad[:, :, :, :].rearrange("p c s u -> p (c s u)")[:, c * T:(c + 1) * T],
                                        ALU.mult).then_inc(cact_done, 1)

            def branch(key, arr, j):
                filled(dve, *key)
                dd = arr[:, 2 * j:2 * j + 2, :].rearrange("p h t -> p (h t)")
                V.tensor_tensor(dd, dd, fill_bank(*key)[:, :], ALU.mult).then_inc(dve_evac, 1)

            evacuated(dve, "gb1", 1)
            for j in range(4):
                branch(("pc", j), gb, j)

            def normed(g):
                dve.wait_ge(ob_ready, g + 1)
                oo = o_t[:, 2 * g:2 * g + 2, :].rearrange("p h t -> p (h t)")
                own.step(V.tensor_tensor(oo, oo, bank[6][:, :], ALU.mult))
                V.tensor_tensor(oo, oo, og[:, 2 * g:2 * g + 2, :].rearrange("p h t -> p (h t)"), ALU.mult).then_inc(ob_used, 1)

            for g in range(4):
                dve.wait_ge(osq_ready, g + 1)
                V.tensor_scalar(ssq_o[:, 4 * g:4 * g + 4], bank[7][:, 384 + 4 * g:388 + 4 * g], 1.0 / P, EPS, ALU.mult, ALU.add).then_inc(oms_done, 1)
                if g:
                    normed(g - 1)
                dve.wait_ge(orms_done, g + 1)
                for i in range(4):
                    ins = V.tensor_scalar(tmp[:, g % 2, i * P:(i + 1) * P], ident, rms_o[:, 4 * g + i:4 * g + i + 1], None, ALU.mult)
                ins.then_inc(odiag_done, 1)
            normed(3)

            for j in range(4):
                key = (f"ph{j // 2}", j % 2)
                branch(key, ga, j)
                evacuated(dve, *key)
                dd = ga[:, 2 * j:2 * j + 2, :].rearrange("p h t -> p (h t)")
                V.tensor_tensor(dd, dd, gb[:, 2 * j:2 * j + 2, :].rearrange("p h t -> p (h t)"), ALU.add).then_inc(merged, 1)
            for j in range(4):
                key = (f"wo{j // 2}", j % 2)
                filled(dve, *key)
                for kk in range(2):
                    for s in range(NS):
                        k = 2 * j + kk
                        dst = x_t[:, k, s * P:(s + 1) * P]
                        ins = V.scalar_tensor_tensor(dst, fill_bank(*key)[:, kk * T + s * P:kk * T + (s + 1) * P], mod_v[:, M_GT1 + k, s:s + 1], dst, ALU.mult, ALU.add)
                ins.then_inc(dve_evac, 1)
            dve.wait_ge(own_act, 4)
            V.tensor_scalar(ssq2, ssq2, 1.0 / D, EPS, ALU.mult, ALU.add).then_inc(ssq2_done, 1)
            dve.wait_ge(rms2_done, 1)
            for s in range(NS):
                V.tensor_scalar(xn2[:, s, :], x1[:, s, :], rms2[:, s:s + 1], None, ALU.mult).then_inc(xn2_done, 1)
            for j in range(4):
                filled(dve, "n2", j)
                for kk in range(2):
                    for s in range(NS):
                        k = 2 * j + kk
                        src = fill_bank("n2", j)[:, kk * T + s * P:kk * T + (s + 1) * P]
                        ins = V.tensor_scalar(h_t[:, k, s * P:(s + 1) * P], src, gain2[:, 2 * k + s:2 * k + s + 1],
                                              mod_v[:, M_SH2 + k, s:s + 1], ALU.mult, ALU.add)
                ins.then_inc(dve_evac, 1)

            for j in range(4):
                filled(dve, "hr", j)
                dve.wait_ge(hr_hi, j + 1)
                s, hf = j // 2, j % 2
                V.tensor_tensor(h_lo[:, s, :, 64 * hf:64 * hf + 64].rearrange("t k p -> t p k"),
                                fill_bank("hr", j)[:, :].rearrange("t (p k) -> t p k", k=KD),
                                h_hi[:, s, :, 64 * hf:64 * hf + 64].rearrange("t k p -> t p k").bitcast(F32), ALU.subtract).then_inc(dve_evac, 1)
            dve.wait_ge(lg_sig, 1)
            dve.wait_ge(s_rows, 16 * 12)
            for s in range(NS):
                own.mark(V.tensor_tensor(sel[:, s, :], score[:, s, :], b_router[:, :], ALU.add))
            own.mark(V.memset(selm, -BIG))
            own.mark(V.memset(neg, -1.0))
            own.wait()
            for s in range(NS):
                for g in range(8):
                    own.mark(V.max(top[:, s, g, :], sel[:, s, 8 * g:8 * g + 8]))
            own.wait()
            own.step(V.tensor_tensor(grp, top[:, :, :, 0], top[:, :, :, 1], ALU.add))
            for s in range(NS):
                other = grp[:, s, :].unsqueeze(1).broadcast_to([P, 8, 8])
                mine = grp[:, s, :].unsqueeze(2).broadcast_to([P, 8, 8])
                own.mark(V.tensor_tensor(cmp[:, s], other, mine, ALU.is_gt))
                own.step(V.tensor_tensor(ceq[:, s], other, mine, ALU.is_equal))
                own.step(V.tensor_tensor(ceq[:, s], ceq[:, s], consts[:, C_LT:C_LT + 64].rearrange("p (g j) -> p g j", g=8), ALU.mult))
                own.step(V.tensor_tensor(cmp[:, s], cmp[:, s], ceq[:, s], ALU.add))
            own.step(V.tensor_reduce(rank, cmp.rearrange("p s g j -> p (s g) j"), AX, ALU.add))
            own.step(V.tensor_scalar(gmask.rearrange("p s g -> p (s g)"), rank, 4.0, None, ALU.is_lt))
            for s in range(NS):
                own.step(V.copy_predicated(selm[:, s, :].rearrange("p (g j) -> p g j", g=8), gmask[:, s, :].unsqueeze(2).broadcast_to([P, 8, 8]).bitcast(U32),
                                           sel[:, s, :].rearrange("p (g j) -> p g j", g=8)))
                own.step(V.max(best[:, s, :], selm[:, s, :]))
                own.step(V.match_replace(rep[:, s, :], best[:, s, :], selm[:, s, :], BIG))
            V.tensor_tensor(mask, rep, selm, ALU.not_equal).then_inc(lg_mask, 1)
            dve.wait_ge(lg_mask, 1)
            own.step(V.tensor_tensor(comb, score, mask, ALU.mult))
            own.step(V.tensor_reduce(wsum, comb, AX, ALU.add))
            own.step(V.reciprocal(wrec, wsum))
            for s in range(NS):
                own.mark(V.tensor_scalar(comb[:, s, :], comb[:, s, :], wrec[:, s:s + 1], ROUTED_SCALE, ALU.mult, ALU.mult))
            dve.wait_ge(cnt_ready, 1)
            for s in range(NS):
                own.mark(V.scalar_tensor_tensor(posm[:, s, :], bank[5][:, s * NE:(s + 1) * NE], 1.0, mask[:, s, :], ALU.add, ALU.mult))
            for j in range(3):
                V.tensor_scalar(nxt[0:NE, j:j + 1], bank[5][0:NE, 128:129], C * (j + 1.0), None, ALU.is_gt).then_inc(posm_done, 1)
            dve.wait_ge(posm_done, 3)
            own.step(V.tensor_tensor(nxt[0:NE, 0:1], nxt[0:NE, 0:1], nxt[0:NE, 1:2], ALU.add))
            V.tensor_tensor(nxt[0:NE, 3:4], nxt[0:NE, 0:1], nxt[0:NE, 2:3], ALU.add).then_inc(nx_done, 1)
            dve.wait_ge(nx_done, 1)
            dve.wait_ge(end_ready, 1)
            own.step(V.tensor_copy(endx[0:NE, 0:1], bank[5][0:NE, 130:131]))
            own.step(V.tensor_tensor(endx[0:NE, 1:2], endx[0:NE, 0:1], nxt[0:NE, 3:4], ALU.subtract))
            own.mark(V.tensor_scalar(hot[0:NE, :], iota_x, endx[0:NE, 0:1], None, ALU.is_ge))
            own.mark(V.tensor_scalar(hot2[0:NE, :], iota_x, endx[0:NE, 1:2], None, ALU.is_ge))
            own.step(V.tensor_scalar(hotb[0:NE, :], iota_x, endx[0:NE, 1:2], 1.0, ALU.subtract, ALU.add))
            own.step(V.tensor_tensor(hot[0:NE, :], hot2[0:NE, :], hot[0:NE, :], ALU.subtract))
            V.scalar_tensor_tensor(hotb[0:NE, :], hotb[0:NE, :], float(C), hot[0:NE, :], ALU.mult, ALU.mult).then_inc(oh_done, 1)
            dve.wait_ge(pt1_ready, 1)
            pos_t = tmp[0:NE, 0, 0:T]
            comb_t = tmp[0:NE, 0, T:2 * T]
            V.tensor_copy(tmp[0:NE, 0, :], bank[6][0:NE, :]).then_inc(pt1_copied, 1)
            dve.wait_ge(items_ready, 1)
            own.mark(V.memset(pos_i[:, :, NI:NI + 4], -1.0))
            own.mark(V.memset(comb_i[:, :, NI:NI + 4], 0.0))
            own.mark(V.memset(e_row[:, :], 0))
            own.wait()
            own.mark(V.tensor_copy(e_row[0:1, 0:NX], bank[5][0:1, 256:256 + NX]))
            own.mark(V.tensor_scalar(nwork, bank[5][0:1, 296:297], float(NE), None, ALU.add))
            for s in range(NS):
                own.mark(V.tensor_scalar(pos_i[:, s, 0:NE], posm[:, s, :], 1.0, None, ALU.subtract))
                own.mark(V.tensor_copy(comb_i[:, s, 0:NE], comb[:, s, :]))
                own.mark(V.tensor_scalar(pos_i[:, s, NE:NI], bank[5][:, 320 + s * NX:320 + (s + 1) * NX], 1.0, None, ALU.subtract))
                V.tensor_copy(comb_i[:, s, NE:NI], bank[5][:, 384 + s * NX:384 + (s + 1) * NX]).then_inc(items_done, 1)

            for j in range(4):
                s, hf = j // 2, j % 2
                dve.wait_ge(gr_ready, j + 1)
                V.tensor_copy(g2row[:, s, hf * 512:(hf + 1) * 512], bank[4 + j][:, :]).then_inc(gr_done, 1)
            filled(dve, "su")
            evacuated(dve, "sg")
            V.tensor_tensor(act_s[:, :, :].rearrange("p c t -> p (c t)"), sil_s[:, :, :].rearrange("p c t -> p (c t)"), fill_bank("su")[:, :], ALU.mult).then_inc(dve_evac, 1)

            iota2 = consts[:, C_IOTA:C_IOTA + C].unsqueeze(1).broadcast_to([P, 2, C])

            def one_hots(b, p2):
                for s in range(NS):
                    V.tensor_tensor(sel_p[b][:, s, :].rearrange("t (e j) -> t e j", e=2), iota2,
                                    pos_i[:, s, bass.ds(p2, 2)].unsqueeze(2).broadcast_to([P, 2, C]), ALU.is_equal)
                ins = V.tensor_copy(comb_p[b][:, :, :], comb_i[:, :, bass.ds(p2, 2)])
                ins.then_inc(built, 1)

            def transposed(b, p1):
                dve.wait_ge(pt_ready, p1)
                V.tensor_copy(sel_t[b][:, :], bank[0][:, 0:T])
                V.tensor_copy(w_slot[b][0:C, :], bank[0][0:C, T:T + 1])
                V.tensor_copy(w_slot[b][C:P, :], bank[0][C:P, T + 1:T + 2]).then_inc(pt_evac, 1)

            def right_half(b, p1):
                dve.wait_ge(gbk_ready, p1)
                V.tensor_copy(xg[b][:, 4:8, :].rearrange("p k n -> p (k n)"), bank[1][:, :]).then_inc(gbk_evac, 1)

            own.mark(V.memset(sel_t[1][:, :].bitcast(F32), 0.0))
            V.memset(y_hi[1][:, :].bitcast(F32), 0.0).then_inc(y_ready, 1)
            own.wait()
            V.memset(y_lo[1][:, :].bitcast(F32), 0.0).then_inc(y_ready, 1)
            one_hots(0, 0)
            right_half(0, 1)
            transposed(0, 1)

            def pair(b, p):
                one_hots(1 - b, p * 2 + 2)
                dve.wait_ge(sil_ready, p + 1)
                dve.wait_ge(pt_evac, p + 1)
                V.scalar_tensor_tensor(act_r[:, :], bank[2 + b][:, FF:2 * FF], w_slot[b][:, 0:1], sil[:, :], ALU.mult, ALU.mult).then_inc(act_ready, 1)
                right_half(1 - b, p + 2)
                transposed(1 - b, p + 2)
                for h in range(2):
                    dve.wait_ge(hi_ready, p * 2 + (h + 1))
                    V.tensor_tensor(y_lo[h][:, :], bank[(3 - b, 2 + b)[h]][:, :], y_hi[h][:, :].bitcast(F32), ALU.subtract).then_inc(y_ready, 1)

            loop(dve, pair)
            V.memset(small[:, 179:180], 0.0).then_inc(loop_done, 1)

            dve.wait_ge(y_done, 1)
            for s in range(NS):
                for hf in range(2):
                    c = slice(hf * 512, (hf + 1) * 512)
                    own.step(V.tensor_tensor(fin[:, s, c], g2row[:, s, c], y_acc[s][hf][:, :], ALU.mult))
                    ins = V.tensor_tensor(fin[:, s, c], fin[:, s, c], x1[:, s, c], ALU.add)
                    if hf:
                        ins.then_inc(x2_done, 1)
                    else:
                        own.mark(ins)
            dve.wait_ge(own_act, 6)
            V.tensor_scalar(ssqf, ssqf, 1.0 / D, EPS, ALU.mult, ALU.add).then_inc(f_ssq, 1)
            dve.wait_ge(f_rms, 1)
            dve.wait_ge(s_fing, 16)
            for s in range(NS):
                V.scalar_tensor_tensor(fin[:, s, :], fin[:, s, :], rmsf[:, s:s + 1], fin_g[:, :], ALU.mult, ALU.mult).then_inc(out_done, 1)

        @block.tensor
        def _(pe):
            mm = nc.tensor.matmul

            def arrived(name):
                n = number[name]
                pe.wait_ge(s_w[n % 4], 16 * (n // 4 + 1))

            def open_fill(name, j=0):
                n = fill_no[name, j]
                if n >= 4:
                    pe.wait_ge(fills[n - 4][2], fills[n - 4][3])
                return bank[n % 4]

            pe.wait_ge(s_cst, 16)
            pe.wait_ge(s_rows, 16 * 12)
            nc.tensor.transpose(bank[7][:, 0:R_ALL], rows[0:R_ALL, :], ident[0:R_ALL, 0:R_ALL])
            nc.tensor.transpose(bank[7][:, P:P + CW * CC], rows_dw[0:CW * CC, :], ident[0:CW * CC, 0:CW * CC]).then_inc(vec_ready, 1)
            pe.wait_ge(s_x, 32)

            def to_channels(name, src, j):
                b = open_fill(*name)
                for kk in range(2):
                    for s in range(NS):
                        k = 2 * j + kk
                        ins = nc.tensor.transpose(b[:, kk * T + s * P:kk * T + (s + 1) * P], src[:, s, k * P:(k + 1) * P], ident)
                return ins

            for j in range(4):
                to_channels((f"xt{j}", 0), x_tok, j).then_inc(proj_ready, 1)

            def ada_partial(j):
                arrived(f"ada{j}")
                if j >= 2:
                    pe.wait_ge(part_copied, j - 1)
                w = tile_of(f"ada{j}")
                for k in range(KD):
                    g = k % 4
                    ins = mm(bank[4 + j % 2][32 * g:32 * g + 32, :], c_pad[:, k, :], w[:, k, :], start=(k < 4), stop=(k >= 4))
                ins.then_inc(part_ready, 1)

            def ada_sum(j):
                pe.wait_ge(part_copied, j + 1)
                for c in range(4):
                    col = 256 + 2 * (4 * j + c)
                    ins = mm(bank[7][:, col:col + 2], tmp[:, j % 2, c * P:(c + 1) * P], consts[:, C_SUM:C_SUM + NS], start=True, stop=True)
                ins.then_inc(mod_ready, 1)

            def ada(j0, j1):
                for j in range(j0, j1 + 1):
                    if j < j1:
                        ada_partial(j)
                    if j > j0:
                        ada_sum(j - 1)

            pe.wait_ge(vec_copied, 2)
            pe.wait_ge(c_silu, 1)
            ada(0, 4)
            pe.wait_ge(xn_done, 2)
            for j in range(4):
                to_channels((f"h{j}", 0), xn, j).then_inc(proj_ready, 1)

            def project(name, rhs, kk=KD, n=2, before_k=None):
                arrived(name)
                w = tile_of(name)
                for j in range(n):
                    b = open_fill(name, j)
                    for c in range(2):
                        col = (2 * j + c) * P
                        for k in range(kk):
                            if before_k is not None and j == 0 and c == 0:
                                before_k(k)
                            ins = mm(b[:, c * T:(c + 1) * T], w[:, k, col:col + P], rhs[:, k, :], start=(k == 0), stop=(k == kk - 1))
                            if k == kk - 1 and c == 1:
                                ins.then_inc(proj_ready, 1)

            def quarter(name, q):
                w = tile_of(name)
                if q == 0:
                    arrived(name)
                b = open_fill(name, q // 2) if q % 2 == 0 else fill_bank(name, q // 2)
                if name[0] == "v":
                    s = q // 2
                    for k in range(4 * (q % 2), 4 * (q % 2) + 4):
                        ins = mm(b[:, :], h_t[:, k, s * P:(s + 1) * P], w[:, k, :], start=(k == 0), stop=(k == KD - 1))
                else:
                    for k in range(KD):
                        ins = mm(b[:, (q % 2) * T:(q % 2 + 1) * T], w[:, k, q * P:(q + 1) * P], h_t[:, k, :], start=(k == 0), stop=(k == KD - 1))
                if q % 2:
                    ins.then_inc(proj_ready, 1)

            def scores(level, groups):
                for g in groups:
                    n = 4 * (level + 1) + g
                    if n >= 2:
                        pe.wait_ge(sc_used, n - 1)
                    for i in range(4):
                        out, at_ = bank[4 + n % 2][:, i * P:(i + 1) * P], 4 * g + i
                        if level < 0:
                            q = qk[:, 1, at_ * P:(at_ + 1) * P]
                            mm(out, qk[:, 2, at_ * P:(at_ + 1) * P], q, start=True, stop=False)
                            ins = mm(out, qk[:, 3, at_ * P:(at_ + 1) * P], q, start=False, stop=True)
                        else:
                            ins = mm(out, k_mix[:, at_ * P:(at_ + 1) * P], query_mix(level, at_), start=True, stop=True)
                    ins.then_inc(sc_ready, 1)

            evacuated(pe, "h3")
            pe.wait_ge(mod_done, 2)
            for name in ("u1", "u2", "q0", "zf0", "zb0", "q1", "zf1", "zb1"):
                project(name, h_t)
                if name in ada_after:
                    if name != "u1":
                        ada_sum(ada_after[name] - 1)
                    ada_partial(ada_after[name])
            for level, name in zip(range(-1, LEVELS), ("v0", "v1", "og0", "og1", "ga0", "ga1", "gb0", "gb1")):
                quarter(name, 0)
                if level == -1:
                    ada_sum(11)
                quarter(name, 1)
                quarter(name, 2)
                if level == -1:
                    pe.wait_ge(fk_done, 32)
                    evacuated(pe, "q1", 1)
                else:
                    pe.wait_ge(q_done, 2 * (level + 1))
                    pe.wait_ge(mix_done, level + 1)
                scores(level, (0, 1))
                quarter(name, 3)
                scores(level, (2, 3))
                if level == -1:
                    pe.wait_ge(conv_done, CC)
                    pe.wait_ge(s_init, 3)
                    for c in range(CC):
                        ins = mm(bank[6][:, 0:T], ones[:, :], conv[:, c, :], start=(c == 0), stop=(c == CC - 1))
                    ins.then_inc(mean_ready, 1)
                if level == 1:
                    pe.wait_ge(csq_done, 1)
                    sq = upad[:, :, :, :].rearrange("p c s u -> p (c s u)")
                    for s in range(NS):
                        for c in range(CC):
                            ins = mm(bank[6][:, 256 + s:257 + s], sq[:, c * T + s * P:c * T + (s + 1) * P], ones[:, 0:1], start=(c == 0), stop=(c == CC - 1))
                    ins.then_inc(cvar_ready, 1)
                if level == 4:
                    pe.wait_ge(cdiag_done, 2)
                    mm(bank[6][:, 0:T], ones[:, :], tmp[:, 0, 0:T], start=True, stop=True).then_inc(cb_ready, 1)
            pe.wait_ge(cact_done, CC)
            project("pc", conv, kk=CC, n=4)
            pe.wait_ge(sc_used, 4 * (LEVELS + 1))
            pe.wait_ge(q_done, 2 * (LEVELS + 1))
            pe.wait_ge(s_s0, 16)
            evacuated(pe, "v1", 1)

            def heads_out(g):
                if g >= 2:
                    pe.wait_ge(o_copied, g - 1)
                for i in range(4):
                    at_ = 4 * g + i
                    h, s = at_ // 2, at_ % 2
                    out = bank[4 + g % 2][:, i * P:(i + 1) * P]
                    ins = mm(out, v_tok[:, s, h * P:(h + 1) * P], att[:, at_, :], start=True, stop=(s == 0))
                    if s:
                        mm(out, s0[:, h, :], qk[:, 1, at_ * P:(at_ + 1) * P], start=False, stop=False)
                        ins = mm(out, s0[:, H + h, :], qk[:, 0, at_ * P:(at_ + 1) * P], start=False, stop=True)
                ins.then_inc(o_ready, 1)

            def squares(g):
                pe.wait_ge(o_copied, g + 1)
                if g == 0:
                    pe.wait_ge(mod_done, 4)
                else:
                    pe.wait_ge(oms_done, g)
                for i in range(4):
                    col = 384 + 4 * g + i
                    ins = mm(bank[7][:, col:col + 1], tmp[:, g % 2, i * P:(i + 1) * P], ones[:, 0:1], start=True, stop=True)
                ins.then_inc(osq_ready, 1)

            def spread(g):
                pe.wait_ge(odiag_done, g + 1)
                if g:
                    pe.wait_ge(ob_used, g)
                mm(bank[6][:, :], ones[:, :], tmp[:, g % 2, :], start=True, stop=True).then_inc(ob_ready, 1)

            def keys_by_token(j):
                b = open_fill("kt", j)
                for i in range(4):
                    d, h = divmod(4 * j + i, H)
                    ins = nc.tensor.transpose(b[:, i * P:(i + 1) * P], qk[:, 2 + d, 2 * h * P:(2 * h + 1) * P], ident)
                ins.then_inc(proj_ready, 1)

            def final_states(j):
                b = open_fill("st", j)
                evacuated(pe, "kt", j)
                for i in range(4):
                    h = (4 * j + i) % H
                    ins = mm(b[:, i * P:(i + 1) * P], k_tok[:, 4 * j + i, :], v_tok[:, 0, h * P:(h + 1) * P], start=True, stop=True)
                ins.then_inc(proj_ready, 1)

            heads_out(0)
            heads_out(1)
            pe.wait_ge(k_done, 2 * LEVELS)
            keys_by_token(0)
            keys_by_token(1)
            squares(0)
            heads_out(2)
            keys_by_token(2)
            squares(1)
            spread(0)
            heads_out(3)
            keys_by_token(3)
            squares(2)
            spread(1)
            final_states(0)
            squares(3)
            spread(2)
            final_states(1)
            final_states(2)
            spread(3)
            final_states(3)
            project("ph0", o_t, before_k=lambda k: pe.wait_ge(ob_used, k // 2 + 1))
            project("ph1", o_t)
            pe.wait_ge(merged, 4)
            project("wo0", ga)
            project("wo1", ga)

            def to_tokens(name, src):
                for j in range(4):
                    s, hf = j // 2, j % 2
                    b = open_fill(name, j)
                    for i in range(4):
                        ins = nc.tensor.transpose(b[:, i * P:(i + 1) * P], src[:, 4 * hf + i, s * P:(s + 1) * P], ident)
                    ins.then_inc(proj_ready, 1)

            evacuated(pe, "wo1", 1)
            to_tokens("t1", x_t)
            pe.wait_ge(xn2_done, 2)
            for j in range(4):
                to_channels(("n2", j), xn2, j).then_inc(proj_ready, 1)
            evacuated(pe, "n2", 3)
            pe.wait_ge(s_wr, 16)
            for s in range(NS):
                for k in range(KD):
                    ins = mm(bank[4][:, s * NE:(s + 1) * NE], h_t[:, k, s * P:(s + 1) * P], w_r[:, k, :], start=(k == 0), stop=(k == KD - 1))
            ins.then_inc(lg_ready, 1)
            to_tokens("hr", h_t)
            pe.wait_ge(s_sg, 16)
            for name, col in (("sg", 0), ("su", FF)):
                b = open_fill(name)
                for c in range(2):
                    for k in range(KD):
                        ins = mm(b[:, c * T:(c + 1) * T], w_sg[:, k, col + c * P:col + (c + 1) * P], h_t[:, k, :], start=(k == 0), stop=(k == KD - 1))
                ins.then_inc(proj_ready, 1)
            tri = consts[:, C_TRI:C_TRI + P]
            pe.wait_ge(lg_mask, 1)
            mm(bank[5][:, 0:NE], tri, mask[:, 0, :], start=True, stop=True)
            mm(bank[5][:, NE:2 * NE], tri, mask[:, 1, :], start=True, stop=False)
            mm(bank[5][:, NE:2 * NE], ones[:, :], mask[:, 0, :], start=False, stop=True)
            for s in range(NS):
                ins = mm(bank[5][0:NE, 128:129], mask[:, s, :], ones[:, 0:1], start=(s == 0), stop=(s == 1))
            ins.then_inc(cnt_ready, 1)
            pe.wait_ge(nx_done, 1)
            mm(bank[5][0:NE, 130:131], consts[0:NE, C_TRIE:C_TRIE + NE], nxt[0:NE, 3:4], start=True, stop=True).then_inc(end_ready, 1)
            for s in range(NS):
                nc.tensor.transpose(bank[6][0:NE, s * P:(s + 1) * P], posm[:, s, :], ident)
                ins = nc.tensor.transpose(bank[6][0:NE, T + s * P:T + (s + 1) * P], comb[:, s, :], ident)
            ins.then_inc(pt1_ready, 1)
            pe.wait_ge(oh_done, 1)
            pe.wait_ge(pt1_copied, 1)
            for s in range(NS):
                out = bank[5][:, 320 + s * NX:320 + (s + 1) * NX]
                mm(out, tmp[0:NE, 0, s * P:(s + 1) * P], hot[0:NE, :], start=True, stop=False)
                mm(out, neg[0:NE, :], hotb[0:NE, :], start=False, stop=True)
                mm(bank[5][:, 384 + s * NX:384 + (s + 1) * NX], tmp[0:NE, 0, T + s * P:T + (s + 1) * P], hot[0:NE, :], start=True, stop=True)
            mm(bank[5][0:1, 256:256 + NX], consts[0:NE, C_ECOL:C_ECOL + 1], hot[0:NE, :], start=True, stop=True)
            mm(bank[5][0:1, 296:297], nxt[0:NE, 3:4], ones[0:NE, 0:1], start=True, stop=True).then_inc(items_ready, 1)
            pe.wait_ge(items_done, 2)
            for j in range(4):
                s, hf = j // 2, j % 2
                for i in range(4):
                    k = 4 * hf + i
                    ins = mm(bank[4 + j][:, i * P:(i + 1) * P], mod_v[:, M_GT2 + k, s:s + 1].broadcast_to([P, P]), ident, start=True, stop=True)
                ins.then_inc(gr_ready, 1)

            def gather(b, half, p1):
                for i in range(4):
                    k = 4 * half + i
                    for n, (s, part) in enumerate(((0, h_hi), (0, h_lo), (1, h_hi), (1, h_lo))):
                        ins = mm(bank[half][:, i * P:(i + 1) * P], part[:, s, k, :], sel_p[b][:, s, :], start=(n == 0), stop=(n == 3))
                ins.then_inc(gbk_ready if half else ga_ready, 1)

            def turn(b):
                for s in range(NS):
                    nc.tensor.transpose(bank[0][:, s * P:(s + 1) * P], sel_p[b][:, s, :].bitcast(F32), ident)
                for s in range(NS):
                    ins = mm(bank[0][:, T:T + 2], sel_p[b][:, s, :].bitcast(F32), comb_p[b][:, s, :], start=(s == 0), stop=(s == 1))
                ins.then_inc(pt_ready, 1)

            def scatter(b, h, start=False):
                for s in range(NS):
                    for part in ((y_hi,) if start else (y_hi, y_lo)):
                        ins = mm(y_acc[s][h][:, :], sel_t[b][:, s * P:(s + 1) * P], part[1 if start else h][:, :], start=start, stop=False)
                return ins

            pe.wait_ge(gr_done, 4)
            pe.wait_ge(y_ready, 2)
            for h in range(2):
                scatter(1, h, start=True)
            pe.wait_ge(built, 1)
            evacuated(pe, "hr", 2)
            evacuated(pe, "hr", 3)
            gather(0, 0, 1)
            gather(0, 1, 1)
            pe.wait_ge(ga_evac, 1)
            turn(0)
            evacuated(pe, "sg")
            evacuated(pe, "su")

            def pair(b, p):
                slots = (2 * b, 2 * b + 1)
                i = p // 2 if isinstance(p, int) else iteration[0]
                gu_bank, other = bank[2 + b], bank[3 - b]
                pe.wait_ge(gbk_evac, p + 1)
                pe.wait_ge(y_ready, p * 2 + 1)
                for e in range(2):
                    pe.wait_ge(s_gu[slots[e]], i * 16 + 16)
                for k in range(KD):
                    for e in range(2):
                        ins = mm(gu_bank[e * C:(e + 1) * C, :], xg[b][:, k, e * C:(e + 1) * C], w_gu[slots[e]][:, k, :], start=(k == 0), stop=(k == KD - 1))
                ins.then_inc(gu_ready, 1)
                pe.wait_ge(y_ready, p * 2 + 2)
                scatter(1 - b, 1)
                pe.wait_ge(built, p + 2)
                pe.wait_ge(pt_evac, p + 1)
                gather(1 - b, 0, p + 2)
                pe.wait_ge(act_ready, p + 1)
                for c in range(2):
                    ins = nc.tensor.transpose(gu_bank[:, c * P:(c + 1) * P], act_r[:, c * P:(c + 1) * P], ident)
                ins.then_inc(t_ready, 1)
                gather(1 - b, 1, p + 2)
                pe.wait_ge(ga_evac, p + 2)
                turn(1 - b)
                for e in range(2):
                    pe.wait_ge(s_dn[slots[e]], i * 16 + 16)
                pe.wait_ge(t_evac, p + 1)
                for h, out in enumerate((other, gu_bank)):
                    for c in range(2):
                        for e in range(2):
                            ins = mm(out[e * C:(e + 1) * C, :], act_t[:, c, e * C:(e + 1) * C], w_dn[slots[e]][:, c, h * 512:(h + 1) * 512],
                                     start=(c == 0), stop=(c == 1))
                    ins.then_inc(dn_ready, 1)
                pe.wait_ge(y_ready, p * 2 + 3)
                scatter(b, 0)

            iteration = [None]
            if USE_IF:
                n = pe.value_load(nwork, min_val=0, max_val=NI)
            with pe.Fori(0, ITERS) as i:
                iteration[0] = i
                if USE_IF:
                    with pe.If(n > i * 4):
                        for b in range(2):
                            pair(b, i * 2 + b)
                else:
                    for b in range(2):
                        pair(b, i * 2 + b)
            pe.wait_ge(loop_done, 1)
            scatter(1, 1)
            pe.wait_ge(s_sd, 16)
            for s in range(NS):
                for hf in range(2):
                    for c in range(2):
                        ins = mm(y_acc[s][hf][:, :], act_s[:, c, s * P:(s + 1) * P], w_sd[:, c, hf * 512:(hf + 1) * 512], start=False, stop=(c == 1))
            ins.then_inc(y_done, 1)


INPUTS = ["x_prompt", "x_sample", "state_hgrn", "c", "c_ctx", "w_ada", "b_ada", "norm1_g", "w_in", "hgrn_lb_logits", "hgrn_norm_g",
          "w_proj_hgrn", "conv_dw_w", "conv_dw_b", "conv_norm_g", "conv_norm_b", "w_proj_conv", "w_out", "norm2_g", "w_router",
          "router_bias", "w_expert_gate_up", "w_expert_down", "w_shared_gate_up", "w_shared_down", "final_norm_g"]


def constants():
    import numpy as np

    n = np.arange(P)
    out = np.zeros((P, C_ALL), np.float32)
    out[:, C_ID:C_ID + P] = n[:, None] == n
    for level in range(LEVELS):
        out[:, C_MASK + P * level:C_MASK + P * (level + 1)] = ((n[:, None] ^ n) >> level) == 1
    out[:, C_TRI:C_TRI + P] = n[:, None] < n
    out[:NE, C_TRIE:C_TRIE + NE] = n[:NE, None] <= n[:NE]
    out[:, C_IOTA:C_IOTA + C] = n[:C]
    out[:, C_LT:C_LT + 64] = (np.arange(8)[:, None] > np.arange(8)).reshape(-1)
    out[:, C_ECOL] = n
    out[:, C_SUM:C_SUM + NS] = (n % 32)[:, None] == np.arange(NS)
    return out


def kernel(**inputs):
    import numpy as np
    import concourse.bacc as bacc
    from concourse.bass_utils import run_bass_kernel_spmd

    nc = bacc.Bacc("TRN2", target_bir_lowering=False, num_devices=1)
    arrays, aps = {}, {}
    for name in INPUTS:
        array = np.ascontiguousarray(inputs[name])
        arrays[f"in_{name}"] = array
        aps[name] = nc.dram_tensor(f"in_{name}", array.shape, mybir.dt.from_np(array.dtype), kind="ExternalInput").ap()
    arrays["in_consts"] = constants()
    aps["consts"] = nc.dram_tensor("in_consts", (P, C_ALL), F32, kind="ExternalInput").ap()
    shapes = [(1, P, D), (1, P, D), (1, 1, 2, H, P, P)]
    outs = [nc.dram_tensor(f"out_{i}", shape, F32, kind="ExternalOutput").ap() for i, shape in enumerate(shapes)]
    build(nc, aps, outs)
    result = run_bass_kernel_spmd(nc, [arrays], core_ids=[0]).results[0]
    return tuple(result[f"out_{i}"] for i in range(len(shapes)))
```

```python
from contextlib import ExitStack

import concourse.bass as bass
from concourse import mybir
from concourse.alu_op_type import AluOpType as ALU

ACT = mybir.ActivationFunctionType
F32 = mybir.dt.float32
F32R = mybir.dt.float32r
I32 = mybir.dt.int32
U32 = mybir.dt.uint32
AX = mybir.AxisListType.X

P = 128
D = 1024
KD = D // P
NS = 2
T = NS * P
H = 8
NE = 64
FF = 256
TOPK = 8
ROUTED_SCALE = 2.5
EPS = 1e-6
CW = 31
CC = 4
PAD = CW // 2
UW = P + 2 * PAD
C = 64
LEVELS = 7

NX = T * TOPK // C
NI = NE + NX
ITERS = NI // 4
MAIN = NE // 4
FEW = MAIN + 1
BIG = 3.0e38

C_ID, C_MASK = 0, P
C_TRI = C_MASK + LEVELS * P
C_TRIE = C_TRI + P
C_IOTA = C_TRIE + NE
C_LT = C_IOTA + C
C_ECOL = C_LT + 64
C_SUM = C_ECOL + 1
C_ALL = C_SUM + NS

R_C, R_BADA, R_G1, R_G2, R_HG, R_LB = 0, 16, 64, 72, 80, 88
R_DWB, R_CNG, R_CNB = 104, 108, 112
R_ALL = 116

Q0, V0, ZF0, ZB0, OG0, U0, GZ0 = 0, 1024, 2048, 3072, 4096, 5120, 6144
M_SH1, M_SC1, M_GT1, M_SH2, M_SC2, M_GT2 = 0, 8, 16, 24, 32, 40

KB = 1024
BASE = 16512


class Own:

    def __init__(self, eng, sem):
        self.eng, self.sem, self.n = eng, sem, 0

    def mark(self, instruction):
        instruction.then_inc(self.sem, 1)
        self.n += 1
        return self.n

    def wait(self, n=None):
        self.eng.wait_ge(self.sem, self.n if n is None else n)

    def step(self, instruction):
        self.mark(instruction)
        self.wait()


def build(nc, A, outs):
    y_prompt, y_sample, new_state = outs
    ctx = ExitStack()
    with ctx:
        def at(name, kb, shape, dt=F32):
            return nc.alloc_sbuf_tensor_at(name, shape, dt, offset=BASE + int(kb * KB))

        def sem(name):
            return ctx.enter_context(nc.semaphore(name))

        ring = [at(f"ring{i}", 16 * i, [P, 4096]) for i in range(4)]
        ga = at("ga", 64, [P, H, T])
        gb = at("gb", 72, [P, H, T])
        att = at("att", 80, [P, 16, P])
        og = at("og", 88, [P, H, T])
        x_t = at("x_t", 96, [P, KD, T])
        h_t = at("h_t", 104, [P, KD, T])
        qk = at("qk", 112, [P, 4, 16 * P])
        xn = at("xn", 128, [P, NS, D])
        fg = at("fg", 144, [P, 2, 16 * P])
        o_t = at("o_t", 144, [P, H, T])
        k_tok = at("k_tok", 152, [P, 16, P])
        x_tok = at("x_tok", 160, [P, NS, D])
        v_tok = at("v_tok", 160, [P, NS, D])
        s0 = at("s0", 168, [P, 16, P])
        h1_hi = at("h1_hi", 168, [P, KD, T], F32R)
        h1_lo = at("h1_lo", 160, [P, KD, T], F32R)
        w_hi = at("w_hi", 64, [P, 4, KD, P], F32R)
        w_lo = at("w_lo", 80, [P, 4, KD, P], F32R)
        h1_rest = at("h1_rest", 104, [P, KD, T], F32R)
        ring_hi = at("ring_hi", 48, [P, KD, 4 * P], F32R)
        ring_lo = [at(f"ring_lo{i}", 16 * i, [P, KD, 4 * P], F32R) for i in range(3)]
        upad = at("upad", 176, [P, CC, NS, UW])
        conv = at("conv", 181, [P, CC, T])
        tmp = at("tmp", 185, [P, 2, 512])
        consts = at("consts", 189, [P, C_ALL])
        vec = at("vec", 194.5, [P, P])
        small = at("small", 195, [P, 256])
        ones = at("ones", 196, [P, P])
        dw = at("dw", 196.5, [P, CW, CC])
        rows = at("rows", 197, [P, P])
        rows_dw = at("rows_dw", 198, [P, P])
        s_new = at("s_new", 197, [P, 16, P])
        k_mix = at("k_mix", 197, [P, 16 * P])
        w_r = at("w_r", 181, [P, KD, NE])
        c_pad = at("c_pad", 205, [P, KD, 32])
        b_router = at("b_router", 207, [P, NE])
        mod = at("mod", 207.25, [P, 48, NS])
        w_gu = [at(f"w_gu{i}", 24 * i, [P, KD, 2 * FF]) for i in range(4)]
        w_dn = [at(f"w_dn{i}", 24 * i + 16, [P, 2, D]) for i in range(4)]
        h_hi = at("h_hi", 112, [P, NS, KD, P], F32R)
        h_lo = at("h_lo", 120, [P, NS, KD, P], F32R)
        x1 = at("x1", 128, [P, NS, D])
        g2row = at("g2row", 136, [P, NS, D])
        xg = at("xg", 144, [P, KD, 4 * C])
        sel_p = at("sel_p", 182, [P, NS, 4 * C], F32R)
        sel_t = [at(f"sel_t{i}", 154 + i, [P, T], F32R) for i in range(2)]
        act_t = at("act_t", 156, [P, 2, P])
        act_r = at("act_r", 157, [P, 2 * P])
        sil = at("sil", 158, [P, 2 * P])
        y_hi = [at(f"y_hi{i}", 160 + 2 * i, [P, 512], F32R) for i in range(2)]
        y_lo = [at(f"y_lo{i}", 164 + 2 * i, [P, 512], F32R) for i in range(2)]
        fin_g = at("fin_g", 168, [P, D])
        pos_i = at("pos_i", 172, [P, NS, NI + 4])
        comb_i = at("comb_i", 173, [P, NS, NI + 4])
        comb_p = at("comb_p", 174, [P, NS, 4])
        w_slot = [at(f"w_slot{i}", 174.125 + i / 32, [P, 1]) for i in range(2)]
        e_row = at("e_row", 174.5, [P, NX + 4], I32)
        act_s = at("act_s", 176, [P, 2, T])
        sil_s = at("sil_s", 178, [P, 2, T])
        w_sg = at("w_sg", 144, [P, KD, 2 * FF])
        w_sd = at("w_sd", 104, [P, 2, D])
        diag2 = at("diag2", 176, [P, T])
        inv2 = at("inv2", 177, [P, T])
        h_full = at("h_full", 96, [P, NS, KD, P])
        fin = at("fin", 96, [P, NS, D])
        fin_sq = at("fin_sq", 112, [P, NS, D])
        rt = at("rt", 197, [P, 2048])

        def pb(name):
            return ctx.enter_context(nc.psum_tensor(name, [P, 512], F32))

        bank = [pb(f"bank{i}") for i in range(8)]
        y_acc = [[bank[4 + 2 * s + h] for h in range(2)] for s in range(NS)]

        ident = consts[:, C_ID:C_ID + P]

        def sm(lo, n):
            return small[:, lo:lo + n]

        gain1 = sm(16, 16)
        gain2 = sm(32, 16)
        lb = sm(48, 16)
        oml = sm(64, 16)
        csig = sm(80, 16)
        ssq = sm(96, 2)
        rms = sm(98, 2)
        ssq_c = sm(100, 2)
        rms_c = sm(102, 2)
        ssq_o = sm(104, 16)
        rms_o = sm(120, 16)
        mhalf = sm(136, 16)
        ms2 = sm(152, 2)
        rms2 = sm(154, 2)
        ssqf = sm(156, 2)
        rmsf = sm(158, 2)
        nwork = small[0:1, 162:163].bitcast(I32)
        mod_v = mod[:, :, :]

        s_x, s_cst, s_rows, s_s0, s_wr, s_fing = map(sem, ("x_loaded", "consts_loaded", "rows_loaded", "s0_loaded", "router_loaded", "fing_loaded"))
        s_w = [sem(f"ring_loaded{i}") for i in range(4)]
        s_gu = [sem(f"gu_loaded{i}") for i in range(4)]
        s_dn = [sem(f"dn_loaded{i}") for i in range(4)]
        s_init = sem("init_done")
        own_dve, own_act = sem("own_dve"), sem("own_act")
        vec_ready, vec_copied = sem("vec_ready"), sem("vec_copied")
        ssq_ready, rms_ready = sem("ssq_ready"), sem("rms_ready")
        s_pad, part_ready, part_copied = sem("pad_zeroed"), sem("ada_partial"), sem("ada_partial_copied")
        c_sig, c_silu = sem("c_sig"), sem("c_silu")
        xn_done = sem("xn_done")
        mod_ready, mod_done = sem("mod_ready"), sem("mod_done")
        proj_ready = sem("proj_ready")
        act_evac, dve_evac = sem("act_evac"), sem("dve_evac")
        h1_hi_done, h1_lo_done = sem("h1_hi_done"), sem("h1_lo_done")
        w_hi_done, w_lo_done, w_used = sem("w_hi_done"), sem("w_lo_done"), sem("w_even_parts_used")
        u_gated, fk_done, og_sig = sem("u_gated"), sem("fk_done"), sem("og_sig")
        sc_ready, sc_used = sem("scores_ready"), sem("scores_used")
        mix_done = sem("keys_mixed")
        q_done, k_done, tot_done = sem("q_updated"), sem("k_updated"), sem("totals_done")
        conv_done, mean_ready, cen_done, csq_done = map(sem, ("conv_done", "mean_ready", "centred", "conv_squared"))
        cvar_ready, cms_done, crms_done, cdiag_done = map(sem, ("cvar_ready", "cms_done", "crms_done", "cdiag_done"))
        cb_ready, cn_done, cs_done, cact_done = map(sem, ("conv_bcast_ready", "conv_normed", "conv_sig", "conv_act"))
        o_ready, o_copied, osq_ready = sem("o_ready"), sem("o_copied"), sem("o_ssq_ready")
        oms_done, orms_done = sem("o_ms_done"), sem("o_rms_done")
        odiag_done, ob_ready, ob_used = sem("o_diag_done"), sem("o_bcast_ready"), sem("o_normed")
        s_state = sem("state_stored")
        merged = sem("merged")
        x1_sq, ssq2_ready, ms2_done, rms2_done = sem("x1_squared"), sem("ssq2_ready"), sem("ms2_done"), sem("rms2_done")
        diag2_done, spread2, inv2_done = sem("diag2_done"), sem("rms2_spread"), sem("inv2_done")
        x1n_done, h2_done = sem("x1_normed"), sem("h2_done")
        lg_ready, lg_sig, lg_mask = sem("logits_ready"), sem("scores_done"), sem("mask_done")
        hr_lo = sem("h2_lo_done")
        s_sg, s_sd = sem("shared_gate_up_loaded"), sem("shared_down_loaded")
        cnt_ready, nx_done, end_ready, oh_done = map(sem, ("count_ready", "nx_done", "end_ready", "onehot_done"))
        posm_done, pt1_ready, pt1_copied = sem("posm_done"), sem("post_ready"), sem("post_copied")
        items_ready, items_done = sem("items_ready"), sem("items_done")
        built, ga_ready, ga_evac, gbk_ready, gbk_evac = map(sem, ("built", "gather_a", "gather_a_evac", "gather_b", "gather_b_evac"))
        pt_ready, pt_evac = sem("sel_t_ready"), sem("sel_t_evac")
        gu_ready, sil_ready, act_ready = sem("gu_ready"), sem("sil_ready"), sem("act_ready")
        t_ready, t_evac = sem("act_t_ready"), sem("act_t_evac")
        dn_ready, hi_ready, y_ready = sem("dn_ready"), sem("y_hi_ready"), sem("y_split_ready")
        loop_done, y_done, x2_done, sqf_done, f_ssq, f_rms, out_done, s_out = map(sem, ("loop_done", "y_done", "x2_done", "x2_squared", "final_ssq", "final_rms", "out_done", "stored"))

        def cols(w, c0):
            return w.rearrange("(k p) c -> p k c", p=P)[:, :, c0:c0 + 512]

        w_ada, w_in = A["w_ada"][0], A["w_in"][0]
        blocks = [(f"ada{j}", cols(w_ada, 512 * j)) for j in range(4)]
        ada_after = {name: 4 + n for n, name in enumerate(("u1", "u2", "q0", "zf0", "zb0", "q1", "zf1", "zb1"))}
        for name, c0 in (("u1", U0), ("u2", U0 + 512), ("q0", Q0), ("zf0", ZF0), ("zb0", ZB0), ("q1", Q0 + 512),
                         ("zf1", ZF0 + 512), ("zb1", ZB0 + 512), ("v0", V0), ("v1", V0 + 512),
                         ("og0", OG0), ("og1", OG0 + 512), ("ga0", GZ0), ("ga1", GZ0 + 512), ("gb0", GZ0 + 1024), ("gb1", GZ0 + 1536)):
            blocks.append((name, cols(w_in, c0)))
            if name in ada_after:
                j = ada_after[name]
                blocks.append((f"ada{j}", cols(w_ada, 512 * j)))
        blocks.append(("pc", A["w_proj_conv"][0].rearrange("(k p) c -> p k c", p=P)))
        blocks += [(f"ph{j}", cols(A["w_proj_hgrn"][0], 512 * j)) for j in range(2)]
        blocks += [(f"wo{j}", cols(A["w_out"][0], 512 * j)) for j in range(2)]
        split = ["u2", "q0", "zf0", "zb0", "q1", "zf1", "zb1"]
        apart = len(split)
        split += ["og0", "og1", "ga0", "ga1", "gb0", "gb1"]
        h1_rest_done = sem("h1_rest_done")
        number = {name: n for n, (name, _) in enumerate(blocks)}

        place = {name: n % 4 for name, n in number.items()}
        for n, name in enumerate(("v0", "v1", "og0", "og1", "ga0", "ga1", "gb0", "gb1", "pc", "ph0", "ph1", "wo0")):
            place[name] = n % 3
        place["wo1"] = 3
        in_place = [[name for name, _ in blocks if place[name] == i] for i in range(4)]

        def loaded(eng, name):
            eng.wait_ge(s_w[place[name]], 16 * (in_place[place[name]].index(name) + 1))

        def part_hi(n, q):
            return w_hi[:, q, :, :] if n < apart else ring_hi[:, :, q * P:(q + 1) * P]

        def part_lo(n, q):
            return w_lo[:, q, :, :] if n < apart else ring_lo[place[split[n]]][:, :, q * P:(q + 1) * P]

        def tile_of(name):
            src = blocks[number[name]][1]
            k, n = src.shape[1], src.shape[2]
            return ring[place[name]][:, 0:k * n].rearrange("p (k c) -> p k c", k=k)

        gu_src = A["w_expert_gate_up"][0].rearrange("e (p k) f -> e p k f", k=KD)
        dn_src = A["w_expert_down"][0].rearrange("e (c p) d -> e p c d", p=P)

        fills, n_act, n_dve = [], 0, 0
        for name, n, by in ([(f"xt{j}", 1, "act") for j in range(4)] + [(f"h{j}", 1, "dve") for j in range(4)]
                            + [("u1", 2, "act"), ("u2", 2, "act"), ("q0", 2, "act"), ("zf0", 2, "act"), ("zb0", 2, "act"),
                               ("q1", 2, "act"), ("zf1", 2, "act"), ("zb1", 2, "act"), ("v0", 2, "act"), ("v1", 2, "act"),
                               ("og0", 2, "dve"), ("og1", 2, "dve"), ("ga0", 2, "act"), ("ga1", 2, "act"), ("gb0", 2, "act"),
                               ("gb1", 2, "act"), ("pc", 4, "dve"), ("kt", 4, "act"), ("st", 4, "act"), ("ph0", 2, "dve"), ("ph1", 2, "dve"), ("wo0", 2, "dve"), ("wo1", 2, "dve"),
                               ("t1", 4, "act"), ("g2", 4, "act"), ("hr", 4, "act"), ("sg", 1, "act"), ("su", 1, "dve")]):
            for j in range(n):
                if by == "act":
                    n_act += 1
                    fills.append((name, j, act_evac, n_act))
                else:
                    n_dve += 1
                    fills.append((name, j, dve_evac, n_dve))
        fill_no = {(name, j): n for n, (name, j, _, _) in enumerate(fills)}

        def fill_bank(name, j=0):
            return bank[fill_no[name, j] % 4]

        def released(eng, name):
            if name in split[:apart]:
                eng.wait_ge(w_lo_done, 4 * split.index(name) + 4)
            elif name[:3] == "ada":
                eng.wait_ge(part_ready, int(name[3:]) + 1)
            else:
                last = {"pc": ("pc", 3)}.get(name, (name, 1))
                eng.wait_ge(proj_ready, fill_no[last] + 1)

        def evacuated(eng, name, j=0):
            eng.wait_ge(fills[fill_no[name, j]][2], fills[fill_no[name, j]][3])

        def filled(eng, name, j=0):
            eng.wait_ge(proj_ready, fill_no[name, j] + 1)

        def query_mix(level, g):
            m = 1 << level
            base = qk[:, 0, g * P:(g + 1) * P]
            dims = [list(base.ap[0]), [2 * m, P // (2 * m)], [16 * P + m, 2]]
            if m > 1:
                dims.append([1, m])
            return bass.AP(base.tensor, base.offset, dims)

        def halves(arr, level):
            m = 1 << level
            return arr.rearrange("p (n h m) -> p n h m", h=2, m=m)

        off = [0]

        def r(n, *shape):
            v = rt[:, off[0]:off[0] + n]
            off[0] += n
            return v

        score = r(NS * NE).rearrange("p (s e) -> p s e", s=NS)
        sel = r(NS * NE).rearrange("p (s e) -> p s e", s=NS)
        top = r(NS * 64).rearrange("p (s g j) -> p s g j", s=NS, g=8)
        grp = r(16).rearrange("p (s g) -> p s g", s=NS)
        cmp = r(NS * 64).rearrange("p (s g j) -> p s g j", s=NS, g=8)
        ceq = r(NS * 64).rearrange("p (s g j) -> p s g j", s=NS, g=8)
        rank = r(16)
        gmask = r(16).rearrange("p (s g) -> p s g", s=NS)
        selm = r(NS * NE).rearrange("p (s e) -> p s e", s=NS)
        rep = r(NS * NE).rearrange("p (s e) -> p s e", s=NS)
        best = r(16).rearrange("p (s j) -> p s j", s=NS)
        mask = r(NS * NE).rearrange("p (s e) -> p s e", s=NS)
        comb = r(NS * NE).rearrange("p (s e) -> p s e", s=NS)
        wsum = r(2)
        wrec = r(2)
        posm = r(NS * NE).rearrange("p (s e) -> p s e", s=NS)
        nxt = r(4)
        endx = r(2)
        hot = r(NX)
        hot2 = r(NX)
        hotb = r(NX)
        neg = r(P)
        assert off[0] <= 2048
        iota_x = consts[0:NE, C_IOTA:C_IOTA + NX]

        def loop(eng, pair):
            eng.wait_ge(items_done, 2)
            n = eng.value_load(nwork, min_val=0, max_val=NI)

            def iteration(i):
                with eng.If(n > i * 4):
                    pair(0, i, None)
                    pair(1, i, n > i * 4 + 4)

            with eng.Fori(0, FEW) as i:
                iteration(i)
            with eng.If(n > FEW * 4):
                with eng.Fori(FEW, ITERS) as i:
                    iteration(i)

        def by_row(x):
            return x.rearrange("(k p) -> k p", p=P)

        loads_small = [(by_row(A["c_ctx"]), rows[R_C:R_C + 8, :]), (by_row(A["c"][0]), rows[R_C + 8:R_C + 16, :]),
                       (by_row(A["b_ada"][0]), rows[R_BADA:R_BADA + 48, :]), (by_row(A["norm1_g"][0]), rows[R_G1:R_G1 + 8, :]),
                       (by_row(A["norm2_g"][0]), rows[R_G2:R_G2 + 8, :]), (by_row(A["hgrn_norm_g"][0]), rows[R_HG:R_HG + 8, :]),
                       (A["hgrn_lb_logits"][0].rearrange("a (k p) -> (a k) p", p=P), rows[R_LB:R_LB + 16, :]),
                       (by_row(A["conv_dw_b"][0]), rows[R_DWB:R_DWB + 4, :]), (by_row(A["conv_norm_g"][0]), rows[R_CNG:R_CNG + 4, :]),
                       (by_row(A["conv_norm_b"][0]), rows[R_CNB:R_CNB + 4, :]),
                       (A["conv_dw_w"][0].rearrange("w (c p) -> (w c) p", p=P), rows_dw[0:CW * CC, :]),
                       (A["router_bias"].broadcast_to([P, NE]), b_router[:, :])]

        block = ctx.enter_context(nc.Block())

        @block.sync
        def _(sp):
            sp.dma_start(x_tok[:, 0, :], A["x_prompt"][0]).then_inc(s_x, 16)
            for x, dst in loads_small[0::2]:
                sp.dma_start(dst, x).then_inc(s_rows, 16)
            sp.dma_start(x_tok[:, 1, :], A["x_sample"][0]).then_inc(s_x, 16)
            for n, (name, src) in enumerate(blocks):
                before = in_place[place[name]].index(name) - 1
                if before >= 0:
                    released(sp, in_place[place[name]][before])
                sp.dma_start(tile_of(name), src).then_inc(s_w[place[name]], 16)
                if name == "ph1":
                    filled(sp, "gb1", 1)
                    sp.dma_start(s0[:, :, :], A["state_hgrn"][0, 0].rearrange("a h k v -> k (a h) v")).then_inc(s_s0, 16)
                if name == "ph1":
                    released(sp, "pc")
                    sp.dma_start(w_r[:, :, :], A["w_router"][0].rearrange("(k p) e -> p k e", p=P)).then_inc(s_wr, 16)
                if name == "ph1":
                    evacuated(sp, "st", 3)
                    sp.dma_start(new_state[0, 0].rearrange("a h k v -> k (a h) v"), s_new[:, :, :]).then_inc(s_state, 16)
                if name == "wo1":
                    released(sp, "ph1")
                    sp.dma_start(w_sg[:, :, :], cols(A["w_shared_gate_up"][0], 0)).then_inc(s_sg, 16)
                    sp.dma_start(fin_g[:, :], A["final_norm_g"].rearrange("(a d) -> a d", a=1).broadcast_to([P, D])).then_inc(s_fing, 16)

            def load(slot, e):
                sp.dma_start(w_gu[slot][:, :, :], gu_src[e]).then_inc(s_gu[slot], 16)
                sp.dma_start(w_dn[slot][:, :, :], dn_src[e]).then_inc(s_dn[slot], 16)

            for slot, over in ((0, (0, 1)), (3, ()), (1, (1, 2)), (2, (3,))):
                for i in over:
                    released(sp, in_place[i][-1])
                if slot == 2:
                    released(sp, "wo1")
                if slot == 3:
                    sp.wait_ge(merged, 4)
                load(slot, slot)
            filled(sp, "su")
            sp.dma_start(w_sd[:, :, :], A["w_shared_down"][0].rearrange("(k p) c -> p k c", p=P)).then_inc(s_sd, 16)

            def slots_free(i, b, down):
                if down:
                    sp.wait_ge(dn_ready, i * 4 + (2 * b - 2))
                else:
                    sp.wait_ge(gu_ready, i * 2 + (b - 1))

            with sp.Fori(1, MAIN) as i:
                for b in range(2):
                    slots_free(i, b, False)
                    for slot in (2 * b, 2 * b + 1):
                        sp.dma_start(w_gu[slot][:, :, :], gu_src[i * 4 + slot]).then_inc(s_gu[slot], 16)
                    slots_free(i, b, True)
                    for slot in (2 * b, 2 * b + 1):
                        sp.dma_start(w_dn[slot][:, :, :], dn_src[i * 4 + slot]).then_inc(s_dn[slot], 16)
            sp.wait_ge(items_done, 2)
            n = sp.value_load(nwork, min_val=0, max_val=NI)
            with sp.Fori(MAIN, ITERS) as i:
                with sp.If(n > i * 4):
                    for b in range(2):
                        experts = [sp.value_load(e_row[0:1, bass.ds(i * 4 + (slot - NE), 1)], min_val=0, max_val=NE - 1) for slot in (2 * b, 2 * b + 1)]
                        slots_free(i, b, False)
                        for slot, e in zip((2 * b, 2 * b + 1), experts):
                            sp.dma_start(w_gu[slot][:, :, :], gu_src[bass.ds(e, 1)].rearrange("a p k f -> (a p) k f")).then_inc(s_gu[slot], 16)
                        slots_free(i, b, True)
                        for slot, e in zip((2 * b, 2 * b + 1), experts):
                            sp.dma_start(w_dn[slot][:, :, :], dn_src[bass.ds(e, 1)].rearrange("a p c d -> (a p) c d")).then_inc(s_dn[slot], 16)
            for s, out in enumerate((y_prompt, y_sample)):
                for hf in range(2):
                    c = slice(hf * 512, (hf + 1) * 512)
                    sp.wait_ge(out_done, 2 * s + hf + 1)
                    sp.dma_start(out[0][:, c], fin[:, s, c]).then_inc(s_out, 16)
            sp.wait_ge(s_state, 16)
            sp.wait_ge(s_out, 64)

        @block.gpsimd
        def _(pool):
            def rsqrt(out, in_, n):
                return nc.gpsimd.tensor_tensor(out, in_, mhalf[:, 0:n], ALU.pow)

            nc.gpsimd.memset(c_pad[:, :, :], 0.0).then_inc(s_pad, 1)
            nc.gpsimd.memset(mhalf, -0.5).then_inc(s_init, 1)
            nc.gpsimd.memset(ones[:, :], 1.0).then_inc(s_init, 1)
            nc.gpsimd.memset(upad[:, :, :, :], 0.0).then_inc(s_init, 1)
            pool.wait_ge(s_init, 3)
            pool.wait_ge(ssq_ready, 1)
            rsqrt(rms, ssq, 2).then_inc(rms_ready, 1)
            pool.wait_ge(vec_copied, 3)
            for half in range(2):
                for d in range(2):
                    for j in range(2):
                        evacuated(pool, f"{('zf', 'zb')[d]}{half}", j)
                        for hh in range(2):
                            hd = half * 4 + j * 2 + hh
                            c = slice(hd * T, (hd + 1) * T)
                            i = d * H + hd
                            nc.gpsimd.tensor_scalar(fg[:, d, c], fg[:, d, c], oml[:, i:i + 1], lb[:, i:i + 1],
                                                    ALU.mult, ALU.add).then_inc(fk_done, 1)
                            nc.gpsimd.tensor_scalar(qk[:, 2 + d, c], qk[:, 2 + d, c], oml[:, i:i + 1], None,
                                                    ALU.mult).then_inc(fk_done, 1)
            pool.wait_ge(fk_done, 32)
            for level in range(LEVELS):
                m = 1 << level
                if level == 3:
                    pool.wait_ge(cms_done, 1)
                    rsqrt(rms_c, ssq_c, 2).then_inc(crms_done, 1)
                pool.wait_ge(sc_ready, 4 * (level + 2))
                pool.wait_ge(mix_done, level + 1)
                if level:
                    pool.wait_ge(tot_done, level)
                kf, kb = halves(qk[:, 2, :], level), halves(qk[:, 3, :], level)
                tf, tb = halves(fg[:, 0, :], level), halves(fg[:, 1, :], level)
                nb = 16 * P // (2 * m)
                nc.gpsimd.tensor_tensor(kf[:, :, 0, :], kf[:, :, 0, :], tf[:, :, 1, 0:1].broadcast_to([P, nb, m]), ALU.mult).then_inc(k_done, 1)
                nc.gpsimd.tensor_tensor(kb[:, :, 1, :], kb[:, :, 1, :], tb[:, :, 0, 0:1].broadcast_to([P, nb, m]), ALU.mult).then_inc(k_done, 1)
            for g in range(4):
                pool.wait_ge(oms_done, g + 1)
                rsqrt(rms_o[:, 4 * g:4 * g + 4], ssq_o[:, 4 * g:4 * g + 4], 4).then_inc(orms_done, 1)
            pool.wait_ge(ms2_done, 2)
            rsqrt(rms2, ms2, 2).then_inc(rms2_done, 1)
            pool.wait_ge(inv2_done, 1)
            for j in (2, 3):
                nc.gpsimd.tensor_tensor(h_t[:, 2 * j:2 * j + 2, :], x_t[:, 2 * j:2 * j + 2, :], inv2[:, :].unsqueeze(1).broadcast_to([P, 2, T]), ALU.mult).then_inc(x1n_done, 1)
            for j in range(4):
                evacuated(pool, "hr", j)
                s, hf = j // 2, j % 2
                ps = slice(64 * hf, 64 * hf + 64)
                nc.gpsimd.tensor_tensor(h_lo[:, s, :, ps], h_full[:, s, :, ps], h_hi[:, s, :, ps].bitcast(F32), ALU.subtract).then_inc(hr_lo, 1)
            for s in range(NS):
                pool.wait_ge(f_ssq, s + 1)
                rsqrt(rmsf[:, s:s + 1], ssqf[:, s:s + 1], 1).then_inc(f_rms, 1)

        @block.scalar
        def _(act):
            own = Own(act, own_act)

            act.dma_start(consts[:, :], A["consts"]).then_inc(s_cst, 16)
            for x, dst in loads_small[1::2]:
                act.dma_start(dst, x).then_inc(s_rows, 16)

            act.wait_ge(s_x, 32)
            for s in range(NS):
                junk = tmp[:, :, :].rearrange("p a n -> p (a n)")
                if s:
                    own.wait()
                own.mark(nc.scalar.activation(junk, x_tok[:, s, :], ACT.Square, accum_out=ssq[:, s:s + 1]))
            act.wait_ge(vec_copied, 1)
            nc.scalar.activation(csig, vec[:, R_C:R_C + 16], ACT.Sigmoid).then_inc(c_sig, 1)

            def copy_partial(j):
                act.wait_ge(part_ready, j + 1)
                if j >= 2:
                    act.wait_ge(mod_ready, j - 1)
                nc.scalar.activation(tmp[:, j % 2, :], bank[4 + j % 2][:, :], ACT.Copy).then_inc(part_copied, 1)

            for j in range(4):
                filled(act, f"xt{j}")
                nc.scalar.activation(x_t[:, 2 * j:2 * j + 2, :].rearrange("p k t -> p (k t)"), fill_bank(f"xt{j}")[:, :],
                                     ACT.Copy).then_inc(act_evac, 1)

            own.wait()
            for j in range(4):
                copy_partial(j)
            act.wait_ge(s_init, 3)
            for j in range(4):
                evacuated(act, f"h{j}")
                nc.scalar.activation(h1_hi[:, 2 * j:2 * j + 2, :], h_t[:, 2 * j:2 * j + 2, :], ACT.Copy).then_inc(h1_hi_done, 1)

            def split_hi(n, quarters):
                loaded(act, split[n])
                for q in quarters:
                    if n not in (0, apart):
                        if q % 2:
                            filled(act, split[n - 1], q // 2)
                        else:
                            act.wait_ge(w_used, 2 * n - 1 + q // 2)
                    nc.scalar.activation(part_hi(n, q), tile_of(split[n])[:, :, q * P:(q + 1) * P], ACT.Copy).then_inc(w_hi_done, 1)

            for j in range(2):
                filled(act, "u1", j)
                for c in range(2):
                    ins = nc.scalar.activation(upad[:, 2 * j + c, :, PAD:PAD + P],
                                               fill_bank("u1", j)[:, c * T:(c + 1) * T].rearrange("p (s t) -> p s t", s=NS), ACT.Copy)
                ins.then_inc(act_evac, 1)
                split_hi(0, (2 * j, 2 * j + 1))
            copy_partial(ada_after["u1"])
            act.wait_ge(mod_ready, ada_after["u1"] + 1)
            for j in range(2):
                filled(act, "u2", j)
                nc.scalar.activation(tmp[:, j, :], fill_bank("u2", j)[:, :], ACT.Sigmoid).then_inc(act_evac, 1)
                split_hi(1, (2 * j, 2 * j + 1))
            act.wait_ge(u_gated, 2)
            copy_partial(ada_after["u2"])

            def heads(arr, half, j):
                h0 = (half * 4 + j * 2) * T
                return arr[:, h0:h0 + 2 * T]

            for half in range(2):
                for j in range(2):
                    filled(act, f"q{half}", j)
                    nc.scalar.activation(heads(qk[:, 1, :], half, j), fill_bank(f"q{half}", j)[:, :], ACT.Copy).then_inc(act_evac, 1)
                    split_hi(split.index(f"q{half}") + 1, (2 * j, 2 * j + 1))
                copy_partial(ada_after[f"q{half}"])
                for d, z in enumerate(("zf", "zb")):
                    for j in range(2):
                        filled(act, f"{z}{half}", j)
                        src = fill_bank(f"{z}{half}", j)[:, :]
                        nc.scalar.activation(heads(fg[:, d, :], half, j), src, ACT.Sigmoid)
                        nc.scalar.activation(heads(qk[:, 2 + d, :], half, j), src, ACT.Sigmoid, scale=-1.0).then_inc(act_evac, 1)
                        if split.index(f"{z}{half}") + 1 < apart:
                            split_hi(split.index(f"{z}{half}") + 1, (2 * j, 2 * j + 1))
                    copy_partial(ada_after[f"{z}{half}"])
            def mix_keys(level):
                if level:
                    act.wait_ge(k_done, 2 * level)
                    act.wait_ge(sc_ready, 4 * (level + 1))
                else:
                    act.wait_ge(fk_done, 32)
                dst = halves(k_mix[:, :], level)
                nc.scalar.activation(dst[:, :, 0, :], halves(qk[:, 2, :], level)[:, :, 0, :], ACT.Copy)
                nc.scalar.activation(dst[:, :, 1, :], halves(qk[:, 3, :], level)[:, :, 1, :], ACT.Copy).then_inc(mix_done, 1)

            for half in range(2):
                for s in range(NS):
                    filled(act, f"v{half}", s)
                    nc.scalar.activation(v_tok[:, s, half * 512:(half + 1) * 512], fill_bank(f"v{half}", s)[:, :], ACT.Copy).then_inc(act_evac, 1)
                    if half == 1 and s == 0:
                        mix_keys(0)
                        act.wait_ge(part_ready, 12)
                        split_hi(apart, range(4))
            upad_row = upad[:, :, :, :].rearrange("p c s u -> p (c s u)")
            act.wait_ge(cen_done, CC)
            nc.scalar.activation(upad_row[:, 0:CC * T], conv[:, :, :].rearrange("p c t -> p (c t)"), ACT.Square).then_inc(csq_done, 1)
            for half in range(2):
                for j in range(2):
                    n = half * 2 + j
                    filled(act, f"og{half}", j)
                    if n < 2:
                        act.wait_ge(mod_ready, 12)
                    else:
                        evacuated(act, f"og{(n - 2) // 2}", n % 2)
                    nc.scalar.activation(tmp[:, n % 2, :], fill_bank(f"og{half}", j)[:, :], ACT.Sigmoid).then_inc(og_sig, 1)
                    if j == 0:
                        mix_keys(1 + half)
                    split_hi(apart + 1 + half, (3,) if j else (0, 1, 2))
            for name, dst in (("ga", ga), ("gb", gb)):
                for half in range(2):
                    for j in range(2):
                        filled(act, f"{name}{half}", j)
                        h0 = half * 4 + j * 2
                        nc.scalar.activation(dst[:, h0:h0 + 2, :].rearrange("p h t -> p (h t)"), fill_bank(f"{name}{half}", j)[:, :],
                                             ACT.Sigmoid).then_inc(act_evac, 1)
                        if j == 0:
                            mix_keys(3 + 2 * (name == "gb") + half)
                        if f"{name}{half}" != split[-1]:
                            split_hi(split.index(f"{name}{half}") + 1, (3,) if j else (0, 1, 2))
                    if name == "gb" and half == 0:
                        act.wait_ge(cn_done, CC)
                        for c in range(CC):
                            nc.scalar.activation(upad_row[:, c * T:(c + 1) * T], conv[:, c, :], ACT.Sigmoid).then_inc(cs_done, 1)
            act.wait_ge(cb_ready, 1)
            def o_and_squares(g):
                act.wait_ge(o_ready, g + 1)
                src = bank[4 + g % 2][:, :]
                nc.scalar.activation(o_t[:, 2 * g:2 * g + 2, :].rearrange("p h t -> p (h t)"), src, ACT.Copy)
                if g >= 2:
                    act.wait_ge(ob_ready, g - 1)
                nc.scalar.activation(tmp[:, g % 2, :], src, ACT.Square).then_inc(o_copied, 1)

            def four_heads(name, dst, j):
                filled(act, name, j)
                nc.scalar.activation(dst[:, 4 * j:4 * j + 4, :].rearrange("p a b -> p (a b)"), fill_bank(name, j)[:, :], ACT.Copy).then_inc(act_evac, 1)

            act.wait_ge(tot_done, LEVELS)
            act.wait_ge(k_done, 2 * LEVELS)
            act.wait_ge(q_done, 2 * (LEVELS + 1))
            o_and_squares(0)
            o_and_squares(1)
            four_heads("kt", k_tok, 0)
            four_heads("kt", k_tok, 1)
            o_and_squares(2)
            four_heads("kt", k_tok, 2)
            o_and_squares(3)
            four_heads("kt", k_tok, 3)
            for j in range(4):
                four_heads("st", s_new, j)
            act.wait_ge(ob_ready, 4)
            for j in range(4):
                evacuated(act, f"wo{j // 2}", j % 2)
                if j >= 2:
                    act.wait_ge(ssq2_ready, j - 1)
                nc.scalar.activation(tmp[:, j % 2, :], x_t[:, 2 * j:2 * j + 2, :].rearrange("p k t -> p (k t)"), ACT.Square).then_inc(x1_sq, 1)
            for name, dst in (("t1", x1), ("g2", g2row)):
                if name == "g2":
                    act.wait_ge(spread2, 1)
                    nc.scalar.activation(inv2[:, :], bank[5][:, 0:T], ACT.Copy).then_inc(inv2_done, 1)
                for s in range(NS):
                    for hf in range(2):
                        filled(act, name, 2 * s + hf)
                        nc.scalar.activation(dst[:, s, hf * 512:(hf + 1) * 512], fill_bank(name, 2 * s + hf)[:, :], ACT.Copy).then_inc(act_evac, 1)
            act.wait_ge(lg_ready, 1)
            act.wait_ge(s_state, 16)
            nc.scalar.activation(rt[:, 0:NS * NE], bank[4][:, 0:NS * NE], ACT.Sigmoid).then_inc(lg_sig, 1)
            for j in range(4):
                filled(act, "hr", j)
                s, hf = j // 2, j % 2
                src = fill_bank("hr", j)[:, :].rearrange("t (p k) -> t p k", k=KD)
                ps = slice(64 * hf, 64 * hf + 64)
                nc.scalar.activation(h_hi[:, s, :, ps].rearrange("t k p -> t p k"), src, ACT.Copy)
                nc.scalar.activation(h_full[:, s, :, ps].rearrange("t k p -> t p k"), src, ACT.Copy).then_inc(act_evac, 1)
            filled(act, "sg", 0)
            nc.scalar.activation(sil_s[:, :, :].rearrange("p c t -> p (c t)"), fill_bank("sg")[:, :], ACT.Silu).then_inc(act_evac, 1)
            def gathered(part, n):
                act.wait_ge(ga_ready, n)
                nc.scalar.activation(xg[:, 2 * part:2 * part + 2, :].rearrange("p k n -> p (k n)"), bank[0][:, :], ACT.Copy).then_inc(ga_evac, 1)

            gathered(0, 1)
            gathered(2, 2)

            def pair(b, i, more):
                p = i * 2 + b
                act.wait_ge(gu_ready, p + 1)
                nc.scalar.activation(sil[:, :], bank[2 + b][:, 0:FF], ACT.Silu).then_inc(sil_ready, 1)
                act.wait_ge(t_ready, p + 1)
                nc.scalar.activation(act_t[:, :, :].rearrange("p c n -> p (c n)"), bank[2 + b][:, 0:2 * P], ACT.Copy).then_inc(t_evac, 1)
                if b:
                    with act.If(more):
                        gathered(0, i * 2 + 3)
                        gathered(2, i * 2 + 4)
                for h in range(2):
                    act.wait_ge(dn_ready, p * 2 + (h + 1))
                    nc.scalar.activation(y_hi[h][:, :], bank[(3 - b, 2 + b)[h]][:, :], ACT.Copy).then_inc(hi_ready, 1)

            loop(act, pair)
            for s in range(NS):
                act.wait_ge(x2_done, s + 1)
                nc.scalar.activation(fin_sq[:, s, :], fin[:, s, :], ACT.Square, accum_out=ssqf[:, s:s + 1]).then_inc(sqf_done, 1)

        @block.vector
        def _(dve):
            own = Own(dve, own_dve)
            V = nc.vector

            dve.wait_ge(vec_ready, 1)
            V.tensor_copy(vec[:, 0:R_ALL], bank[7][:, 0:R_ALL]).then_inc(vec_copied, 1)
            V.tensor_copy(dw[:, :, :].rearrange("p w c -> p (w c)"), bank[7][:, P:P + CW * CC]).then_inc(vec_copied, 1)
            dve.wait_ge(vec_copied, 2)
            own.step(V.tensor_tensor(oml, vec[:, R_LB:R_LB + 16], vec[:, R_LB:R_LB + 16], ALU.subtract))
            own.step(V.tensor_scalar(oml, oml, 1.0, None, ALU.add))
            own.step(V.tensor_tensor(lb, oml, oml, ALU.subtract))
            V.tensor_scalar(oml, lb, -1.0, 1.0, ALU.mult, ALU.add).then_inc(vec_copied, 1)
            dve.wait_ge(c_sig, 1)
            dve.wait_ge(s_pad, 1)
            V.tensor_tensor(c_pad[:, :, 0:NS].rearrange("p k s -> p s k"), csig.rearrange("p (s k) -> p s k", s=NS),
                            vec[:, R_C:R_C + 16].rearrange("p (s k) -> p s k", s=NS), ALU.mult).then_inc(c_silu, 1)
            dve.wait_ge(own_act, 2)
            V.tensor_scalar(ssq, ssq, 1.0 / D, EPS, ALU.mult, ALU.add).then_inc(ssq_ready, 1)
            dve.wait_ge(rms_ready, 1)
            for s in range(NS):
                V.tensor_scalar(xn[:, s, :], x_tok[:, s, :], rms[:, s:s + 1], None, ALU.mult).then_inc(xn_done, 1)

            def modulation(j0, j1, ready):
                dve.wait_ge(mod_ready, ready)
                for s in range(NS):
                    last = V.tensor_tensor(mod_v[:, j0:j1, s], bank[7][:, 256 + 2 * j0:256 + 2 * j1].rearrange("p (j s) -> p j s", s=NS)[:, :, s],
                                           vec[:, R_BADA + j0:R_BADA + j1], ALU.add)
                    last.then_inc(mod_done, 1)
                dve.wait_ge(mod_done, 2 if j0 == 0 else 4)

            def gains(dst, scale, gain):
                g = dst.rearrange("p (k s) -> p k s", s=NS)
                for s in range(NS):
                    own.step(V.scalar_tensor_tensor(g[:, :, s], mod_v[:, scale:scale + 8, s], 1.0, vec[:, gain:gain + 8], ALU.add, ALU.mult))

            modulation(0, 16, 4)
            gains(gain1, M_SC1, R_G1)
            for j in range(4):
                filled(dve, f"h{j}")
                for kk in range(2):
                    for s in range(NS):
                        k = 2 * j + kk
                        src = fill_bank(f"h{j}")[:, kk * T + s * P:kk * T + (s + 1) * P]
                        ins = V.tensor_scalar(h_t[:, k, s * P:(s + 1) * P], src, gain1[:, 2 * k + s:2 * k + s + 1],
                                              mod_v[:, M_SH1 + k, s:s + 1], ALU.mult, ALU.add)
                ins.then_inc(dve_evac, 1)

            for j in range(4):
                dve.wait_ge(h1_hi_done, j + 1)
                c = slice(2 * j, 2 * j + 2)
                V.tensor_tensor(h1_lo[:, c, :], h_t[:, c, :], h1_hi[:, c, :].bitcast(F32), ALU.subtract).then_inc(h1_lo_done, 1)

            def split_lo(n, quarters):
                for q in quarters:
                    dve.wait_ge(w_hi_done, 4 * n + q + 1)
                    V.tensor_tensor(part_lo(n, q), tile_of(split[n])[:, :, q * P:(q + 1) * P], part_hi(n, q).bitcast(F32), ALU.subtract).then_inc(w_lo_done, 1)

            split_lo(0, range(4))
            for j in range(2):
                split_lo(1, (2 * j, 2 * j + 1))
                evacuated(dve, "u2", j)
                sg = tmp[:, j, :].rearrange("p (c s t) -> p c s t", c=2, s=NS)
                for c in range(2):
                    uu = upad[:, 2 * j + c, :, PAD:PAD + P]
                    ins = V.tensor_tensor(uu, uu, sg[:, c], ALU.mult)
                ins.then_inc(u_gated, 1)
            dve.wait_ge(u_gated, 2)
            marks = []
            parts = [(n, (2 * j, 2 * j + 1)) for n in range(2, apart) for j in range(2)]
            before_tap = {(5 * n + 1) // 2: part for n, part in enumerate(parts)}
            for w in range(CW):
                if w in before_tap:
                    split_lo(*before_tap[w])
                for c in range(CC):
                    dst = conv[:, c, :].rearrange("p (s t) -> p s t", s=NS)
                    src = upad[:, c, :, w:w + P]
                    tap = dw[:, w, c:c + 1]
                    if w == 0:
                        ins = V.tensor_scalar(dst, src, tap, vec[:, R_DWB + c:R_DWB + c + 1], ALU.mult, ALU.add)
                    else:
                        own.wait(marks[CC * (w - 1) + c])
                        ins = V.scalar_tensor_tensor(dst, src, tap, dst, ALU.mult, ALU.add)
                    if w < CW - 1:
                        marks.append(own.mark(ins))
                    else:
                        ins.then_inc(conv_done, 1)

            mask_of = [consts[:, C_MASK + P * lv:C_MASK + P * (lv + 1)].unsqueeze(1).broadcast_to([P, 4, P]) for lv in range(LEVELS)]
            dve.wait_ge(s_cst, 16)

            def score_tiles(level, groups=range(4)):
                for g in groups:
                    n = 4 * (level + 1) + g
                    dve.wait_ge(sc_ready, n + 1)
                    src = bank[4 + n % 2][:, :].rearrange("p (a t) -> p a t", a=4)
                    dst = att[:, 4 * g:4 * g + 4, :]
                    if level < 0:
                        V.tensor_tensor(dst, src, ident.unsqueeze(1).broadcast_to([P, 4, P]), ALU.mult).then_inc(sc_used, 1)
                    else:
                        V.copy_predicated(dst, mask_of[level].bitcast(U32), src).then_inc(sc_used, 1)

            score_tiles(-1)
            dve.wait_ge(fk_done, 32)
            for d in (1, 0):
                V.tensor_tensor(qk[:, 1 - d, :], qk[:, 1, :], fg[:, d, :], ALU.mult).then_inc(q_done, 1)
            dve.wait_ge(q_done, 2)

            dve.wait_ge(mean_ready, 1)
            for c in range(CC):
                V.scalar_tensor_tensor(conv[:, c, :], bank[6][:, 0:T], -1.0 / (CC * P), conv[:, c, :], ALU.mult, ALU.add).then_inc(cen_done, 1)

            def og_gate(half):
                for j in range(2):
                    n = half * 2 + j
                    dve.wait_ge(og_sig, n + 1)
                    for hh in range(2):
                        hd = half * 4 + j * 2 + hh
                        ins = V.scalar_tensor_tensor(og[:, hd, :], fill_bank(f"og{half}", j)[:, hh * T:(hh + 1) * T], vec[:, R_HG + hd:R_HG + hd + 1],
                                                     tmp[:, n % 2, hh * T:(hh + 1) * T], ALU.mult, ALU.mult)
                    ins.then_inc(dve_evac, 1)

            modulation(16, 48, 12)
            gains(gain2, M_SC2, R_G2)
            for level in range(LEVELS):
                m = 1 << level
                n_split = apart + level
                if n_split < len(split):
                    split_lo(n_split, (0, 1))
                score_tiles(level, (0, 1))
                if n_split < len(split):
                    split_lo(n_split, (2,))
                if level == 0:
                    filled(dve, "v1", 1)
                    for j in range(4):
                        c = slice(2 * j, 2 * j + 2)
                        V.tensor_tensor(h1_rest[:, c, :], h_t[:, c, :], h1_hi[:, c, :].bitcast(F32), ALU.subtract).then_inc(h1_rest_done, 1)
                score_tiles(level, (2, 3))
                nb = 16 * P // (2 * m)
                qb, qf = halves(qk[:, 0, :], level), halves(qk[:, 1, :], level)
                tf, tb = halves(fg[:, 0, :], level), halves(fg[:, 1, :], level)
                if level:
                    dve.wait_ge(tot_done, level)
                V.tensor_tensor(qf[:, :, 1, :], qf[:, :, 1, :], tf[:, :, 0, 0:1].broadcast_to([P, nb, m]), ALU.mult).then_inc(q_done, 1)
                V.tensor_tensor(qb[:, :, 0, :], qb[:, :, 0, :], tb[:, :, 1, 0:1].broadcast_to([P, nb, m]), ALU.mult).then_inc(q_done, 1)
                dve.wait_ge(q_done, 2 * (level + 2))
                dve.wait_ge(k_done, 2 * (level + 1))
                tot = fg[:, :, :].rearrange("p d (n h m) -> p d n h m", h=2, m=m)[:, :, :, :, 0]
                V.tensor_tensor(tot[:, :, :, 0], tot[:, :, :, 0], tot[:, :, :, 1], ALU.mult).then_inc(tot_done, 1)
                if n_split < len(split):
                    split_lo(n_split, (3,))
                if level in (1, 2):
                    og_gate(level - 1)
                if level == 2:
                    dve.wait_ge(cvar_ready, 1)
                    V.tensor_scalar(ssq_c, bank[6][:, 256:258], 1.0 / (CC * P), EPS, ALU.mult, ALU.add).then_inc(cms_done, 1)
                if level == 3:
                    dve.wait_ge(crms_done, 1)
                    diag = tmp[:, 0, 0:T]
                    for s in range(NS):
                        V.tensor_scalar(diag[:, s * P:(s + 1) * P], ident, rms_c[:, s:s + 1], None, ALU.mult).then_inc(cdiag_done, 1)
                if level == 4:
                    dve.wait_ge(cb_ready, 1)
                    for c in range(CC):
                        own.mark(V.tensor_tensor(conv[:, c, :], conv[:, c, :], bank[6][:, 0:T], ALU.mult))
                    own.wait()
                    for c in range(CC):
                        V.tensor_scalar(conv[:, c, :], conv[:, c, :], vec[:, R_CNG + c:R_CNG + c + 1], vec[:, R_CNB + c:R_CNB + c + 1],
                                        ALU.mult, ALU.add).then_inc(cn_done, 1)
                if level == 5:
                    dve.wait_ge(cn_done, CC)
                    dve.wait_ge(cs_done, CC)
                    for c in range(CC):
                        V.tensor_tensor(conv[:, c, :], conv[:, c, :], upad[:, :, :, :].rearrange("p c s u -> p (c s u)")[:, c * T:(c + 1) * T],
                                        ALU.mult).then_inc(cact_done, 1)

            def branch(key, arr, j):
                filled(dve, *key)
                dd = arr[:, 2 * j:2 * j + 2, :].rearrange("p h t -> p (h t)")
                V.tensor_tensor(dd, dd, fill_bank(*key)[:, :], ALU.mult).then_inc(dve_evac, 1)

            evacuated(dve, "gb1", 1)
            for j in range(4):
                branch(("pc", j), gb, j)

            def normed(g):
                dve.wait_ge(ob_ready, g + 1)
                oo = o_t[:, 2 * g:2 * g + 2, :].rearrange("p h t -> p (h t)")
                own.step(V.tensor_tensor(oo, oo, bank[6][:, :], ALU.mult))
                V.tensor_tensor(oo, oo, og[:, 2 * g:2 * g + 2, :].rearrange("p h t -> p (h t)"), ALU.mult).then_inc(ob_used, 1)

            for g in range(4):
                dve.wait_ge(osq_ready, g + 1)
                V.tensor_scalar(ssq_o[:, 4 * g:4 * g + 4], bank[7][:, 384 + 4 * g:388 + 4 * g], 1.0 / P, EPS, ALU.mult, ALU.add).then_inc(oms_done, 1)
                if g:
                    normed(g - 1)
                dve.wait_ge(orms_done, g + 1)
                for i in range(4):
                    ins = V.tensor_scalar(tmp[:, g % 2, i * P:(i + 1) * P], ident, rms_o[:, 4 * g + i:4 * g + i + 1], None, ALU.mult)
                ins.then_inc(odiag_done, 1)
            normed(3)

            for j in range(4):
                key = (f"ph{j // 2}", j % 2)
                branch(key, ga, j)
                evacuated(dve, *key)
                dd = ga[:, 2 * j:2 * j + 2, :].rearrange("p h t -> p (h t)")
                V.tensor_tensor(dd, dd, gb[:, 2 * j:2 * j + 2, :].rearrange("p h t -> p (h t)"), ALU.add).then_inc(merged, 1)
            for j in range(4):
                key = (f"wo{j // 2}", j % 2)
                filled(dve, *key)
                for kk in range(2):
                    for s in range(NS):
                        k = 2 * j + kk
                        dst = x_t[:, k, s * P:(s + 1) * P]
                        ins = V.scalar_tensor_tensor(dst, fill_bank(*key)[:, kk * T + s * P:kk * T + (s + 1) * P], mod_v[:, M_GT1 + k, s:s + 1], dst, ALU.mult, ALU.add)
                ins.then_inc(dve_evac, 1)
            dve.wait_ge(ssq2_ready, 4)
            for s in range(NS):
                V.tensor_scalar(ms2[:, s:s + 1], bank[4 + s][:, 0:1], 1.0 / D, EPS, ALU.mult, ALU.add).then_inc(ms2_done, 1)
            dve.wait_ge(rms2_done, 1)
            for s in range(NS):
                V.tensor_scalar(diag2[:, s * P:(s + 1) * P], ident, rms2[:, s:s + 1], None, ALU.mult).then_inc(diag2_done, 1)
            dve.wait_ge(inv2_done, 1)
            for j in range(2):
                own.mark(V.tensor_tensor(h_t[:, 2 * j:2 * j + 2, :], x_t[:, 2 * j:2 * j + 2, :], inv2[:, :].unsqueeze(1).broadcast_to([P, 2, T]), ALU.mult))
            own.wait()
            for j in range(4):
                if j >= 2:
                    dve.wait_ge(x1n_done, j - 1)
                for kk in range(2):
                    for s in range(NS):
                        k = 2 * j + kk
                        hh = h_t[:, k, s * P:(s + 1) * P]
                        ins = V.tensor_scalar(hh, hh, gain2[:, 2 * k + s:2 * k + s + 1], mod_v[:, M_SH2 + k, s:s + 1], ALU.mult, ALU.add)
                ins.then_inc(h2_done, 1)

            iota4 = consts[:, C_IOTA:C_IOTA + C].unsqueeze(1).broadcast_to([P, 4, C])

            def one_hots(i4):
                for s in range(NS):
                    V.tensor_tensor(sel_p[:, s, :].rearrange("t (e j) -> t e j", e=4), iota4,
                                    pos_i[:, s, bass.ds(i4, 4)].unsqueeze(2).broadcast_to([P, 4, C]), ALU.is_equal)
                V.tensor_copy(comb_p[:, :, :], comb_i[:, :, bass.ds(i4, 4)]).then_inc(built, 1)

            dve.wait_ge(s_state, 16)
            own.mark(V.memset(selm, -BIG))
            own.mark(V.memset(neg, -1.0))
            own.mark(V.memset(pos_i[:, :, NI:NI + 4], -1.0))
            own.mark(V.memset(comb_i[:, :, NI:NI + 4], 0.0))
            own.mark(V.memset(e_row[:, :], 0))
            dve.wait_ge(lg_sig, 1)
            dve.wait_ge(s_rows, 16 * 12)
            for s in range(NS):
                own.mark(V.tensor_tensor(sel[:, s, :], score[:, s, :], b_router[:, :], ALU.add))
            own.wait()
            for s in range(NS):
                for g in range(8):
                    own.mark(V.max(top[:, s, g, :], sel[:, s, 8 * g:8 * g + 8]))
            own.wait()
            own.step(V.tensor_tensor(grp, top[:, :, :, 0], top[:, :, :, 1], ALU.add))
            for s in range(NS):
                other = grp[:, s, :].unsqueeze(1).broadcast_to([P, 8, 8])
                mine = grp[:, s, :].unsqueeze(2).broadcast_to([P, 8, 8])
                own.mark(V.tensor_tensor(cmp[:, s], other, mine, ALU.is_gt))
                own.step(V.tensor_tensor(ceq[:, s], other, mine, ALU.is_equal))
                own.step(V.tensor_tensor(ceq[:, s], ceq[:, s], consts[:, C_LT:C_LT + 64].rearrange("p (g j) -> p g j", g=8), ALU.mult))
                own.step(V.tensor_tensor(cmp[:, s], cmp[:, s], ceq[:, s], ALU.add))
            own.step(V.tensor_reduce(rank, cmp.rearrange("p s g j -> p (s g) j"), AX, ALU.add))
            own.step(V.tensor_scalar(gmask.rearrange("p s g -> p (s g)"), rank, 4.0, None, ALU.is_lt))
            for s in range(NS):
                own.step(V.copy_predicated(selm[:, s, :].rearrange("p (g j) -> p g j", g=8), gmask[:, s, :].unsqueeze(2).broadcast_to([P, 8, 8]).bitcast(U32),
                                           sel[:, s, :].rearrange("p (g j) -> p g j", g=8)))
                own.step(V.max(best[:, s, :], selm[:, s, :]))
                own.step(V.match_replace(rep[:, s, :], best[:, s, :], selm[:, s, :], BIG))
            V.tensor_tensor(mask, rep, selm, ALU.not_equal).then_inc(lg_mask, 1)
            dve.wait_ge(lg_mask, 1)
            own.step(V.tensor_tensor(comb, score, mask, ALU.mult))
            own.step(V.tensor_reduce(wsum, comb, AX, ALU.add))
            own.step(V.reciprocal(wrec, wsum))
            for s in range(NS):
                own.mark(V.tensor_scalar(comb[:, s, :], comb[:, s, :], wrec[:, s:s + 1], ROUTED_SCALE, ALU.mult, ALU.mult))
            dve.wait_ge(cnt_ready, 1)
            for s in range(NS):
                own.mark(V.scalar_tensor_tensor(posm[:, s, :], bank[5][:, s * NE:(s + 1) * NE], 1.0, mask[:, s, :], ALU.add, ALU.mult))
            for j in range(3):
                V.tensor_scalar(nxt[0:NE, j:j + 1], bank[5][0:NE, 128:129], C * (j + 1.0), None, ALU.is_gt).then_inc(posm_done, 1)
            dve.wait_ge(posm_done, 3)
            own.step(V.tensor_tensor(nxt[0:NE, 0:1], nxt[0:NE, 0:1], nxt[0:NE, 1:2], ALU.add))
            V.tensor_tensor(nxt[0:NE, 3:4], nxt[0:NE, 0:1], nxt[0:NE, 2:3], ALU.add).then_inc(nx_done, 1)
            dve.wait_ge(nx_done, 1)
            dve.wait_ge(end_ready, 1)
            own.step(V.tensor_copy(endx[0:NE, 0:1], bank[5][0:NE, 130:131]))
            own.step(V.tensor_tensor(endx[0:NE, 1:2], endx[0:NE, 0:1], nxt[0:NE, 3:4], ALU.subtract))
            own.mark(V.tensor_scalar(hot[0:NE, :], iota_x, endx[0:NE, 0:1], None, ALU.is_ge))
            own.mark(V.tensor_scalar(hot2[0:NE, :], iota_x, endx[0:NE, 1:2], None, ALU.is_ge))
            own.step(V.tensor_scalar(hotb[0:NE, :], iota_x, endx[0:NE, 1:2], 1.0, ALU.subtract, ALU.add))
            own.step(V.tensor_tensor(hot[0:NE, :], hot2[0:NE, :], hot[0:NE, :], ALU.subtract))
            V.scalar_tensor_tensor(hotb[0:NE, :], hotb[0:NE, :], float(C), hot[0:NE, :], ALU.mult, ALU.mult).then_inc(oh_done, 1)
            for s in range(NS):
                own.mark(V.tensor_scalar(pos_i[:, s, 0:NE], posm[:, s, :], 1.0, None, ALU.subtract))
                own.mark(V.tensor_copy(comb_i[:, s, 0:NE], comb[:, s, :]))
            own.wait()
            one_hots(0)
            filled(dve, "su")
            evacuated(dve, "sg")
            V.tensor_tensor(act_s[:, :, :].rearrange("p c t -> p (c t)"), sil_s[:, :, :].rearrange("p c t -> p (c t)"), fill_bank("su")[:, :], ALU.mult).then_inc(dve_evac, 1)
            dve.wait_ge(pt1_ready, 1)
            V.tensor_copy(tmp[0:NE, 0, :], bank[6][0:NE, :]).then_inc(pt1_copied, 1)
            dve.wait_ge(items_ready, 1)
            own.mark(V.tensor_copy(e_row[0:1, 0:NX], bank[5][0:1, 256:256 + NX]))
            own.mark(V.tensor_scalar(nwork, bank[5][0:1, 296:297], float(NE), None, ALU.add))
            for s in range(NS):
                own.mark(V.tensor_scalar(pos_i[:, s, NE:NI], bank[5][:, 320 + s * NX:320 + (s + 1) * NX], 1.0, None, ALU.subtract))
                V.tensor_copy(comb_i[:, s, NE:NI], bank[5][:, 384 + s * NX:384 + (s + 1) * NX]).then_inc(items_done, 1)

            def transposed(b, p1):
                dve.wait_ge(pt_ready, p1)
                V.tensor_copy(sel_t[b][:, :], bank[0][:, 0:T])
                V.tensor_copy(w_slot[b][0:C, :], bank[0][0:C, T:T + 1])
                V.tensor_copy(w_slot[b][C:P, :], bank[0][C:P, T + 1:T + 2]).then_inc(pt_evac, 1)

            def gathered(part, n):
                dve.wait_ge(gbk_ready, n)
                V.tensor_copy(xg[:, 2 * part:2 * part + 2, :].rearrange("p k n -> p (k n)"), bank[1][:, :]).then_inc(gbk_evac, 1)

            gathered(1, 1)
            gathered(3, 2)
            transposed(0, 1)

            def pair(b, i, more):
                p = i * 2 + b
                dve.wait_ge(sil_ready, p + 1)
                dve.wait_ge(pt_evac, p + 1)
                V.scalar_tensor_tensor(act_r[:, :], bank[2 + b][:, FF:2 * FF], w_slot[b][:, 0:1], sil[:, :], ALU.mult, ALU.mult).then_inc(act_ready, 1)
                if b:
                    with dve.If(more):
                        gathered(1, i * 2 + 3)
                        gathered(3, i * 2 + 4)
                        transposed(0, i * 2 + 3)
                else:
                    transposed(1, i * 2 + 2)
                    one_hots(i * 4 + 4)
                for h in range(2):
                    dve.wait_ge(hi_ready, p * 2 + (h + 1))
                    V.tensor_tensor(y_lo[h][:, :], bank[(3 - b, 2 + b)[h]][:, :], y_hi[h][:, :].bitcast(F32), ALU.subtract).then_inc(y_ready, 1)

            loop(dve, pair)
            V.memset(small[:, 179:180], 0.0).then_inc(loop_done, 1)

            dve.wait_ge(s_fing, 16)
            def gated_y(s):
                dve.wait_ge(y_done, s + 1)
                for hf in range(2):
                    c = slice(hf * 512, (hf + 1) * 512)
                    own.mark(V.tensor_tensor(fin[:, s, c], g2row[:, s, c], y_acc[s][hf][:, :], ALU.mult))

            def residual(s):
                own.wait()
                V.tensor_tensor(fin[:, s, :], fin[:, s, :], x1[:, s, :], ALU.add).then_inc(x2_done, 1)

            def mean_square(s):
                dve.wait_ge(sqf_done, s + 1)
                V.tensor_scalar(ssqf[:, s:s + 1], ssqf[:, s:s + 1], 1.0 / D, EPS, ALU.mult, ALU.add).then_inc(f_ssq, 1)

            def final_norm(s):
                dve.wait_ge(f_rms, s + 1)
                for hf in range(2):
                    c = slice(hf * 512, (hf + 1) * 512)
                    V.scalar_tensor_tensor(fin[:, s, c], fin[:, s, c], rmsf[:, s:s + 1], fin_g[:, c], ALU.mult, ALU.mult).then_inc(out_done, 1)

            gated_y(0)
            residual(0)
            gated_y(1)
            mean_square(0)
            residual(1)
            final_norm(0)
            mean_square(1)
            final_norm(1)

        @block.tensor
        def _(pe):
            mm = nc.tensor.matmul

            def arrived(name):
                loaded(pe, name)

            def open_fill(name, j=0):
                n = fill_no[name, j]
                if n >= 4:
                    pe.wait_ge(fills[n - 4][2], fills[n - 4][3])
                return bank[n % 4]

            pe.wait_ge(s_cst, 16)
            pe.wait_ge(s_rows, 16 * 12)
            nc.tensor.transpose(bank[7][:, 0:R_ALL], rows[0:R_ALL, :], ident[0:R_ALL, 0:R_ALL])
            nc.tensor.transpose(bank[7][:, P:P + CW * CC], rows_dw[0:CW * CC, :], ident[0:CW * CC, 0:CW * CC]).then_inc(vec_ready, 1)
            pe.wait_ge(s_x, 32)

            def to_channels(name, src, j):
                b = open_fill(*name)
                for kk in range(2):
                    for s in range(NS):
                        k = 2 * j + kk
                        ins = nc.tensor.transpose(b[:, kk * T + s * P:kk * T + (s + 1) * P], src[:, s, k * P:(k + 1) * P], ident)
                return ins

            for j in range(4):
                to_channels((f"xt{j}", 0), x_tok, j).then_inc(proj_ready, 1)

            def ada_partial(j):
                arrived(f"ada{j}")
                if j >= 2:
                    pe.wait_ge(part_copied, j - 1)
                w = tile_of(f"ada{j}")
                for k in range(KD):
                    g = k % 4
                    ins = mm(bank[4 + j % 2][32 * g:32 * g + 32, :], c_pad[:, k, :], w[:, k, :], start=(k < 4), stop=(k >= 4))
                ins.then_inc(part_ready, 1)

            def ada_sum(j):
                pe.wait_ge(part_copied, j + 1)
                for c in range(4):
                    col = 256 + 2 * (4 * j + c)
                    ins = mm(bank[7][:, col:col + 2], tmp[:, j % 2, c * P:(c + 1) * P], consts[:, C_SUM:C_SUM + NS], start=True, stop=True)
                ins.then_inc(mod_ready, 1)

            pe.wait_ge(vec_copied, 2)
            pe.wait_ge(c_silu, 1)
            for j in range(4):
                ada_partial(j)
                ada_sum(j)
                if j == 0:
                    pe.wait_ge(xn_done, 2)
                to_channels((f"h{j}", 0), xn, j).then_inc(proj_ready, 1)

            def project(name, rhs, kk=KD, n=2, before_k=None):
                arrived(name)
                w = tile_of(name)
                for j in range(n):
                    b = open_fill(name, j)
                    for c in range(2):
                        col = (2 * j + c) * P
                        for k in range(kk):
                            if before_k is not None and j == 0 and c == 0:
                                before_k(k)
                            ins = mm(b[:, c * T:(c + 1) * T], w[:, k, col:col + P], rhs[:, k, :], start=(k == 0), stop=(k == kk - 1))
                            if k == kk - 1 and c == 1:
                                ins.then_inc(proj_ready, 1)

            def project_parts(name, q):
                n = split.index(name)
                b = open_fill(name, q // 2) if q % 2 == 0 else fill_bank(name, q // 2)
                out = b[:, (q % 2) * T:(q % 2 + 1) * T]
                pe.wait_ge(w_lo_done, 4 * n + q + 1)
                for k in range(KD):
                    mm(out, part_hi(n, q)[:, k, :], h1_hi[:, k, :], start=(k == 0), stop=False)
                for k in range(KD):
                    mm(out, part_lo(n, q)[:, k, :], h1_hi[:, k, :], start=False, stop=False)
                if n < apart:
                    pe.wait_ge(h1_lo_done, 4)
                else:
                    pe.wait_ge(h1_rest_done, 4)
                for k in range(KD):
                    ins = mm(out, part_hi(n, q)[:, k, :], (h1_lo if n < apart else h1_rest)[:, k, :], start=False, stop=(k == KD - 1))
                ins.then_inc(proj_ready if q % 2 else w_used, 1)

            def quarter(name, q):
                if name in split:
                    project_parts(name, q)
                    return
                w = tile_of(name)
                if q == 0:
                    arrived(name)
                b = open_fill(name, q // 2) if q % 2 == 0 else fill_bank(name, q // 2)
                if name[0] == "v":
                    s = q // 2
                    for k in range(4 * (q % 2), 4 * (q % 2) + 4):
                        ins = mm(b[:, :], h_t[:, k, s * P:(s + 1) * P], w[:, k, :], start=(k == 0), stop=(k == KD - 1))
                else:
                    for k in range(KD):
                        ins = mm(b[:, (q % 2) * T:(q % 2 + 1) * T], w[:, k, q * P:(q + 1) * P], h_t[:, k, :], start=(k == 0), stop=(k == KD - 1))
                if q % 2:
                    ins.then_inc(proj_ready, 1)

            def scores(level, groups):
                for g in groups:
                    n = 4 * (level + 1) + g
                    if n >= 2:
                        pe.wait_ge(sc_used, n - 1)
                    for i in range(4):
                        out, at_ = bank[4 + n % 2][:, i * P:(i + 1) * P], 4 * g + i
                        if level < 0:
                            q = qk[:, 1, at_ * P:(at_ + 1) * P]
                            mm(out, qk[:, 2, at_ * P:(at_ + 1) * P], q, start=True, stop=False)
                            ins = mm(out, qk[:, 3, at_ * P:(at_ + 1) * P], q, start=False, stop=True)
                        else:
                            ins = mm(out, k_mix[:, at_ * P:(at_ + 1) * P], query_mix(level, at_), start=True, stop=True)
                    ins.then_inc(sc_ready, 1)

            pe.wait_ge(mod_done, 2)
            for name in ("u1", "u2", "q0", "zf0", "zb0", "q1", "zf1", "zb1"):
                if name in split:
                    for q in range(4):
                        project_parts(name, q)
                else:
                    project(name, h_t, before_k=(lambda k: evacuated(pe, f"h{k // 2}")) if name == "u1" else None)
                if name in ada_after:
                    if name != "u1":
                        ada_sum(ada_after[name] - 1)
                    ada_partial(ada_after[name])
            for level, name in zip(range(-1, LEVELS), ("v0", "v1", "og0", "og1", "ga0", "ga1", "gb0", "gb1")):
                quarter(name, 0)
                if level == -1:
                    ada_sum(11)
                quarter(name, 1)
                quarter(name, 2)
                if level == -1:
                    pe.wait_ge(fk_done, 32)
                    evacuated(pe, "q1", 1)
                else:
                    pe.wait_ge(q_done, 2 * (level + 1))
                    pe.wait_ge(mix_done, level + 1)
                scores(level, (0, 1))
                quarter(name, 3)
                scores(level, (2, 3))
                if level == -1:
                    pe.wait_ge(conv_done, CC)
                    pe.wait_ge(s_init, 3)
                    for c in range(CC):
                        ins = mm(bank[6][:, 0:T], ones[:, :], conv[:, c, :], start=(c == 0), stop=(c == CC - 1))
                    ins.then_inc(mean_ready, 1)
                if level == 1:
                    pe.wait_ge(csq_done, 1)
                    sq = upad[:, :, :, :].rearrange("p c s u -> p (c s u)")
                    for s in range(NS):
                        for c in range(CC):
                            ins = mm(bank[6][:, 256 + s:257 + s], sq[:, c * T + s * P:c * T + (s + 1) * P], ones[:, 0:1], start=(c == 0), stop=(c == CC - 1))
                    ins.then_inc(cvar_ready, 1)
                if level == 4:
                    pe.wait_ge(cdiag_done, 2)
                    mm(bank[6][:, 0:T], ones[:, :], tmp[:, 0, 0:T], start=True, stop=True).then_inc(cb_ready, 1)
            pe.wait_ge(cact_done, CC)
            project("pc", conv, kk=CC, n=4)
            pe.wait_ge(sc_used, 4 * (LEVELS + 1))
            pe.wait_ge(q_done, 2 * (LEVELS + 1))
            pe.wait_ge(s_s0, 16)
            evacuated(pe, "v1", 1)

            def heads_out(g):
                if g >= 2:
                    pe.wait_ge(o_copied, g - 1)
                for i in range(4):
                    at_ = 4 * g + i
                    h, s = at_ // 2, at_ % 2
                    out = bank[4 + g % 2][:, i * P:(i + 1) * P]
                    ins = mm(out, v_tok[:, s, h * P:(h + 1) * P], att[:, at_, :], start=True, stop=(s == 0))
                    if s:
                        mm(out, s0[:, h, :], qk[:, 1, at_ * P:(at_ + 1) * P], start=False, stop=False)
                        ins = mm(out, s0[:, H + h, :], qk[:, 0, at_ * P:(at_ + 1) * P], start=False, stop=True)
                ins.then_inc(o_ready, 1)

            def squares(g):
                pe.wait_ge(o_copied, g + 1)
                if g == 0:
                    pe.wait_ge(mod_done, 4)
                else:
                    pe.wait_ge(oms_done, g)
                for i in range(4):
                    col = 384 + 4 * g + i
                    ins = mm(bank[7][:, col:col + 1], tmp[:, g % 2, i * P:(i + 1) * P], ones[:, 0:1], start=True, stop=True)
                ins.then_inc(osq_ready, 1)

            def spread(g):
                pe.wait_ge(odiag_done, g + 1)
                if g:
                    pe.wait_ge(ob_used, g)
                mm(bank[6][:, :], ones[:, :], tmp[:, g % 2, :], start=True, stop=True).then_inc(ob_ready, 1)

            def keys_by_token(j):
                b = open_fill("kt", j)
                for i in range(4):
                    d, h = divmod(4 * j + i, H)
                    ins = nc.tensor.transpose(b[:, i * P:(i + 1) * P], qk[:, 2 + d, 2 * h * P:(2 * h + 1) * P], ident)
                ins.then_inc(proj_ready, 1)

            def final_states(j):
                b = open_fill("st", j)
                evacuated(pe, "kt", j)
                for i in range(4):
                    h = (4 * j + i) % H
                    ins = mm(b[:, i * P:(i + 1) * P], k_tok[:, 4 * j + i, :], v_tok[:, 0, h * P:(h + 1) * P], start=True, stop=True)
                ins.then_inc(proj_ready, 1)

            heads_out(0)
            heads_out(1)
            pe.wait_ge(k_done, 2 * LEVELS)
            keys_by_token(0)
            keys_by_token(1)
            squares(0)
            heads_out(2)
            keys_by_token(2)
            squares(1)
            spread(0)
            heads_out(3)
            keys_by_token(3)
            squares(2)
            spread(1)
            final_states(0)
            squares(3)
            spread(2)
            final_states(1)
            final_states(2)
            spread(3)
            final_states(3)
            project("ph0", o_t, before_k=lambda k: pe.wait_ge(ob_used, k // 2 + 1))
            project("ph1", o_t)
            pe.wait_ge(merged, 4)
            project("wo0", ga)

            def sum_squares(j):
                pe.wait_ge(x1_sq, j + 1)
                if j == 0:
                    pe.wait_ge(o_copied, 4)
                for s in range(NS):
                    for c in range(2):
                        ins = mm(bank[4 + s][:, 0:1], tmp[:, j % 2, c * T + s * P:c * T + (s + 1) * P], ones[:, 0:1], start=(j == 0 and c == 0), stop=(j == 3 and c == 1))
                ins.then_inc(ssq2_ready, 1)

            def to_tokens(name, src, j):
                s, hf = j // 2, j % 2
                b = open_fill(name, j)
                for i in range(4):
                    ins = nc.tensor.transpose(b[:, i * P:(i + 1) * P], src[:, 4 * hf + i, s * P:(s + 1) * P], ident)
                ins.then_inc(proj_ready, 1)

            sum_squares(0)
            project("wo1", ga)
            sum_squares(1)
            sum_squares(2)
            to_tokens("t1", x_t, 0)
            sum_squares(3)
            for j in range(1, 4):
                to_tokens("t1", x_t, j)
            pe.wait_ge(diag2_done, 2)
            mm(bank[5][:, 0:T], ones[:, :], diag2[:, :], start=True, stop=True).then_inc(spread2, 1)
            for j in range(4):
                s, hf = j // 2, j % 2
                b = open_fill("g2", j)
                for i in range(4):
                    ins = mm(b[:, i * P:(i + 1) * P], mod_v[:, M_GT2 + 4 * hf + i, s:s + 1].broadcast_to([P, P]), ident, start=True, stop=True)
                ins.then_inc(proj_ready, 1)
            pe.wait_ge(s_wr, 16)
            pe.wait_ge(ms2_done, 2)
            for s in range(NS):
                for k in range(KD):
                    if s == 0 and k % 2 == 0:
                        pe.wait_ge(h2_done, k // 2 + 1)
                    ins = mm(bank[4][:, s * NE:(s + 1) * NE], h_t[:, k, s * P:(s + 1) * P], w_r[:, k, :], start=(k == 0), stop=(k == KD - 1))
            ins.then_inc(lg_ready, 1)
            for j in range(4):
                to_tokens("hr", h_t, j)

            def shared_up(name, c):
                b = open_fill(name) if c == 0 else fill_bank(name)
                col = (0 if name == "sg" else FF) + c * P
                for k in range(KD):
                    ins = mm(b[:, c * T:(c + 1) * T], w_sg[:, k, col:col + P], h_t[:, k, :], start=(k == 0), stop=(k == KD - 1))
                if c:
                    ins.then_inc(proj_ready, 1)

            pe.wait_ge(s_sg, 16)
            shared_up("sg", 0)
            shared_up("sg", 1)
            def gather(part):
                for c in range(2):
                    k = 2 * part + c
                    for n, (s, src) in enumerate(((0, h_hi), (0, h_lo), (1, h_hi), (1, h_lo))):
                        ins = mm(bank[part % 2][:, c * 4 * C:(c + 1) * 4 * C], src[:, s, k, :], sel_p[:, s, :], start=(n == 0), stop=(n == 3))
                ins.then_inc(gbk_ready if part % 2 else ga_ready, 1)

            def turn(b):
                for s in range(NS):
                    nc.tensor.transpose(bank[0][:, s * P:(s + 1) * P], sel_p[:, s, b * P:(b + 1) * P].bitcast(F32), ident)
                for s in range(NS):
                    ins = mm(bank[0][:, T:T + 2], sel_p[:, s, b * P:(b + 1) * P].bitcast(F32), comb_p[:, s, 2 * b:2 * b + 2], start=(s == 0), stop=(s == 1))
                ins.then_inc(pt_ready, 1)

            def scatter(b, s, h, last=False):
                for part in (y_hi, y_lo):
                    ins = mm(y_acc[s][h][:, :], sel_t[b][:, s * P:(s + 1) * P], part[h][:, :], start=False, stop=(last and part is y_lo))
                return ins

            tri = consts[:, C_TRI:C_TRI + P]
            pe.wait_ge(lg_mask, 1)
            mm(bank[5][:, 0:NE], tri, mask[:, 0, :], start=True, stop=True)
            mm(bank[5][:, NE:2 * NE], tri, mask[:, 1, :], start=True, stop=False)
            mm(bank[5][:, NE:2 * NE], ones[:, :], mask[:, 0, :], start=False, stop=True)
            for s in range(NS):
                ins = mm(bank[5][0:NE, 128:129], mask[:, s, :], ones[:, 0:1], start=(s == 0), stop=(s == 1))
            ins.then_inc(cnt_ready, 1)
            shared_up("su", 0)
            pe.wait_ge(nx_done, 1)
            mm(bank[5][0:NE, 130:131], consts[0:NE, C_TRIE:C_TRIE + NE], nxt[0:NE, 3:4], start=True, stop=True).then_inc(end_ready, 1)
            for s in range(NS):
                nc.tensor.transpose(bank[6][0:NE, s * P:(s + 1) * P], posm[:, s, :], ident)
                ins = nc.tensor.transpose(bank[6][0:NE, T + s * P:T + (s + 1) * P], comb[:, s, :], ident)
            ins.then_inc(pt1_ready, 1)
            shared_up("su", 1)
            pe.wait_ge(built, 1)
            pe.wait_ge(hr_lo, 4)
            evacuated(pe, "sg")
            gather(0)
            pe.wait_ge(oh_done, 1)
            pe.wait_ge(pt1_copied, 1)
            for s in range(NS):
                out = bank[5][:, 320 + s * NX:320 + (s + 1) * NX]
                mm(out, tmp[0:NE, 0, s * P:(s + 1) * P], hot[0:NE, :], start=True, stop=False)
                mm(out, neg[0:NE, :], hotb[0:NE, :], start=False, stop=True)
                mm(bank[5][:, 384 + s * NX:384 + (s + 1) * NX], tmp[0:NE, 0, T + s * P:T + (s + 1) * P], hot[0:NE, :], start=True, stop=True)
            mm(bank[5][0:1, 256:256 + NX], consts[0:NE, C_ECOL:C_ECOL + 1], hot[0:NE, :], start=True, stop=True)
            mm(bank[5][0:1, 296:297], nxt[0:NE, 3:4], ones[0:NE, 0:1], start=True, stop=True).then_inc(items_ready, 1)
            evacuated(pe, "su")
            gather(1)
            pe.wait_ge(ga_evac, 1)
            gather(2)
            pe.wait_ge(gbk_evac, 1)
            gather(3)
            pe.wait_ge(ga_evac, 2)
            turn(0)

            def shared_down():
                pe.wait_ge(items_done, 2)
                pe.wait_ge(s_sd, 16)
                for s in range(NS):
                    for hf in range(2):
                        for c in range(2):
                            mm(y_acc[s][hf][:, :], act_s[:, c, s * P:(s + 1) * P], w_sd[:, c, hf * 512:(hf + 1) * 512], start=(c == 0), stop=False)

            def gather_next(i):
                pe.wait_ge(built, i + 2)
                pe.wait_ge(pt_evac, i * 2 + 2)
                gather(0)
                pe.wait_ge(gbk_evac, i * 2 + 2)
                gather(1)
                pe.wait_ge(ga_evac, i * 2 + 3)
                gather(2)
                pe.wait_ge(gbk_evac, i * 2 + 3)
                gather(3)
                pe.wait_ge(ga_evac, i * 2 + 4)
                turn(0)

            def gate_up(b, i):
                pe.wait_ge(ga_evac, i * 2 + 2)
                pe.wait_ge(gbk_evac, i * 2 + 2)
                for e in range(2):
                    pe.wait_ge(s_gu[2 * b + e], i * 16 + 16)
                for k in range(KD):
                    for e in range(2):
                        c = (2 * b + e) * C
                        ins = mm(bank[2 + b][e * C:(e + 1) * C, :], xg[:, k, c:c + C], w_gu[2 * b + e][:, k, :], start=(k == 0), stop=(k == KD - 1))
                ins.then_inc(gu_ready, 1)

            def last_results(b, p):
                for h in range(2):
                    pe.wait_ge(y_ready, p * 2 - (1 - h))
                    for s in range(NS):
                        scatter(1 - b, s, h)

            def second_pair_turn(i):
                pe.wait_ge(pt_evac, i * 2 + 1)
                turn(1)

            def act_to_channels(b, p):
                pe.wait_ge(act_ready, p + 1)
                for c in range(2):
                    ins = nc.tensor.transpose(bank[2 + b][:, c * P:(c + 1) * P], act_r[:, c * P:(c + 1) * P], ident)
                ins.then_inc(t_ready, 1)

            def down(b, p, i):
                for e in range(2):
                    pe.wait_ge(s_dn[2 * b + e], i * 16 + 16)
                pe.wait_ge(t_evac, p + 1)
                for h, out in enumerate((bank[3 - b], bank[2 + b])):
                    for c in range(2):
                        for e in range(2):
                            ins = mm(out[e * C:(e + 1) * C, :], act_t[:, c, e * C:(e + 1) * C], w_dn[2 * b + e][:, c, h * 512:(h + 1) * 512],
                                     start=(c == 0), stop=(c == 1))
                    ins.then_inc(dn_ready, 1)

            evacuated(pe, "hr", 3)
            gate_up(0, 0)
            second_pair_turn(0)
            act_to_channels(0, 0)
            down(0, 0, 0)
            pe.wait_ge(y_ready, 1)
            gate_up(1, 0)
            shared_down()
            last_results(1, 1)
            act_to_channels(1, 1)
            gather_next(0)
            down(1, 1, 0)
            n = pe.value_load(nwork, min_val=0, max_val=NI)

            def iteration(i):
                with pe.If(n > i * 4):
                    pe.wait_ge(y_ready, i * 4 - 1)
                    gate_up(0, i)
                    last_results(0, i * 2)
                    second_pair_turn(i)
                    act_to_channels(0, i * 2)
                    down(0, i * 2, i)
                    pe.wait_ge(y_ready, i * 4 + 1)
                    gate_up(1, i)
                    last_results(1, i * 2 + 1)
                    act_to_channels(1, i * 2 + 1)
                    with pe.If(n > i * 4 + 4):
                        gather_next(i)
                    down(1, i * 2 + 1, i)

            with pe.Fori(1, FEW) as i:
                iteration(i)
            with pe.If(n > FEW * 4):
                with pe.Fori(FEW, ITERS) as i:
                    iteration(i)
            pe.wait_ge(loop_done, 1)
            for s in range(NS):
                for h in range(2):
                    ins = scatter(1, s, h, last=True)
                ins.then_inc(y_done, 1)


INPUTS = ["x_prompt", "x_sample", "state_hgrn", "c", "c_ctx", "w_ada", "b_ada", "norm1_g", "w_in", "hgrn_lb_logits", "hgrn_norm_g",
          "w_proj_hgrn", "conv_dw_w", "conv_dw_b", "conv_norm_g", "conv_norm_b", "w_proj_conv", "w_out", "norm2_g", "w_router",
          "router_bias", "w_expert_gate_up", "w_expert_down", "w_shared_gate_up", "w_shared_down", "final_norm_g"]


def constants():
    import numpy as np

    n = np.arange(P)
    out = np.zeros((P, C_ALL), np.float32)
    out[:, C_ID:C_ID + P] = n[:, None] == n
    for level in range(LEVELS):
        out[:, C_MASK + P * level:C_MASK + P * (level + 1)] = ((n[:, None] ^ n) >> level) == 1
    out[:, C_TRI:C_TRI + P] = n[:, None] < n
    out[:NE, C_TRIE:C_TRIE + NE] = n[:NE, None] <= n[:NE]
    out[:, C_IOTA:C_IOTA + C] = n[:C]
    out[:, C_LT:C_LT + 64] = (np.arange(8)[:, None] > np.arange(8)).reshape(-1)
    out[:, C_ECOL] = n
    out[:, C_SUM:C_SUM + NS] = (n % 32)[:, None] == np.arange(NS)
    return out


def kernel(**inputs):
    import numpy as np
    import concourse.bacc as bacc
    from concourse.bass_utils import run_bass_kernel_spmd

    nc = bacc.Bacc("TRN2", target_bir_lowering=False, num_devices=1)
    arrays, aps = {}, {}
    for name in INPUTS:
        array = np.ascontiguousarray(inputs[name])
        arrays[f"in_{name}"] = array
        aps[name] = nc.dram_tensor(f"in_{name}", array.shape, mybir.dt.from_np(array.dtype), kind="ExternalInput").ap()
    arrays["in_consts"] = constants()
    aps["consts"] = nc.dram_tensor("in_consts", (P, C_ALL), F32, kind="ExternalInput").ap()
    shapes = [(1, P, D), (1, P, D), (1, 1, 2, H, P, P)]
    outs = [nc.dram_tensor(f"out_{i}", shape, F32, kind="ExternalOutput").ap() for i, shape in enumerate(shapes)]
    build(nc, aps, outs)
    result = run_bass_kernel_spmd(nc, [arrays], core_ids=[0]).results[0]
    return tuple(result[f"out_{i}"] for i in range(len(shapes)))
```
